# Optimizing a Trainium2 kernel written in Bass

```python
import math
import jax
import jax.numpy as jnp
from jax import lax
import numpy as np

D_MODEL = 1024
BATCH = 1
SEQ = 256
DEPTH = 2
DEC_BATCH = 8
DEC_SEQ = 4
PAST_LEN = 1024
PAGE_SIZE = 128

HEAD_DIM = 64
H_FOX = 4
H_DIL = 4
H_DELTA = 8
W_FOX = H_FOX * HEAD_DIM
W_DIL = H_DIL * HEAD_DIM
W_DELTA = H_DELTA * HEAD_DIM
FOX_QBLK = 128
FOX_FORGET_BIAS = (2.0, 5.0, 8.0, 11.0)
DIL_PATTERNS = ((128, 1), (512, 4), (2048, 16))
DIL_WIN_MAX = 2048
DELTA_CHUNK = 64
CONV_W = 4
CONV_CH = 3 * W_DELTA
IN_SIZES = (3 * W_FOX, H_FOX, 3 * W_DIL, CONV_CH, H_DELTA, H_DELTA, W_DELTA)
IN_WIDTH = 3 * W_FOX + H_FOX + 3 * W_DIL + CONV_CH + 2 * H_DELTA + W_DELTA
PEER_HEADS = 8
PEER_NKEYS = 128
PEER_EXPERTS = PEER_NKEYS * PEER_NKEYS
PEER_QDIM = 256
PEER_HALF = PEER_QDIM // 2
PEER_TOPK = 16
PEER_TOK_BLK = 256
NORM_EPS = 1e-6
L2_EPS = 1e-6
NEG_INF = -1e30

kernel_name = 'hymba_fox_dilated_gdn_peer_step'

def rms_norm(x, gain):
    xf = x.astype(jnp.float32)
    y = xf * lax.rsqrt(jnp.mean(xf * xf, axis=-1, keepdims=True) + NORM_EPS)
    return (y * gain.astype(jnp.float32)).astype(x.dtype)

def l2_normalize(x):
    return x * lax.rsqrt(jnp.sum(x * x, axis=-1, keepdims=True) + L2_EPS)

def heads(t, n_heads):
    return t.reshape(t.shape[:-1] + (n_heads, HEAD_DIM))

def alibi_slopes():
    return jnp.exp2(-8.0 * jnp.arange(1, H_DIL + 1, dtype=jnp.float32) / H_DIL)

def split_projection(h, w_in, b_fox_f):
    offsets = [int(o) for o in np.cumsum(IN_SIZES)[:-1]]
    fox_qkv, fox_f, dil_qkv, delta_qkv, delta_b, delta_a, delta_z = jnp.split(h @ w_in, offsets, axis=-1)
    fox_q, fox_k, fox_v = [heads(t, H_FOX) for t in jnp.split(fox_qkv, 3, axis=-1)]
    fox_logf = jax.nn.log_sigmoid((fox_f + b_fox_f).astype(jnp.float32))
    dil_q, dil_k, dil_v = [heads(t, H_DIL) for t in jnp.split(dil_qkv, 3, axis=-1)]
    return (fox_q, fox_k, fox_v, fox_logf, dil_q, dil_k, dil_v, delta_qkv, delta_b, delta_a, delta_z)

def fox_attention_prompt(q, k, v, logf):
    B, S, H, hd = q.shape
    nblk = S // FOX_QBLK
    kf = k.astype(jnp.float32)
    vf = v.astype(jnp.float32)
    cum = jnp.cumsum(logf, axis=1).transpose(0, 2, 1)
    q_blocks = (q.astype(jnp.float32) * hd ** -0.5).reshape(B, nblk, FOX_QBLK, H, hd).swapaxes(0, 1)
    cum_blocks = cum.reshape(B, H, nblk, FOX_QBLK).transpose(2, 0, 1, 3)
    k_pos = jnp.arange(S)

    def block(args):
        qb, cb, n = args
        q_pos = n * FOX_QBLK + jnp.arange(FOX_QBLK)
        s = jnp.einsum('bqhd,bkhd->bhqk', qb, kf) + cb[..., None] - cum[:, :, None, :]
        s = jnp.where(k_pos[None, :] <= q_pos[:, None], s, NEG_INF)
        p = jax.nn.softmax(s, axis=-1)
        return jnp.einsum('bhqk,bkhd->bqhd', p, vf)

    out = lax.map(block, (q_blocks, cum_blocks, jnp.arange(nblk)))
    return out.swapaxes(0, 1).reshape(B, S, H, hd)

def fox_attention_sample(q, k_new, v_new, logf_new, kv_pages, logf_pages, page_table):
    B, T, H, hd = q.shape
    n_past = page_table.shape[1] * kv_pages.shape[1]
    kv_past = kv_pages[page_table].reshape(B, n_past, 2, H, hd).astype(jnp.float32)
    lf_past = logf_pages[page_table].reshape(B, n_past, H).astype(jnp.float32)
    cum_q = jnp.cumsum(logf_new, axis=1)
    after_past = lax.cumsum(lf_past, axis=1, reverse=True) - lf_past
    cum_k = jnp.concatenate([-after_past, cum_q], axis=1).transpose(0, 2, 1)
    keys = jnp.concatenate([kv_past[:, :, 0], k_new.astype(jnp.float32)], axis=1)
    vals = jnp.concatenate([kv_past[:, :, 1], v_new.astype(jnp.float32)], axis=1)
    s = jnp.einsum('bqhd,bkhd->bhqk', q.astype(jnp.float32) * hd ** -0.5, keys)
    s = s + cum_q.transpose(0, 2, 1)[..., None] - cum_k[:, :, None, :]
    allowed = jnp.arange(n_past + T)[None, :] <= n_past + jnp.arange(T)[:, None]
    p = jax.nn.softmax(jnp.where(allowed, s, NEG_INF), axis=-1)
    return jnp.einsum('bhqk,bkhd->bqhd', p, vals)

def dilated_branch_prompt(q, k, v, slopes, window, dil):
    B, S, H, hd = q.shape
    span = window // dil
    unit = span * dil
    L = -(-S // unit) * unit
    nb = L // unit

    def to_blocks(t):
        t = jnp.pad(t, ((0, 0), (0, L - S), (0, 0), (0, 0))).reshape(B, L // dil, dil, H, hd)
        return t.transpose(0, 2, 1, 3, 4).reshape(B, dil, nb, span, H, hd)

    def with_prev(t):
        prev = jnp.pad(t, ((0, 0), (0, 0), (1, 0), (0, 0), (0, 0), (0, 0)))[:, :, :-1]
        return jnp.concatenate([prev, t], axis=3)

    qb = to_blocks(q)
    kb = with_prev(to_blocks(k))
    vb = with_prev(to_blocks(v))
    s = jnp.einsum('brnqhd,brnkhd->brnhqk', qb, kb)
    dist = jnp.arange(span)[:, None] + span - jnp.arange(2 * span)[None, :]
    key_idx = jnp.arange(nb)[:, None, None] * span + jnp.arange(2 * span)[None, None, :] - span
    valid = (dist >= 0) & (dist <= span) & (key_idx >= 0)
    s = s - slopes[:, None, None] * (dist * dil).astype(jnp.float32)
    s = jnp.where(valid[:, None], s, NEG_INF)
    m = jnp.max(s, axis=-1)
    p = jnp.exp(s - m[..., None])
    den = jnp.sum(p, axis=-1)
    num = jnp.einsum('brnhqk,brnkhd->brnqhd', p, vb)

    def from_blocks(t):
        rest = t.shape[4:]
        t = t.reshape((B, dil, nb * span) + rest).swapaxes(1, 2).reshape((B, L) + rest)
        return t[:, :S]

    return (from_blocks(m.swapaxes(-1, -2)), from_blocks(den.swapaxes(-1, -2)), from_blocks(num))

def dilated_branch_sample(q, k_all, v_all, slopes, window, dil, n_buf):
    T = q.shape[1]
    span = window // dil
    j = jnp.arange(span + 1)
    idx = n_buf + jnp.arange(T)[:, None] - j[None, :] * dil
    valid = idx >= 0
    idx = jnp.maximum(idx, 0)
    kg = k_all[:, idx]
    vg = v_all[:, idx]
    s = jnp.einsum('bthd,btjhd->bthj', q, kg) - slopes[:, None] * (j * dil).astype(jnp.float32)
    s = jnp.where(valid[:, None, :], s, NEG_INF)
    m = jnp.max(s, axis=-1)
    p = jnp.exp(s - m[..., None])
    den = jnp.sum(p, axis=-1)
    num = jnp.einsum('bthj,btjhd->bthd', p, vg)
    return m, den, num

def combine_by_denominator(branches):
    m_all = jnp.stack([b[0] for b in branches])
    weights = jnp.exp(m_all - jnp.max(m_all, axis=0))
    den = sum(w * b[1] for w, b in zip(weights, branches))
    num = sum(w[..., None] * b[2] for w, b in zip(weights, branches))
    return num / den[..., None]

def dilated_attention_prompt(q, k, v):
    qf = q.astype(jnp.float32) * HEAD_DIM ** -0.5
    kf, vf = k.astype(jnp.float32), v.astype(jnp.float32)
    slopes = alibi_slopes()
    return combine_by_denominator([dilated_branch_prompt(qf, kf, vf, slopes, w, d) for (w, d) in DIL_PATTERNS])

def dilated_attention_sample(q, k_new, v_new, buf):
    n_buf = buf.shape[1]
    k_all = jnp.concatenate([buf[:, :, 0].astype(jnp.float32), k_new.astype(jnp.float32)], axis=1)
    v_all = jnp.concatenate([buf[:, :, 1].astype(jnp.float32), v_new.astype(jnp.float32)], axis=1)
    qf = q.astype(jnp.float32) * HEAD_DIM ** -0.5
    slopes = alibi_slopes()
    return combine_by_denominator([dilated_branch_sample(qf, k_all, v_all, slopes, w, d, n_buf) for (w, d) in DIL_PATTERNS])

def delta_preprocess(qkv_raw, conv_buf, conv_w, b_raw, a_raw, a_log, dt_bias):
    T = qkv_raw.shape[1]
    padded = jnp.concatenate([conv_buf.astype(qkv_raw.dtype), qkv_raw], axis=1)
    conv = sum(padded[:, i:i + T] * conv_w[i] for i in range(CONV_W))
    act = jax.nn.silu(conv.astype(jnp.float32))
    q, k, v = [heads(t, H_DELTA) for t in jnp.split(act, 3, axis=-1)]
    q = l2_normalize(q) * HEAD_DIM ** -0.5
    k = l2_normalize(k)
    beta = jax.nn.sigmoid(b_raw.astype(jnp.float32))
    g = -jnp.exp(a_log.astype(jnp.float32)) * jax.nn.softplus(a_raw.astype(jnp.float32) + dt_bias.astype(jnp.float32))
    return q, k, v, g, beta, padded[:, -(CONV_W - 1):]

def delta_chunk(state, q, k, v, g, beta):
    q, k, v = [t.swapaxes(1, 2) for t in (q, k, v)]
    g, beta = g.swapaxes(1, 2), beta.swapaxes(1, 2)
    C = q.shape[2]
    gc = jnp.cumsum(g, axis=-1)
    incl = jnp.tril(jnp.ones((C, C), bool))
    strict = jnp.tril(jnp.ones((C, C), bool), -1)
    decay = jnp.where(incl, jnp.exp(jnp.where(incl, gc[..., :, None] - gc[..., None, :], 0.0)), 0.0)
    kb = k * beta[..., None]
    lower = jnp.where(strict, jnp.einsum('bhid,bhjd->bhij', kb, k) * decay, 0.0)
    rhs = jnp.concatenate([v * beta[..., None], kb * jnp.exp(gc)[..., None]], axis=-1)
    sol = lax.linalg.triangular_solve(lower + jnp.eye(C, dtype=jnp.float32), rhs, left_side=True, lower=True, unit_diagonal=True)
    u, w = sol[..., :HEAD_DIM], sol[..., HEAD_DIM:]
    v_new = u - jnp.einsum('bhik,bhkv->bhiv', w, state)
    attn = jnp.einsum('bhid,bhjd->bhij', q, k) * decay
    o = jnp.einsum('bhik,bhkv->bhiv', q * jnp.exp(gc)[..., None], state) + jnp.einsum('bhij,bhjv->bhiv', attn, v_new)
    g_last = gc[..., -1:]
    new_state = state * jnp.exp(g_last)[..., None] + jnp.einsum('bhik,bhiv->bhkv', k * jnp.exp(g_last - gc)[..., None], v_new)
    return new_state, o.swapaxes(1, 2)

def delta_rule_prompt(q, k, v, g, beta):
    B, S, H, _ = q.shape
    n = S // DELTA_CHUNK

    def chunks(t):
        return t.reshape((B, n, DELTA_CHUNK) + t.shape[2:]).swapaxes(0, 1)

    state0 = jnp.zeros((B, H, HEAD_DIM, HEAD_DIM), jnp.float32)
    final, o = lax.scan(lambda st, inp: delta_chunk(st, *inp), state0, tuple(chunks(t) for t in (q, k, v, g, beta)))
    return o.swapaxes(0, 1).reshape(B, S, H, HEAD_DIM), final

def gated_head_norm(o, z, gain):
    B, T = o.shape[:2]
    return (rms_norm(o, gain) * jax.nn.silu(heads(z, H_DELTA).astype(jnp.float32))).reshape(B, T, W_DELTA)

def mixer_prompt(h, w_in, b_fox_f, conv_w, a_log, dt_bias, delta_norm, w_out):
    B, S, _ = h.shape
    fq, fk, fv, flogf, dq, dk, dv, cqkv, cb, ca, cz = split_projection(h, w_in, b_fox_f)
    o_fox = fox_attention_prompt(fq, fk, fv, flogf)
    o_dil = dilated_attention_prompt(dq, dk, dv)
    conv_zero = jnp.zeros((B, CONV_W - 1, CONV_CH), h.dtype)
    q, k, v, g, beta, conv_state = delta_preprocess(cqkv, conv_zero, conv_w, cb, ca, a_log, dt_bias)
    o_delta, delta_state = delta_rule_prompt(q, k, v, g, beta)
    o_delta = gated_head_norm(o_delta, cz, delta_norm)
    mixed = jnp.concatenate([o_fox.reshape(B, S, W_FOX), o_dil.reshape(B, S, W_DIL), o_delta], axis=-1)
    y = mixed.astype(h.dtype) @ w_out
    n_keep = min(DIL_WIN_MAX, S)
    new_state = (jnp.stack([fk, fv], axis=2), flogf.astype(h.dtype), jnp.stack([dk, dv], axis=2)[:, S - n_keep:], delta_state.astype(h.dtype), conv_state)
    return y, new_state

def mixer_sample(h, kv_pages, logf_pages, dil_buf, delta_state, conv_buf, page_table, w_in, b_fox_f, conv_w, a_log, dt_bias, delta_norm, w_out):
    B, T, _ = h.shape
    fq, fk, fv, flogf, dq, dk, dv, cqkv, cb, ca, cz = split_projection(h, w_in, b_fox_f)
    o_fox = fox_attention_sample(fq, fk, fv, flogf, kv_pages, logf_pages, page_table)
    o_dil = dilated_attention_sample(dq, dk, dv, dil_buf)
    q, k, v, g, beta, conv_state = delta_preprocess(cqkv, conv_buf, conv_w, cb, ca, a_log, dt_bias)
    new_delta, o_delta = delta_chunk(delta_state.astype(jnp.float32), q, k, v, g, beta)
    o_delta = gated_head_norm(o_delta, cz, delta_norm)
    mixed = jnp.concatenate([o_fox.reshape(B, T, W_FOX), o_dil.reshape(B, T, W_DIL), o_delta], axis=-1)
    y = mixed.astype(h.dtype) @ w_out
    new_state = (jnp.stack([fk, fv], axis=2), flogf.astype(h.dtype), jnp.stack([dk, dv], axis=2), new_delta.astype(h.dtype), conv_state)
    return y, new_state

def peer_ffn(h, wq, keys, u, v):
    B, T, D = h.shape
    n = B * T
    n_pad = -(-n // PEER_TOK_BLK) * PEER_TOK_BLK
    hb = jnp.pad(h.reshape(n, D), ((0, n_pad - n), (0, 0))).reshape(n_pad // PEER_TOK_BLK, PEER_TOK_BLK, D)
    keys_f = keys.astype(jnp.float32)

    def block(xb):
        q = (xb @ wq).reshape(PEER_TOK_BLK, PEER_HEADS, 2, PEER_HALF).astype(jnp.float32)
        sc = jnp.einsum('nhcd,hckd->nhck', q, keys_f)
        sv, si = lax.top_k(sc, PEER_TOPK)
        cand = (sv[:, :, 0, :, None] + sv[:, :, 1, None, :]).reshape(PEER_TOK_BLK, PEER_HEADS, PEER_TOPK * PEER_TOPK)
        cidx = (si[:, :, 0, :, None] * PEER_NKEYS + si[:, :, 1, None, :]).reshape(PEER_TOK_BLK, PEER_HEADS, PEER_TOPK * PEER_TOPK)
        fv, fp = lax.top_k(cand, PEER_TOPK)
        experts = jnp.take_along_axis(cidx, fp, axis=-1)
        gate = jax.nn.softmax(fv, axis=-1)
        ug = u[experts]
        vg = v[experts]
        act = jax.nn.gelu(jnp.einsum('nd,nhkd->nhk', xb, ug).astype(jnp.float32), approximate=False)
        return jnp.einsum('nhk,nhkd->nd', (gate * act).astype(xb.dtype), vg)

    out = lax.map(block, hb).reshape(n_pad, D)[:n]
    return out.reshape(B, T, D)

def stack_field(states, i):
    return jnp.stack([s[i] for s in states])

def setup_inputs(seed: int = 0) -> dict:
    key = jax.random.key(seed)
    ks = jax.random.split(key, 22)
    f32 = jnp.float32
    n_pages = PAST_LEN // PAGE_SIZE
    n_used = DEC_BATCH * n_pages
    n_pool = n_used + max(1, n_used // 4)
    n_buf = min(DIL_WIN_MAX, PAST_LEN)
    forget_bias = jnp.array(FOX_FORGET_BIAS, f32)

    def nrm(k, shape, scale=1.0):
        return scale * jax.random.normal(k, shape, f32)

    dt = jnp.exp(jax.random.uniform(ks[12], (DEPTH, H_DELTA), f32, math.log(1e-3), math.log(1e-1)))
    return {
        'x_prompt': nrm(ks[0], (BATCH, SEQ, D_MODEL)),
        'x_sample': nrm(ks[1], (DEC_BATCH, DEC_SEQ, D_MODEL)),
        'cache_fox_kv': nrm(ks[2], (DEPTH, n_pool, PAGE_SIZE, 2, H_FOX, HEAD_DIM)),
        'cache_fox_logf': jax.nn.log_sigmoid(forget_bias + nrm(ks[3], (DEPTH, n_pool, PAGE_SIZE, H_FOX), 0.5)),
        'cache_dil_kv': nrm(ks[4], (DEPTH, DEC_BATCH, n_buf, 2, H_DIL, HEAD_DIM)),
        'state_delta': nrm(ks[5], (DEPTH, DEC_BATCH, H_DELTA, HEAD_DIM, HEAD_DIM), 0.1),
        'state_conv': nrm(ks[6], (DEPTH, DEC_BATCH, CONV_W - 1, CONV_CH)),
        'page_table': jax.random.permutation(ks[7], n_pool)[:n_used].reshape(DEC_BATCH, n_pages).astype(jnp.int32),
        'norm_mix': 1.0 + nrm(ks[8], (DEPTH, D_MODEL), 0.02),
        'w_in': nrm(ks[9], (DEPTH, D_MODEL, IN_WIDTH), D_MODEL ** -0.5),
        'b_fox_f': forget_bias + nrm(ks[10], (DEPTH, H_FOX), 0.1),
        'conv_w': nrm(ks[11], (DEPTH, CONV_W, CONV_CH), CONV_W ** -0.5),
        'a_log': jnp.log(jax.random.uniform(ks[13], (DEPTH, H_DELTA), f32, 1.0, 16.0)),
        'dt_bias': dt + jnp.log(-jnp.expm1(-dt)),
        'delta_norm': 1.0 + nrm(ks[14], (DEPTH, HEAD_DIM), 0.02),
        'w_out': nrm(ks[15], (DEPTH, D_MODEL, D_MODEL), D_MODEL ** -0.5),
        'norm_ffn': 1.0 + nrm(ks[16], (DEPTH, D_MODEL), 0.02),
        'peer_wq': nrm(ks[17], (DEPTH, D_MODEL, PEER_HEADS * PEER_QDIM), D_MODEL ** -0.5),
        'peer_keys': nrm(ks[18], (DEPTH, PEER_HEADS, 2, PEER_NKEYS, PEER_HALF), PEER_HALF ** -0.5),
        'peer_u': nrm(ks[19], (DEPTH, PEER_EXPERTS, D_MODEL), D_MODEL ** -0.5),
        'peer_v': nrm(ks[20], (DEPTH, PEER_EXPERTS, D_MODEL), PEER_HEADS ** -0.5),
        'norm_final': 1.0 + nrm(ks[21], (D_MODEL,), 0.02),
    }

def reference(x_prompt, x_sample, cache_fox_kv, cache_fox_logf, cache_dil_kv, state_delta, state_conv, page_table, norm_mix, w_in, b_fox_f, conv_w, a_log, dt_bias, delta_norm, w_out, norm_ffn, peer_wq, peer_keys, peer_u, peer_v, norm_final):
    xp, xs = x_prompt, x_sample
    prompt_states, sample_states = [], []
    for l in range(DEPTH):
        yp, st_p = mixer_prompt(rms_norm(xp, norm_mix[l]), w_in[l], b_fox_f[l], conv_w[l], a_log[l], dt_bias[l], delta_norm[l], w_out[l])
        ys, st_s = mixer_sample(rms_norm(xs, norm_mix[l]), cache_fox_kv[l], cache_fox_logf[l], cache_dil_kv[l], state_delta[l], state_conv[l], page_table, w_in[l], b_fox_f[l], conv_w[l], a_log[l], dt_bias[l], delta_norm[l], w_out[l])
        xp = xp + yp
        xs = xs + ys
        xp = xp + peer_ffn(rms_norm(xp, norm_ffn[l]), peer_wq[l], peer_keys[l], peer_u[l], peer_v[l])
        xs = xs + peer_ffn(rms_norm(xs, norm_ffn[l]), peer_wq[l], peer_keys[l], peer_u[l], peer_v[l])
        prompt_states.append(st_p)
        sample_states.append(st_s)
    y_prompt = rms_norm(xp, norm_final)
    y_sample = rms_norm(xs, norm_final)
    fox_kv_prompt = stack_field(prompt_states, 0)
    fox_logf_prompt = stack_field(prompt_states, 1)
    dil_kv_prompt = stack_field(prompt_states, 2)
    delta_state_prompt = stack_field(prompt_states, 3)
    conv_state_prompt = stack_field(prompt_states, 4)
    fox_kv_sample = stack_field(sample_states, 0)
    fox_logf_sample = stack_field(sample_states, 1)
    dil_kv_sample = stack_field(sample_states, 2)
    delta_state_sample = stack_field(sample_states, 3)
    conv_state_sample = stack_field(sample_states, 4)
    return (y_prompt, y_sample, fox_kv_prompt, fox_logf_prompt, dil_kv_prompt, delta_state_prompt, conv_state_prompt, fox_kv_sample, fox_logf_sample, dil_kv_sample, delta_state_sample, conv_state_sample)


_drawn_inputs = setup_inputs


def setup_inputs(seed=0):
    import zlib

    import numpy as np

    out = dict(_drawn_inputs(seed))
    spreads = {}
    factors = {}
    for name, (base, spread) in spreads.items():
        noise = np.random.default_rng([zlib.crc32(name.encode()), seed]).standard_normal(out[name].shape)
        drawn = base * np.exp(spread * noise) if base else spread * noise
        out[name] = jnp.asarray(drawn.astype(out[name].dtype))
    for name, factor in factors.items():
        out[name] = (out[name] * factor).astype(out[name].dtype)
    return out
```

```python
from contextlib import ExitStack

import numpy as np

import concourse.bass as bass
from concourse import mybir
from concourse.alu_op_type import AluOpType as ALU

F32 = mybir.dt.float32
U32 = mybir.dt.uint32
I32 = mybir.dt.int32
ACT = mybir.ActivationFunctionType
AX = mybir.AxisListType

P = 128
D = 1024
DC = D // P
SEQ = 256
B = 8
T = 4
NS = B * T
N = SEQ + NS
DEPTH = 2
PAST = 1024
PAGES = PAST // P
HD = 64
NPOOL = 80
CONV = 1536
INW = 3604
NH = 8
EPS = 1e-6
NEG = -1e30
TILES = [(0, 128), (128, 128), (256, 32)]
SLOPES = [2.0 ** (-8.0 * (h + 1) / 4) for h in range(4)]
DILK = 5
TOPK = 16
NCH = 128


def shape_constants():
    def dist_table(q, k):
        d = q[:, None] - k[None, :]
        ok = d >= 0
        cnt = ((d <= 128).astype(float) + ((d % 4 == 0) & (d <= 512)) + ((d % 16 == 0) & (d <= 2048))) * ok
        return d, cnt

    r = np.arange(P)
    keep, mix = {}, {}
    keep["ident"] = np.eye(P)
    keep["ones"] = np.ones((P, P))
    keep["iota"] = np.tile(r, (P, 1))
    keep["iota16"] = np.tile(np.arange(16), (P, 1))
    keep["zero"] = np.zeros((P, 512))
    gt = (r[:, None] > r[None, :]).astype(float)
    mix["ones_gt"] = np.concatenate([np.ones((P, 896)), gt], 1)
    mix["neg_le"] = -(r[:, None] <= r[None, :]).astype(float)
    mix["neg_one"] = -np.ones((P, P))
    for name, blk in (("64", 64), ("4", 4)):
        w = P if blk == 64 else NS
        same = (r[:, None] // blk == r[None, :w] // blk)
        mix["le" + name] = ((r[:, None] <= r[None, :w]) & same).astype(float)
        mix["gt" + name] = ((r[:, None] > r[None, :w]) & same).astype(float)
    for s in (1, 2, 4, 8, 16, 32):
        mix[f"lev{s}"] = ((r[:, None] // (2 * s) == r[None, :] // (2 * s)) & (r[:, None] % (2 * s) < s)
                          & (r[None, :] % (2 * s) >= s)).astype(float)
    mix["rowb"] = (r[:, None] // T == np.arange(B)[None, :]).astype(float)
    mix["colb"] = np.tile((np.arange(NS)[None, :] // T == np.arange(B)[:, None]).reshape(1, -1).astype(float), (P, 1))
    mix["half"] = np.concatenate([np.tile((r < 64)[:, None], (1, 64)), np.tile((r >= 64)[:, None], (1, 64))], 1)
    dd, cc = [], []
    for qt in range(2):
        d, cnt = dist_table(128 * qt + r, np.arange(SEQ))
        dd.append(np.where(cnt > 0, d, 1e32))
        cc.append(cnt)
    mix["pdist"] = np.concatenate(dd, 1)
    mix["pcnt"] = np.concatenate(cc, 1)
    mix["causal"] = np.where(r[None, :] <= r[:, None], 0.0, NEG)
    rb, rh, rt = r // 16, (r % 16) // 4, r % 4
    kb, kt = np.arange(NS) // T, np.arange(NS) % T
    mine = (rb[:, None] == kb[None, :]) & (kt[None, :] <= rt[:, None])
    mix["smask"] = np.where(mine, 0.0, NEG)
    mix["neg_le4"] = np.zeros((P, NS))
    mix["neg_le4"][:NS] = -((kb[:, None] == kb[None, :]) & (kt[:, None] <= kt[None, :])).astype(float)
    pos = np.concatenate([(16 * np.arange(32)[:, None] + np.arange(4)[None, :]).ravel(), np.arange(512, PAST)])
    d = PAST + rt[:, None] - pos[None, :]
    cnt = (d <= 128).astype(float) + ((d % 4 == 0) & (d <= 512)) + ((d % 16 == 0) & (d <= 2048))
    dn = rt[:, None] - kt[None, :]
    cn = np.where(mine, 1.0 + (dn % 4 == 0) + (dn % 16 == 0), 0.0)
    d, cnt = np.concatenate([d, dn], 1), np.concatenate([cnt, cn], 1)
    sl = np.array(SLOPES)[rh][:, None]
    mix["sbias"] = np.where(cnt > 0, -sl * d, NEG)
    mix["scnt"] = cnt
    blocks, where = [], {}
    for part in (keep, mix):
        at = 0
        for k, v in part.items():
            where[k] = (at, v.shape[1])
            at += v.shape[1]
        blocks.append(np.ascontiguousarray(np.concatenate(list(part.values()), 1).astype(np.float32)))
    return blocks[0], blocks[1], where


class Banks:

    def __init__(self, filled, drained, psum):
        self.filled, self.drained, self.psum = filled, drained, psum
        self.at, self.uses, self.where = 0, [0] * 8, {}

    def plan(self, name, i, n=1, banks=None):
        got = []
        for b in banks or [(self.at + m) % 8 for m in range(n)]:
            self.at = b + 1
            got.append((b, self.uses[b]))
            self.uses[b] += 1
        self.where[(name, i)] = got

    def ap(self, name, i=0, k=0):
        return self.psum[:, self.where[(name, i)][k][0], :]

    def full_sem(self, name, i=0, k=0):
        return self.filled[self.where[(name, i)][k][0]]

    def out_sem(self, name, i=0, k=0):
        return self.drained[self.where[(name, i)][k][0]]

    def wait_free(self, eng, l, name, i=0, k=0):
        b, o = self.where[(name, i)][k]
        if l * self.uses[b] + o > 0:
            eng.wait_ge(self.drained[b], l * self.uses[b] + o)

    def wait_full(self, eng, l, name, i=0, k=0):
        b, o = self.where[(name, i)][k]
        eng.wait_ge(self.filled[b], l * self.uses[b] + o + 1)

    def wait_out(self, eng, l, name, i=0, k=0):
        b, o = self.where[(name, i)][k]
        eng.wait_ge(self.drained[b], l * self.uses[b] + o + 1)


class Signal:

    def __init__(self, sem, n, step=1):
        self.sem, self.n, self.step, self.given = sem, n, step, 0

    def by(self, ins):
        self.given += 1
        ins.then_inc(self.sem, self.step)
        return ins

    def wait(self, eng, l, k):
        eng.wait_ge(self.sem, l * (self.n * self.step) + k * self.step)


class Steps:

    def __init__(self, sem):
        self.sem, self.given = sem, 0

    def by(self, ins):
        self.given += 1
        ins.then_inc(self.sem, 1)

    def settle(self, eng):
        eng.wait_ge(self.sem, self.given)


STORES = 27


def build(nc, a, where):
    ctx = ExitStack()
    with ctx:
        def sb(name, shape, dt=F32):
            return ctx.enter_context(nc.sbuf_tensor(name, shape, dt))

        def sem(name):
            return ctx.enter_context(nc.semaphore(name))


        KEEPW, MIXW = a["c_keep"].shape[1], a["c_mix"].shape[1]
        SIDEW = 9088
        keep = sb("keep", [P, KEEPW])
        x = sb("x", [P, 3, D])
        hT = sb("hT", [P, DC, N])
        small = sb("small", [P, 640])
        ptab = sb("ptab", [1, B * PAGES], I32)
        pidx = sb("pidx", [B * PAGES, 2], I32)
        arena = sb("arena", [P, NCH * N])
        side = sb("side", [P, SIDEW])
        psum = ctx.enter_context(nc.psum_tensor("psum", [P, 8, 512], F32))

        class Area:
            def __init__(self, tensor, at, end):
                self.t, self.at, self.end = tensor, at, end

            def take(self, n):
                got = self.t[:, self.at:self.at + n]
                self.at += n
                assert self.at <= self.end, (self.at, self.end)
                return got

            def rest(self):
                return Area(self.t, self.at, self.end)

        def K(name):
            o, w = where[name]
            return keep[:, o:o + w]

        ident, ones, iota, iota16, zero = (K(n) for n in ("ident", "ones", "iota", "iota16", "zero"))
        sm = Area(small, 0, 640)
        ms, gain, fbias, alog, naexp = sm.take(8), sm.take(64), sm.take(12), sm.take(8), sm.take(8)
        fraw, baraw = sm.take(12), sm.take(48)
        y12, e12, s12, q12, p12, lg = (sm.take(36) for _ in range(6))
        beta, eg, qkss = sm.take(24), sm.take(48), sm.take(16)
        mneg, den, dnorm, gm = sm.take(4), sm.take(4), sm.take(HD), sm.take(64)
        lgv = lg.rearrange("p (t c) -> p t c", t=3)
        egv = eg.rearrange("p (t c) -> p t c", t=3)
        betav = beta.rearrange("p (t c) -> p t c", t=3)

        whole = Area(arena, 0, NCH * N)
        mixc = whole.take(MIXW)
        mixT = whole.take(DC * N).rearrange("p (c n) -> p c n", n=N)
        qkT = whole.take(8 * N).rearrange("p (c n) -> p c n", n=N)
        kvrow = whole.take(3 * 1024).rearrange("p (t g c) -> p t g c", t=3, g=2)
        zrow = whole.take(3 * 512).rearrange("p (t c) -> p t c", t=3)
        tok = whole.take(3 * 1536).rearrange("p (t s c) -> p t s c", t=3, s=3)

        def C(name):
            o, w = where[name]
            return mixc[:, o:o + w]

        pj, bj = whole.rest(), Area(side, 0, SIDEW)
        wring = [pj.take(DC * 528) for _ in range(3)]
        LPAD, LOUT = 3 + SEQ + 7 * B, SEQ + 7 * B
        cT = pj.take(12 * LPAD).rearrange("p (c n) -> p c n", n=LPAD)
        cO = bj.take(12 * LPAD).rearrange("p (c n) -> p c n", n=LPAD)
        cOseq = cO[:, :, 3 + SEQ:LPAD].rearrange("p c (b s) -> p c b s", b=B)
        cS = bj.take(12 * N).rearrange("p (c n) -> p c n", n=N)
        crow = bj.take(CONV)
        xn = side[:, 0:2 * D].rearrange("p (s c) -> p s c", s=2)
        vrows = side[:, 2 * D:2 * D + P]

        dl, db = whole.rest(), Area(side, 0, SIDEW)
        per = [dict(zip(("attnT", "TT", "qeT", "nwT", "vb", "kd"), [dl.take(n) for n in (1024,) * 4 + (512,) * 2]))
               for _ in range(2)]
        sb2 = whole.rest()
        nwm, qem, vnm, s0 = sb2.take(2048), sb2.take(2048), sb2.take(2048), sb2.take(4096)
        GG, EX, EXI, LT = (dl.take(1024) for _ in range(4))
        T0, P1, kT, kq = db.take(1024), db.take(1024), db.take(1024), db.take(2048)
        kb, kbe, qe = (db.take(512) for _ in range(3))
        LM = GG
        per.append(dict(zip(("attnT", "TT", "qeT", "nwT", "vb", "kd"),
                        [db.take(256)] + [dl.take(n) for n in (256,) * 3 + (512,) * 2])))
        vnw = dl.take(512), db.take(512), db.take(512)
        st = dl.take(512)
        otok = db.take(512), db.take(512), dl.take(512)
        eglT = db.take(96)

        at, ab = whole.rest(), Area(side, 0, SIDEW)
        ring = [at.take(2048).rearrange("p (k c) -> p k c", c=256) for _ in range(4)]
        KT = [at.take(2048).rearrange("p (g k) -> p g k", g=2) for _ in range(2)]
        lfr = at.take(1024).rearrange("p (g r) -> p g r", g=PAGES)
        lfb = at.take(1024).rearrange("p (t h q) -> p t h q", t=2, h=4)
        PTs = at.take(1024).rearrange("p (g r) -> p g r", g=PAGES)
        QZ = ab.take(2048).rearrange("p (g b r) -> p g b r", g=2, b=B)
        QA = ab.take(256).rearrange("p (g r) -> p g r", g=2)
        SMp = [ab.take(512).rearrange("p (a k) -> p a k", a=2) for _ in range(2)]
        PRp = [ab.take(512).rearrange("p (a k) -> p a k", a=2) for _ in range(2)]
        PTp = [ab.take(512).rearrange("p (g a q) -> p g a q", g=2, a=2) for _ in range(2)]
        PRs = ab.take(1056)
        SNs, PTn, lfrn = ab.take(32), ab.take(128), ab.take(128)
        lfg = ab.take(512)

        ff = Area(arena, MIXW + DC * N, NCH * N)
        wo = ff.take(DC * D).rearrange("p (c n) -> p c n", n=D)
        wq = ff.take(DC * 2 * D).rearrange("p (c n) -> p c n", n=2 * D)
        topv = ff.take(256).rearrange("p (g k) -> p g k", k=TOPK)
        topf = ff.take(256).rearrange("p (g k) -> p g k", k=TOPK)
        fv, fa, fb = (ff.take(128).rearrange("p (h k) -> p h k", h=NH) for _ in range(3))
        ijw = ff.take(384).rearrange("p (s k) -> p s k", s=3)
        hsum = ff.take(16)
        fu = Area(arena, 0, MIXW)
        qTf = fu.take(16 * N).rearrange("p (c n) -> p c n", n=N)
        over_wo = wo.rearrange("p c n -> p (c n)")
        keysr = side[:, 2048:4096].rearrange("p (g d) -> p g d", g=16)
        keysT = side[:, 4096:6144].rearrange("p (g k) -> p g k", g=16)
        scb = [over_wo[:, 2048 * i:2048 * (i + 1)].rearrange("p (g k) -> p g k", g=16) for i in range(2)]
        sc2 = over_wo[:, 4096:6144].rearrange("p (g k) -> p g k", g=16)
        cand = over_wo[:, 6144:8192]
        cand2 = side[:, 0:2048]
        oneh = sc2
        topu = ff.take(256).bitcast(U32).rearrange("p (g k) -> p g k", k=TOPK)
        posu = ff.take(128).bitcast(U32).rearrange("p (h k) -> p h k", h=NH)
        posw = ff.take(256).bitcast(U32).rearrange("p (s h k) -> p s h k", s=2, h=NH)

        G = arena[:, :].rearrange("p (j n) -> p j n", n=N)
        pr = Area(side, 0, SIDEW)
        ubuf = [pr.take(D) for _ in range(2)]
        vbuf = [pr.take(D) for _ in range(2)]
        UT = [pr.take(D).rearrange("p (c e) -> p c e", c=DC) for _ in range(2)]
        ge = [pr.take(N) for _ in range(2)]
        aT = [pr.take(N) for _ in range(2)]
        ijwT = pr.take(3 * N).rearrange("p (s n) -> p s n", s=3)
        YT = side[:, 0:DC * N].rearrange("p (c n) -> p c n", n=N)
        hot = [side[:, 4096 + 1024 * i:5120 + 1024 * i].rearrange("p (s m k) -> p s m k", s=2, m=4) for i in range(2)]

        filled = [sem(f"bank_filled{b}") for b in range(8)]
        drained = [sem(f"bank_drained{b}") for b in range(8)]
        bk = Banks(filled, drained, psum)
        sigs = {}

        def sig(name, n, step=1):
            sigs[name] = Signal(sem(name), n, step)
            return sigs[name]

        keep_loaded = sem("keep_loaded")
        ptab_loaded = sem("ptab_loaded")
        pidx_loaded = sem("pidx_loaded")
        x_loaded = sem("x_loaded")
        y_stored = sem("y_stored")
        init_done = sem("init_done")
        final_step = sem("final_step")
        pidx_moved = sem("pidx_moved")
        final_ready = sem("final_ready")
        final_ms = sem("final_ms")
        final_root = sem("final_root")
        gfin_loaded = sem("gfin_loaded")
        phase_done = sem("phase_done")
        NPH, ARRIVE = 5, 4
        dve_step = Steps(sem("dve_step"))
        mixc_loaded = sig("mixc_loaded", 1, 16)
        rows_loaded = sig("rows_loaded", 3, 16)
        params_loaded = sig("params_loaded", 4, 16)
        crow_loaded = sig("crow_loaded", 1, 16)
        w_loaded = [sem(f"w_loaded{i}") for i in range(3)]
        ms_ready = sig("ms_ready", 12)
        root_ready = sig("root_ready", 12)
        xn_ready = sig("xn_ready", 6)
        gate_arg = sig("gate_arg", 1)
        gate_exp = sig("gate_exp", 1)
        gates_ready = sig("gates_ready", 1)
        pad_zeroed = sig("pad_zeroed", 1)
        conv_done = sig("conv_done", 3)
        silu_done = sig("silu_done", 3)
        tile_rows = sig("tile_rows", 3)
        gg_ready = sig("gg_ready", 3)
        lm_ready = sig("lm_ready", 14)
        gm_ready = sig("gm_ready", 1)
        state_zeroed = sig("state_zeroed", 1)
        spread_ready = sig("spread_ready", 1)
        vnm_ready = sig("vnm_ready", 2)
        s0_loaded = sig("s0_loaded", 8, 16)
        states_ready = sig("states_ready", 2)
        onorm_ready = sig("onorm_ready", 3)
        lfb_ready = sig("lfb_ready", 1)
        negmax_ready = sig("negmax_ready", 8)
        exp_ready = sig("exp_ready", 8)
        probs_ready = sig("probs_ready", 8)
        lfg_loaded = sig("lfg_loaded", 1, 16)
        q_zeroed = sig("q_zeroed", 1)
        q_spread = sig("q_spread", 2)
        s_negmax = sig("s_negmax", 2)
        s_exp = sig("s_exp", 2)
        s_probs = sig("s_probs", 2)
        ring_loaded = [sem(f"ring_loaded{i}") for i in range(4)]
        v_used = sig("v_used", 16)
        wo_loaded = sig("wo_loaded", 1, 16)
        wq_loaded = sig("wq_loaded", 4, 16)
        keys_loaded = sig("keys_loaded", 2, 16)
        top_done = sig("top_done", 3)
        fv_ready = sig("fv_ready", 3)
        fv_exp = sig("fv_exp", 3)
        ijw_ready = sig("ijw_ready", 3)
        stored = sig("stored", STORES, 16)
        hot_ready = sem("hot_ready")
        gate_filled = sem("gate_filled")
        gate_out = sem("gate_out")
        u_loaded = [sem(f"u_loaded{i}") for i in range(2)]
        v_loaded = [sem(f"v_loaded{i}") for i in range(2)]
        ut_filled = [sem(f"ut_filled{i}") for i in range(2)]
        ut_ready = [sem(f"ut_ready{i}") for i in range(2)]
        h_filled = sem("h_filled")
        gelu_done = sem("gelu_done")
        at_ready = sem("at_ready")
        y_done = sem("y_done")
        yt_ready = sig("yt_ready", 1)

        bk.plan("vecT", 0)
        for i in range(6):
            bk.plan("xT_mix", i)
        bk.plan("csT", 0)
        for t in range(3):
            bk.plan("fv", t)
        for t in range(3):
            bk.plan("ba", t)
            bk.plan("z", t)
        for i in range(8):
            bk.plan("pT", i)
        for t in range(3):
            bk.plan("ktok", t)
        for t in range(3):
            bk.plan("dv", t)
        for i in range(8, 16):
            bk.plan("pT", i)
        for t in range(3):
            bk.plan("tk", (0, t))
        for i in range(16, 20):
            bk.plan("pT", i)
        for t in range(3):
            bk.plan("tk", (1, t))
        for i in range(3):
            bk.plan("craw", i)
        for t in range(3):
            bk.plan("tk", (2, t))
        LEV = ((1, 2, 4, 8, 16, 32), (1, 2, 4, 8, 16, 32), (1, 2))
        bk.plan("gl", 0)
        bk.plan("gls", 0)
        for t in range(3):
            nb = 2 if t < 2 else 1
            bk.plan("gcs", t)
            bk.plan("dec", t, nb)
            for kind in range(4):
                bk.plan("tr", (t, kind), nb)
            bk.plan("kk", t, 4 if t < 2 else 1)
            for s in LEV[t]:
                bk.plan("p1", (t, s), nb)
                if s > 1:
                    if s != LEV[t][-1]:
                        bk.plan("dd", (t, s), nb)
                    bk.plan("dt", (t, s), nb)
            bk.plan("wT", t, nb)
            if t == 1:
                for c in range(4):
                    bk.plan("vn", c)
                    bk.plan("oo", c)
                    bk.plan("st", c)
        bk.plan("vn", 4)
        bk.plan("oo", 4)
        for h in range(NH):
            bk.plan("st", 4 + h)
        for t in range(3):
            bk.plan("oT", t)
        bk.plan("S", (0, 0))
        bk.plan("S", (0, 1))
        for u in range(8):
            if u < 7:
                bk.plan("S", (u + 1, 0))
                bk.plan("S", (u + 1, 1))
            bk.plan("PT", u)
            bk.plan("O", u)
        bk.plan("lfT", 0)
        for g in range(2):
            bk.plan("SS", g, banks=(0, 1))
            bk.plan("SN", g, banks=(2,))
            for b in range(B):
                bk.plan("kTs", (g, b), banks=(3, 4, 5, 6))
            bk.plan("PTs", g, banks=(3, 4, 5))
            bk.plan("OS", g, banks=(7,))
        for i in range(6):
            bk.plan("y", i)
        for i in range(6):
            bk.plan("xT_ffn", i)
        for i in range(4):
            bk.plan("kyT", i)
        for i in range(16):
            bk.plan("qf", i)
        for t in range(3):
            for g in range(4):
                bk.plan("sc", (t, g))
        for t in range(3):
            bk.plan("ijwT", t)
        for i in range(6):
            bk.plan("yb", i)

        CHUNKS = [(512, 260), (3076, 528), (0, 512), (772, 512), (1284, 256), (1540, 512), (2052, 512), (2564, 512)]
        LASTUSE = [("fv", 2), ("z", 2), ("pT", 3), ("pT", 7), ("dv", 2), ("pT", 11), ("pT", 15), ("pT", 19)]
        WUSES = [3, 3, 2]
        CACHE = [(g, kv, b) for g in range(2) for kv in range(2) for b in range(B)]
        RINC = [8 * 16, 2 * 16]
        rcount, RUSE = [0] * 4, {}
        for i, (g, kv, b) in enumerate(CACHE):
            rcount[i % 4] += RINC[g]
            RUSE[(g, kv, b)] = (i % 4, rcount[i % 4])

        def wchunk(i):
            return wring[i % 3][:, 0:DC * CHUNKS[i][1]].rearrange("p (c n) -> p c n", c=DC)

        def w_wait(eng, l, i):
            eng.wait_ge(w_loaded[i % 3], (l * WUSES[i % 3] + i // 3 + 1) * 16)

        def ring_wait(eng, l, key):
            s, c = RUSE[key]
            eng.wait_ge(ring_loaded[s], l * rcount[s] + c)

        def phase(eng, l, k, arrive=True):
            if arrive:
                eng.drain().then_inc(phase_done, 1)
            eng.wait_ge(phase_done, l * (NPH * ARRIVE) + ARRIVE * (k + 1))

        def row0(l, ap):
            return ap[l:l + 1]

        block = ctx.enter_context(nc.Block())

        @block.sync
        def _(sp):
            sp.dma_start(keep[:, :], a["c_keep"]).then_inc(keep_loaded, 16)
            for t, (n0, r) in enumerate(TILES):
                src = a["x_prompt"][0, n0:n0 + r, :] if t < 2 else a["x_sample"].rearrange("b t d -> (b t) d")
                sp.dma_start(x[0:r, t, :], src).then_inc(x_loaded, 16)
            sp.dma_start(ptab[:, :], a["page_table"].rearrange("(o b) g -> o (b g)", o=1)).then_inc(ptab_loaded, 16)
            sp.wait_ge(ptab_loaded, 16)
            sp.wait_ge(init_done, 1)
            for l in range(DEPTH):
                if l:
                    sp.wait_ge(phase_done, l * (NPH * ARRIVE))
                mixc_loaded.by(sp.dma_start(mixc, a["c_mix"]))
                rows_loaded.by(sp.dma_start(vrows[0:48, :], row0(l, a["conv_w"]).rearrange(
                    "o i (c p) -> (o i c) p", p=P)))
                rows_loaded.by(sp.dma_start(vrows[48:56, :], row0(l, a["norm_mix"]).rearrange(
                    "o (c p) -> (o c) p", p=P)))
                rows_loaded.by(sp.dma_start(vrows[56:64, :], row0(l, a["norm_ffn"]).rearrange(
                    "o (c p) -> (o c) p", p=P)))
                for dst, name, w in ((fbias[:, 0:4], "b_fox_f", 4), (fbias[:, 4:12], "dt_bias", 8), (alog, "a_log", 8),
                                     (dnorm, "delta_norm", HD)):
                    params_loaded.by(sp.dma_start(dst, row0(l, a[name]).to_broadcast([P, w])))
                crow_loaded.by(sp.dma_start(crow[0:24, :], row0(l, a["state_conv"]).rearrange("o b i c -> (o b i) c")))
                for i, (c0, w) in enumerate(CHUNKS):
                    if i >= 3:
                        bk.wait_full(sp, l, *LASTUSE[i - 3])
                    src = row0(l, a["w_in"]).rearrange("o (c p) n -> (o p) c n", p=P)[:, :, c0:c0 + w]
                    sp.dma_start(wchunk(i), src).then_inc(w_loaded[i % 3], 16)
                phase(sp, l, 0, arrive=False)
                bk.wait_full(sp, l, "st", 3)
                for b in range(B):
                    s0_loaded.by(sp.dma_start(
                        s0[0:HD, 512 * b:512 * (b + 1)].rearrange("p (h v) -> p h v", h=NH),
                        row0(l, a["state_delta"])[:, b].rearrange("o h d v -> (o d) h v")))
                phase(sp, l, 1, arrive=False)
                for i, (g, kv, b) in enumerate(CACHE):
                    if i >= 4:
                        g0, kv0, b0 = CACHE[i - 4]
                        if kv0:
                            v_used.wait(sp, l, B * g0 + b0 + 1)
                        else:
                            bk.wait_full(sp, l, "kTs", (g0, b0), 3)
                    dst = ring[i % 4]
                    if g == 0:
                        for pg in range(PAGES):
                            page = sp.value_load(ptab[0:1, b * PAGES + pg:b * PAGES + pg + 1], min_val=0,
                                                 max_val=NPOOL - 1)
                            src = a["cache_fox_kv"].rearrange("l n s k h d -> (l n) s k (h d)")[
                                bass.ds(page + l * NPOOL, 1), :, kv, :].rearrange("o s c -> (o s) c")
                            sp.dma_start(dst[:, pg, :], src).then_inc(ring_loaded[i % 4], 16)
                    else:
                        src = row0(l, a["cache_dil_kv"])[:, b, :, kv].rearrange("o s h d -> (o s) (h d)")
                        sp.dma_start(dst[:, 0, :], src[0:512, :].rearrange("(m s) c -> m s c", s=16)[:, 0:4, :])\
                            .then_inc(ring_loaded[i % 4], 16)
                        sp.dma_start(dst[:, 1:DILK, :], src[512:PAST, :].rearrange("(k s) c -> s k c", s=P))\
                            .then_inc(ring_loaded[i % 4], 16)
                phase(sp, l, 2, arrive=False)
                wo_loaded.by(sp.dma_start(wo, row0(l, a["w_out"]).rearrange("o (c p) n -> (o p) c n", p=P)))
                for i in range(4):
                    wq_loaded.by(sp.dma_start(wq[:, :, 512 * i:512 * (i + 1)], row0(l, a["peer_wq"]).rearrange(
                        "o (c p) n -> (o p) c n", p=P)[:, :, 512 * i:512 * (i + 1)]))
                for i in range(2):
                    keys_loaded.by(sp.dma_start(keysr[:, 8 * i:8 * i + 8, :], row0(l, a["peer_keys"]).rearrange(
                        "o h c k d -> (o k) (h c) d")[:, 8 * i:8 * i + 8, :]))
                phase(sp, l, 3, arrive=False)

                def load_u(j, s, turned):
                    rows = row0(l, a["peer_u"]).rearrange("o (i j) d -> (o i) j d", j=NCH)[:, j, :]
                    if turned is not None:
                        sp.wait_ge(ut_filled[1], turned)
                    sp.dma_start(ubuf[s], rows).then_inc(u_loaded[s], 16)

                def load_v(j, s, used):
                    rows = row0(l, a["peer_v"]).rearrange("o (i j) d -> (o i) j d", j=NCH)[:, j, :]
                    if used is not None:
                        sp.wait_ge(y_done, used)
                    sp.dma_start(vbuf[s], rows).then_inc(v_loaded[s], 16)

                first = l * NCH
                for j in range(2):
                    load_u(j, j, None)
                    load_v(j, j, None)
                load_u(2, 0, first + 1)
                with sp.Fori(1, NCH // 2 - 1) as m:
                    for s in range(2):
                        load_u(bass.ds(m * 2 + (s + 1), 1), 1 - s, m * 2 + (first + s))
                        load_v(bass.ds(m * 2 + s, 1), s, m * 2 + (first + s - 1))
                load_u(NCH - 1, 1, first + NCH - 2)
                load_v(NCH - 2, 0, first + NCH - 3)
                load_v(NCH - 1, 1, first + NCH - 2)
            sp.wait_ge(phase_done, DEPTH * NPH * ARRIVE)
            sp.dma_start(arena[:, 0:D], a["norm_final"].rearrange("(o n) -> o n", o=1).to_broadcast([P, D]))\
                .then_inc(gfin_loaded, 16)

        @block.gpsimd
        def _(pool):
            outs = a["outs"]
            pool.wait_ge(ptab_loaded, 16)
            pool.dma_start(pidx[:, 0:1], a["page_table"].rearrange("b g -> (b g)").rearrange("(n o) -> n o", o=1))\
                .then_inc(pidx_loaded, 16)
            pool.wait_ge(pidx_loaded, 16)
            for l in range(DEPTH):
                gates_ready.wait(pool, l, 1)
                lo = row0(l, outs["fox_logf_prompt"]).rearrange("o b s h -> (o b s) h")
                stored.by(pool.dma_start(lo[0:128, :], lgv[:, 0, 0:4]))
                stored.by(pool.dma_start(lo[128:256, :], lgv[:, 1, 0:4]))
                stored.by(pool.dma_start(row0(l, outs["fox_logf_sample"]).rearrange("o b s h -> (o b s) h"),
                                         lgv[0:NS, 2, 0:4]))
                for t in range(3):
                    bk.wait_out(pool, l, "ktok", t)
                    bk.wait_out(pool, l, "fv", t)
                    bk.wait_out(pool, l, "dv", t)
                    for g, name in ((0, "fox_kv"), (1, "dil_kv")):
                        dst = row0(l, outs[name + ("_prompt" if t < 2 else "_sample")])\
                            .rearrange("o b s k h d -> (o b s) (k h d)")
                        n0, r = TILES[t] if t < 2 else (0, NS)
                        stored.by(pool.dma_start(dst[n0:n0 + r, :], kvrow[0:r, t, g, :]))
                for i in range(3):
                    bk.wait_out(pool, l, "craw", i)
                stored.by(pool.dma_start(row0(l, outs["conv_state_prompt"]).rearrange("o b i c -> (o b i) c"),
                                         crow[0:3, :]))
                for b in range(B):
                    stored.by(pool.dma_start(row0(l, outs["conv_state_sample"])[:, b].rearrange("o i c -> (o i) c"),
                                             crow[7 + 7 * b:10 + 7 * b, :]))
                NP0 = 3 + 6 + 9
                stored.wait(pool, l, NP0)
                phase(pool, l, 0)
                states_ready.wait(pool, l, 1)
                stored.by(pool.dma_start(row0(l, outs["delta_state_prompt"]).rearrange("o b h d v -> (o b d) h v"),
                                         st[0:HD, :].rearrange("p (h v) -> p h v", h=NH)))
                states_ready.wait(pool, l, 2)
                for b in range(B):
                    stored.by(pool.dma_start(
                        row0(l, outs["delta_state_sample"])[:, b].rearrange("o h d v -> (o d) h v"),
                        s0[0:HD, 512 * b:512 * (b + 1)].rearrange("p (h v) -> p h v", h=NH)))
                stored.wait(pool, l, NP0 + 9)
                phase(pool, l, 1)
                if l:
                    pool.wait_ge(pidx_moved, l)
                q_zeroed.by(pool.memset(side[:, 0:2304], 0.0))
                lfg_loaded.by(pool.indirect_dma_start(
                    lfg[0:B * PAGES, :], None, a["cache_fox_logf"].rearrange("l n s h -> (l n) (s h)"),
                    bass.IndirectOffsetOnAxis(ap=pidx[:, 0:1].bitcast(U32), axis=0)))
                lfg_loaded.wait(pool, l, 1)
                pool.tensor_scalar(pidx[:, 0:1], pidx[:, 0:1], float(NPOOL), None, ALU.add).then_inc(pidx_moved, 1)
                phase(pool, l, 2)
                phase(pool, l, 3)
                phase(pool, l, 4)
            for t, (n0, r) in enumerate(TILES):
                dst = outs["y_prompt"][0, n0:n0 + r, :] if t < 2 else outs["y_sample"].rearrange("b t d -> (b t) d")
                pool.wait_ge(final_ready, t + 1)
                pool.dma_start(dst, arena[0:r, D * (t + 1):D * (t + 2)]).then_inc(y_stored, 16)
            pool.wait_ge(y_stored, 48)

        @block.tensor
        def _(pe):
            pe.wait_ge(keep_loaded, 16)

            def mm(out, lhsT, rhs, start=True, stop=True):
                return pe.matmul(out, lhsT, rhs, start=start, stop=stop)

            def transposes(l, name, i, k, pieces):
                bk.wait_free(pe, l, name, i, k)
                o = 0
                for piece in pieces:
                    r, w = piece.shape[0], piece.shape[1]
                    last = pe.transpose(bk.ap(name, i, k)[0:w, o:o + r], piece, ident[0:r, 0:r])
                    o += r
                last.then_inc(bk.full_sem(name, i, k), 1)

            def norm_transposes(l, name, base):
                for t, (n0, r) in enumerate(TILES):
                    xn_ready.wait(pe, l, base + t + 1)
                    for hf in range(2):
                        transposes(l, name, 2 * t + hf, 0,
                                   [xn[0:r, t % 2, (4 * hf + k) * P:(4 * hf + k + 1) * P] for k in range(4)])

            def token_rows(l, name, t, chunk, c0, w):
                n0, r = TILES[t]
                bk.wait_free(pe, l, name, t)
                for c in range(DC):
                    last = mm(bk.ap(name, t)[0:r, 0:w], hT[:, c, n0:n0 + r], wchunk(chunk)[:, c, c0:c0 + w],
                              c == 0, c == DC - 1)
                last.then_inc(bk.full_sem(name, t), 1)

            def feature_rows(l, chunk, i0):
                w_wait(pe, l, chunk)
                for i in range(i0, i0 + 4):
                    bk.wait_free(pe, l, "pT", i)
                    o = (i - i0) * P
                    for c in range(DC):
                        last = mm(bk.ap("pT", i)[:, 0:N], wchunk(chunk)[:, c, o:o + P], hT[:, c, :],
                                  c == 0, c == DC - 1)
                    last.then_inc(bk.full_sem("pT", i), 1)

            def project(l):
                rows_loaded.wait(pe, l, 3)
                transposes(l, "vecT", 0, 0, [vrows[0:64, :]])
                norm_transposes(l, "xT_mix", 0)
                crow_loaded.wait(pe, l, 1)
                transposes(l, "csT", 0, 0, [crow[0:24, c * P:(c + 1) * P] for c in range(12)])
                bk.wait_out(pe, l, "xT_mix", 5)
                w_wait(pe, l, 0)
                for t in range(3):
                    token_rows(l, "fv", t, 0, 0, 260)
                w_wait(pe, l, 1)
                for t in range(3):
                    token_rows(l, "ba", t, 1, 0, 16)
                    token_rows(l, "z", t, 1, 16, 512)
                feature_rows(l, 2, 0)
                feature_rows(l, 3, 4)
                for t, (n0, r) in enumerate(TILES):
                    if t == 0:
                        for i in (2, 3, 6, 7):
                            bk.wait_out(pe, l, "pT", i)
                    transposes(l, "ktok", t, 0, [qkT[:, i, n0:n0 + r] for i in (2, 3, 6, 7)])
                w_wait(pe, l, 4)
                for t in range(3):
                    token_rows(l, "dv", t, 4, 0, 256)
                feature_rows(l, 5, 8)
                feature_rows(l, 6, 12)
                conv_rows(l, 0)
                feature_rows(l, 7, 16)
                conv_rows(l, 1)
                for i in range(3):
                    for c in range(4 * i, 4 * i + 4):
                        bk.wait_out(pe, l, "pT", 8 + c)
                    transposes(l, "craw", i, 0, [cT[:, c, SEQ:SEQ + 59] for c in range(4 * i, 4 * i + 4)])
                conv_rows(l, 2)

            def conv_rows(l, s):
                silu_done.wait(pe, l, s + 1)
                for t, (n0, r) in enumerate(TILES):
                    transposes(l, "tk", (s, t), 0, [cS[:, 4 * s + k, n0:n0 + r] for k in range(4)])

            def each_head(l, name, i, W, r, parts):
                hpb = 512 // W if W > 32 else NH
                for k in range(NH // hpb):
                    bk.wait_free(pe, l, name, i, k)
                    for hh in range(hpb):
                        h = k * hpb + hh
                        lhsT, rhs = parts(h)
                        last = mm(bk.ap(name, i, k)[0:r, hh * W:(hh + 1) * W], lhsT, rhs)
                    last.then_inc(bk.full_sem(name, i, k), 1)

            def delta_tile(l, t):
                r = W = TILES[t][1]
                q = per[t]
                le, gt = (C("le64"), C("gt64")) if t < 2 else (C("le4"), C("gt4"))
                bk.wait_free(pe, l, "gcs", t)
                mm(bk.ap("gcs", t)[0:r, 0:8], le[0:r, :], lgv[0:r, t, 4:12])
                mm(bk.ap("gcs", t)[0:r, 8:16], gt[0:r, :], lgv[0:r, t, 4:12]).then_inc(bk.full_sem("gcs", t), 1)
                gg_ready.wait(pe, l, t + 1)
                each_head(l, "dec", t, W, r, lambda h: (GG[0:r, h * W:(h + 1) * W], le[0:r, :]))
                tile_rows.wait(pe, l, t + 1)
                rows = (tok[:, t, 1, :], kb, tok[:, t, 0, :], qe)
                for kind in range(4):
                    for k in range(2 if t < 2 else 1):
                        hs = range(4 * k, 4 * k + 4) if t < 2 else range(NH)
                        transposes(l, "tr", (t, kind), k, [rows[kind][0:r, h * HD:(h + 1) * HD] for h in hs])
                for kind in range(3):
                    for k in range(2 if t < 2 else 1):
                        bk.wait_out(pe, l, "tr", (t, kind), k)
                kqv = kq[0:HD, 0:16 * W].rearrange("p (s h w) -> p s h w", s=2, h=NH)
                hpb = 256 // W
                for k in range(NH // hpb):
                    bk.wait_free(pe, l, "kk", t, k)
                    for hh in range(hpb):
                        h = k * hpb + hh
                        last = mm(bk.ap("kk", t, k)[0:r, hh * 2 * W:(hh + 1) * 2 * W], kT[0:HD, h * W:(h + 1) * W],
                                  kqv[:, :, h, :])
                    last.then_inc(bk.full_sem("kk", t, k), 1)
                for n, s in enumerate(LEV[t]):
                    lm_ready.wait(pe, l, 6 * t + n + 1)
                    nb = 2 if t < 2 else 1
                    if n:
                        if n > 1:
                            for k in range(nb):
                                bk.wait_out(pe, l, "dd", (t, LEV[t][n - 1]), k)
                                bk.wait_out(pe, l, "dt", (t, LEV[t][n - 1]), k)
                        else:
                            for k in range(nb):
                                bk.wait_out(pe, l, "p1", (t, 1), k)
                    each_head(l, "p1", (t, s), W, r,
                              lambda h: (LM[0:r, h * W:(h + 1) * W], T0[0:r, h * W:(h + 1) * W] if n else
                                         ident[0:r, 0:W]))
                    if n:
                        for k in range(nb):
                            bk.wait_out(pe, l, "p1", (t, s), k)
                        if s != LEV[t][-1]:
                            each_head(l, "dd", (t, s), W, r, lambda h: (q["TT"][0:r, h * W:(h + 1) * W],
                                                                        P1[0:r, h * W:(h + 1) * W]))
                        each_head(l, "dt", (t, s), W, r, lambda h: (P1[0:r, h * W:(h + 1) * W],
                                                                    q["TT"][0:r, h * W:(h + 1) * W]))
                for k in range(nb):
                    bk.wait_out(pe, l, "dt", (t, LEV[t][-1]), k)
                each_head(l, "wT", t, W, HD, lambda h: (kbe[0:r, h * HD:(h + 1) * HD], q["TT"][0:r, h * W:(h + 1) * W]))

            def delta_chunk(l, c):
                t, hf = c // 2, c % 2
                q = per[t]
                rows = slice(64 * hf, 64 * hf + 64)
                if c == 0:
                    state_zeroed.wait(pe, l, 1)
                else:
                    bk.wait_out(pe, l, "st", c - 1)
                for k in range(2):
                    bk.wait_out(pe, l, "wT", t, k)
                    bk.wait_out(pe, l, "tr", (t, 3), k)
                bk.wait_free(pe, l, "vn", c)
                for h in range(NH):
                    o = bk.ap("vn", c)[:, h * HD:(h + 1) * HD]
                    mm(o, q["TT"][:, h * P:(h + 1) * P], q["vb"][:, h * HD:(h + 1) * HD], True, False)
                    last = mm(o, q["nwT"][0:HD, h * P:(h + 1) * P], st[0:HD, h * HD:(h + 1) * HD], False, True)
                last.then_inc(bk.full_sem("vn", c), 1)
                bk.wait_free(pe, l, "oo", c)
                bk.wait_out(pe, l, "vn", c)
                for h in range(NH):
                    o = bk.ap("oo", c)[:, h * HD:(h + 1) * HD]
                    mm(o, q["qeT"][0:HD, h * P:(h + 1) * P], st[0:HD, h * HD:(h + 1) * HD], True, False)
                    last = mm(o, q["attnT"][:, h * P:(h + 1) * P], vnw[t][:, h * HD:(h + 1) * HD], False, True)
                last.then_inc(bk.full_sem("oo", c), 1)
                bk.wait_free(pe, l, "st", c)
                for h in range(NH):
                    last = mm(bk.ap("st", c)[0:HD, h * HD:(h + 1) * HD], q["kd"][rows, h * HD:(h + 1) * HD],
                              vnw[t][rows, h * HD:(h + 1) * HD])
                last.then_inc(bk.full_sem("st", c), 1)

            def delta_sample(l):
                q = per[2]
                s0_loaded.wait(pe, l, 8)
                spread_ready.wait(pe, l, 1)
                bk.wait_free(pe, l, "vn", 4)
                for h in range(NH):
                    o = bk.ap("vn", 4)[0:NS, h * HD:(h + 1) * HD]
                    mm(o, q["TT"][0:NS, h * NS:(h + 1) * NS], q["vb"][0:NS, h * HD:(h + 1) * HD], True, False)
                    for b in range(B):
                        last = mm(o, nwm[0:HD, (h * B + b) * NS:(h * B + b + 1) * NS],
                                  s0[0:HD, b * 512 + h * HD:b * 512 + (h + 1) * HD], False, b == B - 1)
                last.then_inc(bk.full_sem("vn", 4), 1)
                bk.wait_free(pe, l, "oo", 4)
                bk.wait_out(pe, l, "vn", 4)
                for h in range(NH):
                    o = bk.ap("oo", 4)[0:NS, h * HD:(h + 1) * HD]
                    for b in range(B):
                        mm(o, qem[0:HD, (h * B + b) * NS:(h * B + b + 1) * NS],
                           s0[0:HD, b * 512 + h * HD:b * 512 + (h + 1) * HD], b == 0, False)
                    last = mm(o, q["attnT"][0:NS, h * NS:(h + 1) * NS], vnw[2][0:NS, h * HD:(h + 1) * HD], False, True)
                last.then_inc(bk.full_sem("oo", 4), 1)
                for h in range(NH):
                    vnm_ready.wait(pe, l, h // 4 + 1)
                    bk.wait_free(pe, l, "st", 4 + h)
                    mm(bk.ap("st", 4 + h)[0:HD, :], q["kd"][0:NS, h * HD:(h + 1) * HD],
                       vnm[0:NS, (h % 4) * 512:(h % 4 + 1) * 512]).then_inc(bk.full_sem("st", 4 + h), 1)

            def delta(l):
                gates_ready.wait(pe, l, 1)
                bk.wait_free(pe, l, "gl", 0)
                for c in range(4):
                    last = mm(bk.ap("gl")[0:HD, 8 * c:8 * c + 8], C("half")[:, 64 * (c % 2):64 * (c % 2) + 64],
                              lgv[:, c // 2, 4:12])
                last.then_inc(bk.full_sem("gl"), 1)
                gm_ready.wait(pe, l, 1)
                bk.wait_free(pe, l, "gls", 0)
                mm(bk.ap("gls")[0:HD, 0:64], ones[0:NS, 0:HD], gm[0:NS, :]).then_inc(bk.full_sem("gls"), 1)
                delta_tile(l, 0)
                delta_tile(l, 1)
                for c in range(4):
                    delta_chunk(l, c)
                delta_tile(l, 2)
                delta_sample(l)
                for t, (n0, r) in enumerate(TILES):
                    onorm_ready.wait(pe, l, t + 1)
                    transposes(l, "oT", t, 0, [otok[t][0:r, k * P:(k + 1) * P] for k in range(4)])

            def prompt_scores(l, u):
                g, hp, qt = u // 4, (u // 2) % 2, u % 2
                KW = P * (qt + 1)
                for ah in range(2):
                    po = 64 * ah
                    bk.wait_free(pe, l, "S", (u, ah))
                    o = bk.ap("S", (u, ah))
                    last = mm(o[:, 0:KW], qkT[po:po + 64, 4 * g + hp, qt * P:(qt + 1) * P],
                              qkT[po:po + 64, 4 * g + 2 + hp, 0:KW], True, g == 1)
                    if g == 0:
                        for kt in range(qt + 1):
                            for tt in range(kt + 1):
                                last = mm(o[:, kt * P:(kt + 1) * P], lfb[:, tt, 2 * hp + ah, :],
                                          C("neg_le") if tt == kt else C("neg_one"), False, (kt, tt) == (qt, qt))
                    last.then_inc(bk.full_sem("S", (u, ah)), 1)

            def prompt_values(l, u):
                g, hp, qt = u // 4, (u // 2) % 2, u % 2
                probs_ready.wait(pe, l, u + 1)
                transposes(l, "PT", u, 0, [PRp[u % 2][:, ah, kt * P:(kt + 1) * P]
                                           for kt in range(qt + 1) for ah in range(2)])
                bk.wait_out(pe, l, "PT", u)
                bk.wait_free(pe, l, "O", u)
                for kt in range(qt + 1):
                    last = mm(bk.ap("O", u)[:, 0:256], kvrow[:, kt, g, 256 + hp * P:256 + (hp + 1) * P],
                              PTp[u % 2][:, kt, :, :], kt == 0, kt == qt)
                last.then_inc(bk.full_sem("O", u), 1)

            def sample_attention(l, g):
                q_spread.wait(pe, l, g + 1)
                nk = PAGES if g == 0 else DILK
                widths = (512, 512) if g == 0 else (512, 128)
                for k in range(2):
                    if k == 0:
                        bk.wait_free(pe, l, "SS", g, 0)
                    else:
                        bk.wait_free(pe, l, "SN", g)
                banks = psum[:, 0:2, :]
                if g == 0:
                    bk.wait_out(pe, l, "lfT", 0)
                    for pg in range(PAGES - 1, -1, -1):
                        if pg >= 4:
                            w = P * (pg - 3)
                            mm(banks[:, 1, 0:w], lfr[:, pg, :], C("ones_gt")[:, 1024 - w:1024], pg == 7, False)
                            mm(banks[:, 0, :], lfr[:, pg, :], C("ones_gt")[:, 0:512], pg == 7, False)
                        else:
                            w = P * (pg + 1)
                            mm(banks[:, 0, 0:w], lfr[:, pg, :], C("ones_gt")[:, 1024 - w:1024], False, False)

                def scores(b):
                    for hp in range(2):
                        for k in range(2):
                            bk.wait_out(pe, l, "kTs", (g, b), 2 * hp + k)
                            w = widths[k]
                            fin = b == B - 1 and hp == 1
                            last = mm(banks[:, k, 0:w], QZ[:, hp, b, :], KT[b % 2][:, hp, 512 * k:512 * k + w],
                                      g == 1 and b == 0 and hp == 0, fin)
                            if fin:
                                last.then_inc(bk.full_sem("SS", g, k), 1)

                for b in range(B):
                    ring_wait(pe, l, (g, 0, b))
                    tile = ring[RUSE[(g, 0, b)][0]]
                    for hp in range(2):
                        for k in range(2):
                            tiles = range(4 * k, min(nk, 4 * k + 4))
                            transposes(l, "kTs", (g, b), 2 * hp + k, [tile[:, kt, hp * P:(hp + 1) * P] for kt in tiles])
                    if b:
                        scores(b - 1)
                scores(B - 1)
                bk.wait_free(pe, l, "SN", g)
                o = bk.ap("SN", g)[:, 0:NS]
                mm(o, QA[:, 0, :], qkT[:, 4 * g + 2, SEQ:N], True, False)
                last = mm(o, QA[:, 1, :], qkT[:, 4 * g + 3, SEQ:N], False, g == 1)
                if g == 0:
                    last = mm(o, lfrn[0:NS, :], C("neg_le4")[0:NS, :], False, True)
                last.then_inc(bk.full_sem("SN", g), 1)
                s_probs.wait(pe, l, g + 1)
                for k in range(2):
                    transposes(l, "PTs", g, k, [PRs[:, kt * P:(kt + 1) * P] for kt in range(4 * k, min(nk, 4 * k + 4))])
                transposes(l, "PTs", g, 2, [PRs[:, nk * P:nk * P + NS]])
                for k in range(3):
                    bk.wait_out(pe, l, "PTs", g, k)
                bk.wait_free(pe, l, "OS", g)
                for b in range(B):
                    ring_wait(pe, l, (g, 1, b))
                    tile = ring[RUSE[(g, 1, b)][0]]
                    for hp in range(2):
                        o = bk.ap("OS", g)[:, hp * P + 16 * b:hp * P + 16 * b + 16]
                        for kt in range(nk):
                            mm(o, tile[:, kt, hp * P:(hp + 1) * P], PTs[:, kt, 16 * b:16 * b + 16], kt == 0, False)
                        last = mm(o, kvrow[0:NS, 2, g, 256 + hp * P:256 + (hp + 1) * P],
                                  PTn[0:NS, 16 * b:16 * b + 16], False, True)
                    v_used.by(last)
                mm(bk.ap("OS", g)[:, 256:272], ident, ones[:, 0:16]).then_inc(bk.full_sem("OS", g), 1)

            def attention(l):
                lfb_ready.wait(pe, l, 1)
                prompt_scores(l, 0)
                for u in range(8):
                    if u < 7:
                        prompt_scores(l, u + 1)
                    prompt_values(l, u)
                lfg_loaded.wait(pe, l, 1)
                transposes(l, "lfT", 0, 0, [lfg[0:B * PAGES, :].rearrange("p (s h) -> p h s", h=4)[:, h, :]
                                            for h in range(4)])
                for g in range(2):
                    sample_attention(l, g)

            def out_projection(l):
                wo_loaded.wait(pe, l, 1)
                for t, (n0, r) in enumerate(TILES):
                    for hf in range(2):
                        bk.wait_free(pe, l, "y", 2 * t + hf)
                        for c in range(DC):
                            last = mm(bk.ap("y", 2 * t + hf)[0:r, :], mixT[:, c, n0:n0 + r],
                                      wo[:, c, 512 * hf:512 * hf + 512], c == 0, c == DC - 1)
                        last.then_inc(bk.full_sem("y", 2 * t + hf), 1)

            def retrieval(l):
                norm_transposes(l, "xT_ffn", 3)
                keys_loaded.wait(pe, l, 2)
                for i in range(4):
                    transposes(l, "kyT", i, 0, [keysr[:, 4 * i + k, :] for k in range(4)])
                bk.wait_out(pe, l, "xT_ffn", 5)
                wq_loaded.wait(pe, l, 4)
                for i in range(16):
                    bk.wait_free(pe, l, "qf", i)
                    for c in range(DC):
                        last = mm(bk.ap("qf", i)[:, 0:N], wq[:, c, i * P:(i + 1) * P], hT[:, c, :], c == 0, c == DC - 1)
                    last.then_inc(bk.full_sem("qf", i), 1)
                for i in range(4):
                    bk.wait_out(pe, l, "kyT", i)
                for i in range(16):
                    bk.wait_out(pe, l, "qf", i)
                for t, (n0, r) in enumerate(TILES):
                    for g in range(4):
                        bk.wait_free(pe, l, "sc", (t, g))
                        for k in range(4):
                            i = 4 * g + k
                            last = mm(bk.ap("sc", (t, g))[0:r, k * P:(k + 1) * P], qTf[:, i, n0:n0 + r], keysT[:, i, :])
                        last.then_inc(bk.full_sem("sc", (t, g)), 1)
                for t, (n0, r) in enumerate(TILES):
                    ijw_ready.wait(pe, l, t + 1)
                    transposes(l, "ijwT", t, 0, [ijw[0:r, s, :] for s in range(3)])

            def gates(l):
                def group(i, s, reuse):
                    pe.wait_ge(hot_ready, i + 1)
                    if reuse:
                        pe.wait_ge(gate_out, i + -1)
                    for m in range(4):
                        last = mm(psum[:, 5 + s, m * P:(m + 1) * P], hot[s][:, 0, m, :], hot[s][:, 1, m, :])
                    last.then_inc(gate_filled, 1)

                for s in range(2):
                    group(l * (N // 4) + s, s, False)
                with pe.Fori(1, N // 8) as m:
                    for s in range(2):
                        group(l * (N // 4) + m * 2 + s, s, True)

            def stream(l):
                for b in range(5):
                    last = mm(psum[:, b, :], zero[0:32, 0:P], zero[0:32, :], True, False)
                first = l * NCH
                pe.wait_ge(gate_out, l * (N // 4) + N // 4)

                def turn(j, s):
                    pe.wait_ge(u_loaded[s], j[1])
                    for k in range(2):
                        if j[2]:
                            pe.wait_ge(ut_ready[k], j[0])
                        for c in range(4):
                            last = pe.transpose(psum[:, 5 + k, c * P:(c + 1) * P],
                                                ubuf[s][:, (4 * k + c) * P:(4 * k + c + 1) * P], ident)
                        last.then_inc(ut_filled[k], 1)

                def hidden(j, s):
                    for k in range(2):
                        pe.wait_ge(ut_ready[k], j[0] + 1)
                    if j[2]:
                        pe.wait_ge(gelu_done, j[0])
                    for c in range(DC):
                        last = mm(psum[:, 7, 0:N], UT[s][:, c, :], hT[:, c, :], c == 0, c == DC - 1)
                    last.then_inc(h_filled, 1)

                def down(j, s, last_chunk=False):
                    pe.wait_ge(v_loaded[s], j[1])
                    pe.wait_ge(at_ready, j[0] + 1)
                    for c in range(DC):
                        v = vbuf[s][:, c * P:(c + 1) * P]
                        pe.matmul(psum[:, c // 2, (c % 2) * 256:(c % 2) * 256 + 256], v, aT[s][:, 0:SEQ],
                                  start=False, stop=False, skip_group_check=True)
                        last = pe.matmul(psum[:, 4, c * NS:(c + 1) * NS], v, aT[s][:, SEQ:N],
                                         start=False, stop=False, skip_group_check=True)
                    if last_chunk:
                        for b in range(5):
                            last = mm(psum[:, b, :], zero[0:32, 0:P], zero[0:32, :], False, True)
                    last.then_inc(y_done, 1)

                def chunk(j):
                    return (first + j, l * (16 * NCH // 2) + 16 * (j // 2 + 1), j > 0)

                turn(chunk(0), 0)
                turn(chunk(1), 1)
                hidden(chunk(0), 0)
                with pe.Fori(0, NCH // 2 - 1) as m:
                    turn((first + m * 2 + 2, l * (16 * NCH // 2) + m * 16 + 32, True), 0)
                    hidden((first + m * 2 + 1, 0, True), 1)
                    down((first + m * 2, l * (16 * NCH // 2) + m * 16 + 16), 0)
                    turn((first + m * 2 + 3, l * (16 * NCH // 2) + m * 16 + 32, True), 1)
                    hidden((first + m * 2 + 2, 0, True), 0)
                    down((first + m * 2 + 1, l * (16 * NCH // 2) + m * 16 + 16), 1)
                hidden(chunk(NCH - 1), 1)
                down(chunk(NCH - 2), 0)
                down(chunk(NCH - 1), 1, True)
                yt_ready.wait(pe, l, 1)
                for t, (n0, r) in enumerate(TILES):
                    for hf in range(2):
                        bk.wait_free(pe, l, "yb", 2 * t + hf)
                        for k in range(4):
                            last = pe.transpose(bk.ap("yb", 2 * t + hf)[0:r, k * P:(k + 1) * P],
                                                YT[:, 4 * hf + k, n0:n0 + r], ident)
                        last.then_inc(bk.full_sem("yb", 2 * t + hf), 1)

            for l in range(DEPTH):
                mixc_loaded.wait(pe, l, 1)
                project(l)
                phase(pe, l, 0)
                delta(l)
                phase(pe, l, 1)
                attention(l)
                phase(pe, l, 2)
                out_projection(l)
                retrieval(l)
                phase(pe, l, 3)
                gates(l)
                stream(l)
                phase(pe, l, 4)

        @block.scalar
        def _(act):
            def out_of(l, name, i, k, dst, src, func=ACT.Copy, scale=1.0):
                bk.wait_full(act, l, name, i, k)
                act.activation(dst, src, func, scale=scale).then_inc(bk.out_sem(name, i, k), 1)

            def roots(l, i, t, r, w=1):
                ms_ready.wait(act, l, i + 1)
                root_ready.by(act.activation(ms[0:r, t:t + w], ms[0:r, t:t + w], ACT.Sqrt))

            def project(l):
                for t, (n0, r) in enumerate(TILES):
                    roots(l, t, t, r)
                bk.wait_full(act, l, "csT")
                seq = cT[:, :, 3 + SEQ:LPAD].rearrange("p c (b s) -> p c b s", b=B)
                for c in range(12):
                    last = act.activation(seq[:, c, :, 0:3], bk.ap("csT")[:, 24 * c:24 * c + 24].rearrange(
                        "p (b s) -> p b s", b=B), ACT.Copy)
                last.then_inc(bk.out_sem("csT"), 1)
                for t, (n0, r) in enumerate(TILES):
                    bk.wait_full(act, l, "fv", t)
                    act.activation(kvrow[0:r, t, 0, 256:512], bk.ap("fv", t)[0:r, 0:256], ACT.Copy)
                    act.activation(fraw[0:r, 4 * t:4 * t + 4], bk.ap("fv", t)[0:r, 256:260], ACT.Copy)\
                        .then_inc(bk.out_sem("fv", t), 1)
                for t, (n0, r) in enumerate(TILES):
                    out_of(l, "ba", t, 0, baraw[0:r, 16 * t:16 * t + 16], bk.ap("ba", t)[0:r, 0:16])
                    out_of(l, "z", t, 0, zrow[0:r, t, :], bk.ap("z", t)[0:r, :], ACT.Silu)
                gate_arg.wait(act, l, 1)
                act.activation(e12, e12, ACT.Exp)
                act.activation(beta.rearrange("p (t c) -> p t c", t=3),
                               baraw.rearrange("p (t c) -> p t c", t=3)[:, :, 0:8], ACT.Exp, scale=-1.0)
                params_loaded.wait(act, l, 4)
                gate_exp.by(act.activation(naexp, alog, ACT.Exp))
                for i in range(8):
                    out_of(l, "pT", i, 0, qkT[:, i, :], bk.ap("pT", i)[:, 0:N], scale=0.125 if i % 4 < 2 else 1.0)
                for t, (n0, r) in enumerate(TILES):
                    out_of(l, "ktok", t, 0, kvrow[0:r, t, :, 0:256],
                           bk.ap("ktok", t)[0:r, :].rearrange("p (g c) -> p g c", g=2))
                for t, (n0, r) in enumerate(TILES):
                    out_of(l, "dv", t, 0, kvrow[0:r, t, 1, 256:512], bk.ap("dv", t)[0:r, 0:256])

                def conv_in(i0):
                    for i in range(i0, i0 + 4):
                        bk.wait_full(act, l, "pT", i)
                        act.activation(cT[:, i - 8, 3:3 + SEQ], bk.ap("pT", i)[:, 0:SEQ], ACT.Copy)
                        act.activation(seq[:, i - 8, :, 3:7], bk.ap("pT", i)[:, SEQ:N].rearrange(
                            "p (b s) -> p b s", b=B), ACT.Copy).then_inc(bk.out_sem("pT", i), 1)

                def conv_silu(s):
                    conv_done.wait(act, l, s + 1)
                    act.activation(cS[:, 4 * s:4 * s + 4, 0:SEQ], cO[:, 4 * s:4 * s + 4, 0:SEQ], ACT.Silu)
                    for c in range(4 * s, 4 * s + 4):
                        last = act.activation(cS[:, c, SEQ:N].rearrange("p (b s) -> p b s", b=B),
                                              cOseq[:, c, :, 0:4], ACT.Silu)
                    silu_done.by(last)

                conv_in(8)
                conv_in(12)
                conv_silu(0)
                for t, (n0, r) in enumerate(TILES):
                    out_of(l, "tk", (0, t), 0, tok[0:r, t, 0, :], bk.ap("tk", (0, t))[0:r, :])
                conv_in(16)
                conv_silu(1)
                for t, (n0, r) in enumerate(TILES):
                    out_of(l, "tk", (1, t), 0, tok[0:r, t, 1, :], bk.ap("tk", (1, t))[0:r, :])
                for i in range(3):
                    out_of(l, "craw", i, 0, crow[0:59, 512 * i:512 * i + 512], bk.ap("craw", i)[0:59, :])
                conv_silu(2)
                for t, (n0, r) in enumerate(TILES):
                    out_of(l, "tk", (2, t), 0, tok[0:r, t, 2, :], bk.ap("tk", (2, t))[0:r, :])

            def delta_tile(l, t):
                r = W = TILES[t][1]
                q = per[t]
                nb = 2 if t < 2 else 1
                bw = 512 if t < 2 else 256
                out_of(l, "gcs", t, 0, egv[0:r, t, :], bk.ap("gcs", t)[0:r, 0:16], ACT.Exp)
                ms_ready.wait(act, l, 3 + t + 1)
                root_ready.by(act.activation(qkss[0:r, :], qkss[0:r, :], ACT.Sqrt))
                for k in range(nb):
                    out_of(l, "dec", t, k, EX[0:r, 512 * k:512 * k + bw], bk.ap("dec", t, k)[0:r, 0:bw], ACT.Exp)
                dsts = (kT, kq, kq[:, NH * W:], q["qeT"])
                for kind in range(4):
                    for k in range(nb):
                        out_of(l, "tr", (t, kind), k, dsts[kind][0:HD, 512 * k:512 * k + bw],
                               bk.ap("tr", (t, kind), k)[0:HD, 0:bw])
                for s in LEV[t][1:]:
                    for k in range(nb):
                        out_of(l, "p1", (t, s), k, P1[0:r, 512 * k:512 * k + bw], bk.ap("p1", (t, s), k)[0:r, 0:bw])
                for k in range(nb):
                    out_of(l, "wT", t, k, q["nwT"][0:HD, 512 * k:512 * k + bw], bk.ap("wT", t, k)[0:HD, 0:bw],
                           scale=-1.0)

            def delta(l):
                out_of(l, "gl", 0, 0, eglT[0:HD, 0:32], bk.ap("gl")[0:HD, 0:32], ACT.Exp)
                out_of(l, "gls", 0, 0, eglT[0:HD, 32:96], bk.ap("gls")[0:HD, 0:64], ACT.Exp)
                delta_tile(l, 0)
                delta_tile(l, 1)
                state_zeroed.wait(act, l, 1)
                for c in range(4):
                    t, rows = c // 2, slice(64 * (c % 2), 64 * (c % 2) + 64)
                    out_of(l, "vn", c, 0, vnw[t][rows, :], bk.ap("vn", c)[rows, :])
                    out_of(l, "oo", c, 0, otok[t][rows, :], bk.ap("oo", c)[rows, :])
                delta_tile(l, 2)
                out_of(l, "vn", 4, 0, vnw[2][0:NS, :], bk.ap("vn", 4)[0:NS, :])
                out_of(l, "oo", 4, 0, otok[2][0:NS, :], bk.ap("oo", 4)[0:NS, :])
                for t, (n0, r) in enumerate(TILES):
                    ms_ready.wait(act, l, 6 + t + 1)
                    root_ready.by(act.activation(ms[0:r, 0:8], ms[0:r, 0:8], ACT.Sqrt))
                for t, (n0, r) in enumerate(TILES):
                    out_of(l, "oT", t, 0, mixT[:, 4:8, n0:n0 + r],
                           bk.ap("oT", t)[:, 0:4 * r].rearrange("p (c n) -> p c n", c=4))

            def attention(l):
                for u in range(8):
                    g, hp, qt = u // 4, (u // 2) % 2, u % 2
                    KW = P * (qt + 1)
                    negmax_ready.wait(act, l, u + 1)
                    for ah in range(2):
                        m = 2 * (u % 2) + ah
                        last = act.activation(PRp[u % 2][:, ah, 0:KW], SMp[u % 2][:, ah, 0:KW], ACT.Exp,
                                              bias=mneg[:, m:m + 1], accum_out=den[:, m:m + 1])
                    exp_ready.by(last)
                    nt = 2 * (qt + 1)
                    out_of(l, "PT", u, 0, PTp[u % 2][:, 0:qt + 1, :, :], bk.ap("PT", u)[:, 0:nt * P].rearrange(
                        "p (g a q) -> p g a q", a=2, q=P))
                    bk.wait_full(act, l, "O", u)
                    for ah in range(2):
                        last = act.activation(mixT[64 * ah:64 * ah + 64, 2 * g + hp, qt * P:(qt + 1) * P],
                                              bk.ap("O", u)[64 * ah:64 * ah + 64, ah * P:(ah + 1) * P], ACT.Copy)
                    last.then_inc(bk.out_sem("O", u), 1)
                bk.wait_full(act, l, "lfT")
                rep = lfr.rearrange("p g (b h q) -> p g b h q", b=B, h=4)
                lf = bk.ap("lfT")[:, 0:256].rearrange("p (h b g) -> p g b h", h=4, b=B)
                for pg in range(PAGES):
                    last = act.activation(rep[:, pg], lf[:, pg][:, :, :, None].to_broadcast([P, B, 4, 4]), ACT.Copy)
                last.then_inc(bk.out_sem("lfT"), 1)
                for g in range(2):
                    w4 = (512, 512) if g == 0 else (512, 128)
                    for b in range(B):
                        for hp in range(2):
                            out_of(l, "kTs", (g, b), 2 * hp, KT[b % 2][:, hp, 0:512], bk.ap("kTs", (g, b), 2 * hp)[:, :])
                    s_negmax.wait(act, l, g + 1)
                    if g == 0:
                        for k in range(2):
                            bk.wait_full(act, l, "SS", 0, k)
                            act.activation(PRs[:, 512 * k:512 * k + 512], psum[:, k, :], ACT.Exp, bias=mneg[:, 0:1],
                                           accum_out=den[:, k:k + 1]).then_inc(bk.out_sem("SS", 0, k), 1)
                        s_exp.by(act.activation(PRs[:, 1024:1056], SNs, ACT.Exp, bias=mneg[:, 0:1],
                                                accum_out=den[:, 2:3]))
                    else:
                        s_exp.by(act.activation(PRs[:, 0:DILK * P + NS], PRs[:, 0:DILK * P + NS], ACT.Exp,
                                                bias=mneg[:, 0:1]))
                    for k in range(2):
                        w = w4[k]
                        out_of(l, "PTs", g, k, PTs[:, 4 * k:4 * k + w // P, :],
                               bk.ap("PTs", g, k)[:, 0:w].rearrange("p (g r) -> p g r", r=P))
                    out_of(l, "PTs", g, 2, PTn[0:NS, :], bk.ap("PTs", g, 2)[0:NS, 0:P])

            def retrieval(l):
                for t, (n0, r) in enumerate(TILES):
                    roots(l, 9 + t, t, r)
                for i in range(4):
                    out_of(l, "kyT", i, 0, keysT[:, 4 * i:4 * i + 4, :],
                           bk.ap("kyT", i)[:, :].rearrange("p (g k) -> p g k", g=4))
                for i in range(16):
                    out_of(l, "qf", i, 0, qTf[:, i, :], bk.ap("qf", i)[:, 0:N])
                for t, (n0, r) in enumerate(TILES):
                    if t == 2:
                        top_done.wait(act, l, 1)
                    for g in range(4):
                        out_of(l, "sc", (t, g), 0, scb[t % 2][0:r, 4 * g:4 * g + 4, :],
                               bk.ap("sc", (t, g))[0:r, :].rearrange("p (g k) -> p g k", g=4))
                for t, (n0, r) in enumerate(TILES):
                    fv_ready.wait(act, l, t + 1)
                    fv_exp.by(act.activation(ijw[0:r, 2, :], ijw[0:r, 2, :], ACT.Exp))
                    out_of(l, "ijwT", t, 0, ijwT[:, :, n0:n0 + r],
                           bk.ap("ijwT", t)[:, 0:3 * r].rearrange("p (s n) -> p s n", s=3))

            def gates(l):
                def group(i, s, n0):
                    act.wait_ge(gate_filled, i + 1)
                    act.activation(G[:, :, n0], psum[:, 5 + s, :].rearrange("p (m j) -> p j m", m=4),
                                   ACT.Copy).then_inc(gate_out, 1)

                with act.Fori(0, N // 8) as m:
                    for s in range(2):
                        group(l * (N // 4) + m * 2 + s, s, bass.ds(m * 8 + 4 * s, 4))

            def stream(l):
                first = l * NCH

                def turned(j, s, again):
                    act.wait_ge(ut_filled[0], j + 1)
                    if again:
                        act.wait_ge(h_filled, j + -1)
                    act.activation(UT[s][:, 0:4, :], psum[:, 5, :].rearrange("p (c e) -> p c e", c=4), ACT.Copy)\
                        .then_inc(ut_ready[0], 1)

                def gelu(j, s, again):
                    act.wait_ge(h_filled, j + 1)
                    if again:
                        act.wait_ge(at_ready, j + -1)
                    act.activation(ge[s], psum[:, 7, 0:N], ACT.Gelu).then_inc(gelu_done, 1)

                turned(first, 0, False)
                turned(first + 1, 1, False)
                gelu(first, 0, False)
                turned(first + 2, 0, True)
                gelu(first + 1, 1, False)
                with act.Fori(1, NCH // 2 - 1) as m:
                    for s in range(2):
                        turned(first + m * 2 + (s + 1), (s + 1) % 2, True)
                        gelu(first + m * 2 + s, s, True)
                turned(first + NCH - 1, 1, True)
                gelu(first + NCH - 2, 0, True)
                gelu(first + NCH - 1, 1, True)
                act.wait_ge(y_done, first + NCH)
                for b in range(4):
                    act.activation(YT[:, 2 * b:2 * b + 2, 0:SEQ], psum[:, b, :].rearrange("p (c n) -> p c n", c=2),
                                   ACT.Copy)
                yt_ready.by(act.activation(YT[:, :, SEQ:N], psum[:, 4, 0:DC * NS].rearrange("p (c n) -> p c n", c=DC),
                                           ACT.Copy))

            for l in range(DEPTH):
                project(l)
                phase(act, l, 0)
                delta(l)
                phase(act, l, 1)
                attention(l)
                phase(act, l, 2)
                retrieval(l)
                phase(act, l, 3)
                gates(l)
                stream(l)
                phase(act, l, 4)
            for t, (n0, r) in enumerate(TILES):
                act.wait_ge(final_ms, t + 1)
                act.activation(ms[0:r, t:t + 1], ms[0:r, t:t + 1], ACT.Sqrt).then_inc(final_root, 1)

        @block.vector
        def _(dve):
            v = nc.vector

            def settle():
                dve_step.settle(dve)

            def step(ins):
                dve_step.by(ins)
                settle()

            def tt(out, in0, in1, op):
                return v.tensor_tensor(out, in0, in1, op)

            def ts(out, in0, s1, op0, s2=None, op1=None):
                if op1 is None:
                    return v.tensor_scalar(out, in0, s1, None, op0)
                return v.tensor_scalar(out, in0, s1, s2, op0, op1)

            def stt(out, in0, scalar, in1, op0, op1):
                return v.scalar_tensor_tensor(out=out, in0=in0, scalar=scalar, in1=in1, op0=op0, op1=op1)

            def norm_rows(l, base, name, g0):
                for t, (n0, r) in enumerate(TILES):
                    if t == 2:
                        bk.wait_full(dve, l, name, 1)
                    junk = xn[0:r, t % 2, :]
                    step(v.tensor_tensor_reduce(junk, x[0:r, t, :], x[0:r, t, :], 1.0, 0.0, ALU.mult, ALU.add,
                                                   ms[0:r, t:t + 1]))
                    ms_ready.by(ts(ms[0:r, t:t + 1], ms[0:r, t:t + 1], 1.0 / D, ALU.mult, EPS, ALU.add))
                    root_ready.wait(dve, l, (0 if base == 0 else 9) + t + 1)
                    step(v.reciprocal(ms[0:r, t:t + 1], ms[0:r, t:t + 1]))
                    xn_ready.by(ts(junk, x[0:r, t, :], ms[0:r, t:t + 1], ALU.mult))
                for t, (n0, r) in enumerate(TILES):
                    for hf in range(2):
                        bk.wait_full(dve, l, name, 2 * t + hf)
                        tt(hT[:, 4 * hf:4 * hf + 4, n0:n0 + r],
                           bk.ap(name, 2 * t + hf)[:, 0:4 * r].rearrange("p (c n) -> p c n", c=4),
                           gain[:, g0 + 4 * hf:g0 + 4 * hf + 4][:, :, None].to_broadcast([P, 4, r]), ALU.mult)\
                            .then_inc(bk.out_sem(name, 2 * t + hf), 1)

            def log1p_exp(l, y, out):
                step(stt(e12, y, -1.0, y, ALU.mult, ALU.min))
                gate_arg.by(ts(q12, y, 1.0, ALU.mult))
                gate_exp.wait(dve, l, 1)
                step(ts(s12, e12, 2.0, ALU.add))
                step(v.reciprocal(s12, s12))
                step(tt(s12, e12, s12, ALU.mult))
                step(tt(q12, s12, s12, ALU.mult))
                step(ts(p12, q12, 1.0 / 17, ALU.mult))
                for n in (15, 13, 11, 9, 7, 5, 3):
                    step(stt(p12, p12, 1.0 / n, q12, ALU.add, ALU.mult))
                step(stt(p12, p12, 1.0, s12, ALU.add, ALU.mult))
                step(ts(p12, p12, 2.0, ALU.mult))
                step(stt(out, y, 0.0, p12, ALU.max, ALU.add))

            def project(l):
                pad_zeroed.by(v.memset(cT[:, :, 0:3], 0.0))
                bk.wait_full(dve, l, "vecT")
                v.tensor_copy(gain, bk.ap("vecT")[:, 0:64]).then_inc(bk.out_sem("vecT"), 1)
                bk.wait_out(dve, l, "vecT")
                norm_rows(l, 0, "xT_mix", 48)
                params_loaded.wait(dve, l, 4)
                for t in range(3):
                    bk.wait_out(dve, l, "fv", t)
                    bk.wait_out(dve, l, "ba", t)
                yv = y12.rearrange("p (t c) -> p t c", t=3)
                fb3 = fbias[:, None, :].to_broadcast([P, 3, 12])
                stt(yv[:, :, 0:4], fraw.rearrange("p (t c) -> p t c", t=3), -1.0, fb3[:, :, 0:4], ALU.mult,
                    ALU.subtract)
                step(tt(yv[:, :, 4:12], baraw.rearrange("p (t c) -> p t c", t=3)[:, :, 8:16], fb3[:, :, 4:12],
                           ALU.add))
                log1p_exp(l, y12, lg)
                step(ts(beta, beta, 1.0, ALU.add))
                step(v.reciprocal(beta, beta))
                step(ts(lgv[:, :, 0:4], lgv[:, :, 0:4], -1.0, ALU.mult))
                gates_ready.by(stt(lgv[:, :, 4:12], lgv[:, :, 4:12], -1.0,
                                   naexp[:, None, :].to_broadcast([P, 3, 8]), ALU.mult, ALU.mult))

                def conv(s):
                    for c in range(4 * s, 4 * s + 4):
                        bk.wait_out(dve, l, "pT", 8 + c)
                    for c in range(4 * s, 4 * s + 4):
                        dve_step.by(ts(cO[:, c, 0:LOUT], cT[:, c, 0:LOUT], gain[:, c:c + 1], ALU.mult))
                    for i in range(1, 4):
                        settle()
                        for c in range(4 * s, 4 * s + 4):
                            last = stt(cO[:, c, 0:LOUT], cT[:, c, i:i + LOUT], gain[:, 12 * i + c:12 * i + c + 1],
                                       cO[:, c, 0:LOUT], ALU.mult, ALU.add)
                            (conv_done if (i, c) == (3, 4 * s + 3) else dve_step).by(last)

                bk.wait_out(dve, l, "csT")
                pad_zeroed.wait(dve, l, 1)
                for s in range(3):
                    conv(s)

            def heads(ap, w=HD):
                return ap.rearrange("p (h d) -> p h d", d=w)

            def delta_tile(l, t):
                r = W = TILES[t][1]
                q = per[t]
                nb = 2 if t < 2 else 1
                hpb = NH // nb
                le, gt = (C("le64"), C("gt64")) if t < 2 else (C("le4"), C("gt4"))
                qk = tok[0:r, t, 0:2, :].rearrange("p s (h d) -> p (s h) d", d=HD)
                if t:
                    for k in range(2):
                        bk.wait_full(dve, l, "wT", t - 1, k)
                gg_ready.by(tt(heads(GG[0:r, 0:NH * W], W), gt[0:r, None, :].to_broadcast([r, NH, W]),
                               lgv[0:r, t, 4:12][:, :, None].to_broadcast([r, NH, W]), ALU.mult))
                sq = LT[0:r, :]
                step(tt(heads(sq), qk, qk, ALU.mult))
                step(v.tensor_reduce(qkss[0:r, :], heads(sq), AX.X, ALU.add))
                ms_ready.by(ts(qkss[0:r, :], qkss[0:r, :], EPS, ALU.add))
                root_ready.wait(dve, l, 3 + t + 1)
                step(v.reciprocal(qkss[0:r, :], qkss[0:r, :]))
                step(ts(qkss[0:r, 0:8], qkss[0:r, 0:8], 0.125, ALU.mult))
                step(tt(qk, qk, qkss[0:r, :][:, :, None].to_broadcast([r, 16, HD]), ALU.mult))
                bk.wait_out(dve, l, "gcs", t)

                def scaled(out, rows, by):
                    return tt(heads(out[0:r, :]), heads(rows), by[:, :, None].to_broadcast([r, NH, HD]), ALU.mult)

                step(scaled(kb, tok[0:r, t, 1, :], betav[0:r, t, :]))
                scaled(q["vb"], tok[0:r, t, 2, :], betav[0:r, t, :])
                scaled(kbe, kb[0:r, :], egv[0:r, t, 0:8])
                scaled(qe, tok[0:r, t, 0, :], egv[0:r, t, 0:8])
                tile_rows.by(scaled(q["kd"], tok[0:r, t, 1, :], egv[0:r, t, 8:16]))
                for k in range(nb):
                    bk.wait_out(dve, l, "dec", t, k)
                step(tt(heads(EXI[0:r, 0:NH * W], W), heads(EX[0:r, 0:NH * W], W),
                           le[0:r, None, :].to_broadcast([r, NH, W]), ALU.mult))
                nk, hk = (4, 2) if t < 2 else (1, 8)
                for k in range(nk):
                    bk.wait_full(dve, l, "kk", t, k)
                    pair = bk.ap("kk", t, k)[0:r, 0:2 * hk * W].rearrange("p (h s w) -> p s h w", h=hk, s=2)
                    cols = slice(k * hk * W, (k + 1) * hk * W)
                    tt(heads(LT[0:r, cols], W), pair[:, 0], heads(EX[0:r, cols], W), ALU.mult)
                    tt(heads(q["attnT"][0:r, cols], W), pair[:, 1], heads(EXI[0:r, cols], W), ALU.mult)\
                        .then_inc(bk.out_sem("kk", t, k), 1)
                for k in range(nk):
                    bk.wait_out(dve, l, "kk", t, k)
                T, TT = T0[0:r, 0:NH * W], q["TT"][0:r, 0:NH * W]
                idb = ident[0:r, None, 0:W].to_broadcast([r, hpb, W])
                for n, s in enumerate(LEV[t]):
                    if n:
                        for k in range(nb):
                            bk.wait_full(dve, l, "p1", (t, LEV[t][n - 1]), k)
                            if n == 1:
                                bk.wait_out(dve, l, "p1", (t, 1), k)
                    lm_ready.by(tt(heads(LM[0:r, 0:NH * W], W), heads(LT[0:r, 0:NH * W], W),
                                   C(f"lev{s}")[0:r, None, 0:W].to_broadcast([r, NH, W]), ALU.mult))
                    for k in range(nb):
                        cols = slice(k * hpb * W, (k + 1) * hpb * W)
                        if n == 0:
                            if k == 0:
                                lm_ready.wait(dve, l, 6 * t + 1)
                            tt(heads(TT[:, cols], W), idb, heads(LM[0:r, cols], W), ALU.subtract)
                            bk.wait_full(dve, l, "p1", (t, s), k)
                            tt(heads(T[:, cols], W), idb, heads(bk.ap("p1", (t, s), k)[0:r, 0:hpb * W], W),
                               ALU.subtract).then_inc(bk.out_sem("p1", (t, s), k), 1)
                        elif s != LEV[t][-1]:
                            bk.wait_out(dve, l, *(("dd", (t, LEV[t][n - 1]), k) if n > 1 else ("p1", (t, 1), k)))
                            bk.wait_full(dve, l, "dd", (t, s), k)
                            tt(T[:, cols], T[:, cols], bk.ap("dd", (t, s), k)[0:r, 0:hpb * W], ALU.subtract)\
                                .then_inc(bk.out_sem("dd", (t, s), k), 1)
                    if n:
                        for k in range(nb):
                            cols = slice(k * hpb * W, (k + 1) * hpb * W)
                            bk.wait_out(dve, l, *(("dt", (t, LEV[t][n - 1]), k) if n > 1 else ("p1", (t, 1), k)))
                            bk.wait_full(dve, l, "dt", (t, s), k)
                            tt(TT[:, cols], TT[:, cols], bk.ap("dt", (t, s), k)[0:r, 0:hpb * W], ALU.subtract)\
                                .then_inc(bk.out_sem("dt", (t, s), k), 1)

            def delta(l):
                v.memset(st[0:HD, :], 0.0)
                v.memset(vnw[0], 0.0)
                state_zeroed.by(v.memset(vnw[1], 0.0))
                gates_ready.wait(dve, l, 1)
                gm_ready.by(tt(gm[0:NS, :].rearrange("p (b h) -> p b h", b=B),
                               C("rowb")[0:NS, :][:, :, None].to_broadcast([NS, B, NH]),
                               lgv[0:NS, 2, 4:12][:, None, :].to_broadcast([NS, B, NH]), ALU.mult))
                delta_tile(l, 0)
                delta_tile(l, 1)
                bk.wait_out(dve, l, "gl")
                state_zeroed.wait(dve, l, 1)
                for c in range(4):
                    bk.wait_full(dve, l, "oo", c)
                    if c:
                        bk.wait_out(dve, l, "st", c - 1)
                    step(tt(heads(st[0:HD, :]), heads(st[0:HD, :]),
                               eglT[0:HD, 8 * c:8 * c + 8][:, :, None].to_broadcast([HD, NH, HD]), ALU.mult))
                    bk.wait_full(dve, l, "st", c)
                    tt(st[0:HD, :], st[0:HD, :], bk.ap("st", c)[0:HD, :], ALU.add).then_inc(bk.out_sem("st", c), 1)
                bk.wait_out(dve, l, "st", 3)
                states_ready.by(v.memset(vnm[0:NS, 0:8], 0.0))
                delta_tile(l, 2)
                bk.wait_out(dve, l, "wT", 2)
                bk.wait_out(dve, l, "tr", (2, 3))
                colb = C("colb").rearrange("p (b n) -> p b n", b=B)

                def per_sequence(out, src):
                    for h in range(NH):
                        last = tt(out[0:HD, h * B * NS:(h + 1) * B * NS].rearrange("p (b n) -> p b n", b=B),
                                  src[0:HD, h * NS:(h + 1) * NS][:, None, :].to_broadcast([HD, B, NS]),
                                  colb[0:HD], ALU.mult)
                    return last

                per_sequence(nwm, per[2]["nwT"])
                spread_ready.by(per_sequence(qem, per[2]["qeT"]))
                bk.wait_full(dve, l, "oo", 4)
                bk.wait_out(dve, l, "gls")
                bk.wait_out(dve, l, "vn", 4)
                s0_loaded.wait(dve, l, 8)
                step(tt(s0[0:HD, :].rearrange("p (g v) -> p g v", v=HD), s0[0:HD, :].rearrange(
                    "p (g v) -> p g v", v=HD), eglT[0:HD, 32:96][:, :, None].to_broadcast([HD, B * NH, HD]), ALU.mult))
                for hf in range(2):
                    if hf:
                        bk.wait_full(dve, l, "st", 7)
                    for h in range(4):
                        last = tt(vnm[0:NS, 512 * h:512 * h + 512].rearrange("p (b v) -> p b v", b=B),
                                  vnw[2][0:NS, (4 * hf + h) * HD:(4 * hf + h + 1) * HD][:, None, :]
                                  .to_broadcast([NS, B, HD]),
                                  C("rowb")[0:NS, :][:, :, None].to_broadcast([NS, B, HD]), ALU.mult)
                    vnm_ready.by(last)
                    for h in range(4 * hf, 4 * hf + 4):
                        bk.wait_full(dve, l, "st", 4 + h)
                        own = s0[0:HD, :].rearrange("p (b h v) -> p b h v", b=B, h=NH)[:, :, h, :]
                        tt(own, own, bk.ap("st", 4 + h)[0:HD, :].rearrange("p (b v) -> p b v", b=B), ALU.add)\
                            .then_inc(bk.out_sem("st", 4 + h), 1)
                bk.wait_out(dve, l, "st", 11)
                states_ready.by(v.memset(ms[:, 0:8], 1.0))
                states_ready.wait(dve, l, 2)
                for t, (n0, r) in enumerate(TILES):
                    for c in ((2 * t, 2 * t + 1) if t < 2 else (4,)):
                        bk.wait_out(dve, l, "oo", c)
                    sq = LT[0:r, 0:512]
                    o = otok[t][0:r, :]
                    step(tt(sq, o, o, ALU.mult))
                    step(v.tensor_reduce(ms[0:r, 0:8], heads(sq), AX.X, ALU.add))
                    ms_ready.by(ts(ms[0:r, 0:8], ms[0:r, 0:8], 1.0 / HD, ALU.mult, EPS, ALU.add))
                    root_ready.wait(dve, l, 6 + t + 1)
                    step(v.reciprocal(ms[0:r, 0:8], ms[0:r, 0:8]))
                    step(tt(heads(o), heads(o), ms[0:r, 0:8][:, :, None].to_broadcast([r, NH, HD]), ALU.mult))
                    step(tt(heads(o), heads(o), dnorm[0:r, None, :].to_broadcast([r, NH, HD]), ALU.mult))
                    onorm_ready.by(tt(o, o, zrow[0:r, t, :], ALU.mult))

            def prompt_unit(l, u):
                g, hp, qt = u // 4, (u // 2) % 2, u % 2
                KW = P * (qt + 1)
                s = u % 2
                for ah in range(2):
                    S = bk.ap("S", (u, ah))
                    bk.wait_full(dve, l, "S", (u, ah))
                    if g == 0:
                        if qt:
                            v.tensor_copy(SMp[s][:, ah, 0:P], S[:, 0:P])
                        last = tt(SMp[s][:, ah, KW - P:KW], S[:, KW - P:KW], C("causal"), ALU.add)
                    else:
                        last = stt(SMp[s][:, ah, 0:KW], C("pdist")[:, qt * SEQ:qt * SEQ + KW], -SLOPES[2 * hp + ah],
                                   S[:, 0:KW], ALU.mult, ALU.add)
                    last.then_inc(bk.out_sem("S", (u, ah)), 1)
                for ah in range(2):
                    bk.wait_out(dve, l, "S", (u, ah))
                negmax_ready.by(v.tensor_reduce(mneg[:, 2 * s:2 * s + 2], SMp[s][:, :, 0:KW], AX.X, ALU.max,
                                                negate=True))

            def prompt_probs(l, u):
                g, hp, qt = u // 4, (u // 2) % 2, u % 2
                KW = P * (qt + 1)
                s = u % 2
                exp_ready.wait(dve, l, u + 1)
                pr, dn = PRp[s][:, :, 0:KW], den[:, 2 * s:2 * s + 2]
                if g:
                    step(tt(pr, pr, C("pcnt")[:, None, qt * SEQ:qt * SEQ + KW].to_broadcast([P, 2, KW]), ALU.mult))
                    step(v.tensor_reduce(dn, pr, AX.X, ALU.add))
                step(v.reciprocal(dn, dn))
                probs_ready.by(tt(pr, pr, dn[:, :, None].to_broadcast([P, 2, KW]), ALU.mult))

            def attention(l):
                lfb_ready.by(v.tensor_copy(lfb, lgv[:, 0:2, 0:4][:, :, :, None].to_broadcast([P, 2, 4, P])))
                prompt_unit(l, 0)
                for u in range(8):
                    if u < 7:
                        prompt_unit(l, u + 1)
                    prompt_probs(l, u)
                for g in range(2):
                    if g == 0:
                        q_zeroed.wait(dve, l, 1)
                        v.tensor_copy(lfrn[0:NS, :].rearrange("p (b h q) -> p b h q", b=B, h=4),
                                      lgv[0:NS, 2, 0:4][:, None, :, None].to_broadcast([NS, B, 4, 4]))
                    else:
                        bk.wait_full(dve, l, "SN", 0)
                    for h in range(4):
                        rows, hp = slice(64 * (h % 2), 64 * (h % 2) + 64), h // 2
                        qs = qkT[rows, 4 * g + hp, SEQ:N].rearrange("p (b q) -> p b q", b=B)
                        v.tensor_copy(QA[rows, hp, :].rearrange("p (b h q) -> p b h q", b=B, h=4)[:, :, h, :], qs)
                        last = v.tensor_copy(diag_of(rows, hp, h), qs)
                    q_spread.by(last)
                    nk = PAGES if g == 0 else DILK
                    w2 = 512 if g == 0 else 128
                    for b in range(B):
                        for hp in range(2):
                            k = 2 * hp + 1
                            bk.wait_full(dve, l, "kTs", (g, b), k)
                            v.tensor_copy(KT[b % 2][:, hp, 512:512 + w2], bk.ap("kTs", (g, b), k)[:, 0:w2])\
                                .then_inc(bk.out_sem("kTs", (g, b), k), 1)
                    for k in range(2):
                        bk.wait_full(dve, l, "SS", g, k)
                    bk.wait_full(dve, l, "SN", g)
                    if g == 0:
                        tt(SNs, bk.ap("SN", 0)[:, 0:NS], C("smask"), ALU.add).then_inc(bk.out_sem("SN", 0), 1)
                        bk.wait_out(dve, l, "SN", 0)
                        v.tensor_reduce(mneg[:, 1:2], psum[:, 0:2, :], AX.XY, ALU.max, negate=True)
                        step(v.tensor_reduce(mneg[:, 2:3], SNs, AX.X, ALU.max, negate=True))
                        s_negmax.by(tt(mneg[:, 0:1], mneg[:, 1:2], mneg[:, 2:3], ALU.min))
                        s_exp.wait(dve, l, 1)
                        step(v.tensor_reduce(den[:, 3:4], den[:, 0:3], AX.X, ALU.add))
                        wd = 1056
                    else:
                        wd = DILK * P + NS
                        tt(PRs[:, 0:512], psum[:, 0, :], C("sbias")[:, 0:512], ALU.add)\
                            .then_inc(bk.out_sem("SS", 1, 0), 1)
                        tt(PRs[:, 512:640], psum[:, 1, 0:128], C("sbias")[:, 512:640], ALU.add)\
                            .then_inc(bk.out_sem("SS", 1, 1), 1)
                        tt(PRs[:, 640:672], bk.ap("SN", 1)[:, 0:NS], C("sbias")[:, 640:672], ALU.add)\
                            .then_inc(bk.out_sem("SN", 1), 1)
                        bk.wait_out(dve, l, "SN", 1)
                        s_negmax.by(v.tensor_reduce(mneg[:, 0:1], PRs[:, 0:wd], AX.X, ALU.max, negate=True))
                        s_exp.wait(dve, l, 2)
                        step(tt(PRs[:, 0:wd], PRs[:, 0:wd], C("scnt"), ALU.mult))
                        step(v.tensor_reduce(den[:, 3:4], PRs[:, 0:wd], AX.X, ALU.add))
                    step(v.reciprocal(den[:, 3:4], den[:, 3:4]))
                    s_probs.by(ts(PRs[:, 0:wd], PRs[:, 0:wd], den[:, 3:4], ALU.mult))
                    bk.wait_full(dve, l, "OS", g)
                    for h in range(4):
                        rows, hp = slice(64 * (h % 2), 64 * (h % 2) + 64), h // 2
                        src = bk.ap("OS", g)[rows, hp * P:(hp + 1) * P].rearrange("p (b h q) -> p b h q", b=B, h=4)
                        last = v.tensor_copy(mixT[rows, 2 * g + hp, SEQ:N].rearrange("p (b q) -> p b q", b=B),
                                             src[:, :, h, :])
                    last.then_inc(bk.out_sem("OS", g), 1)

            def diag_of(rows, hp, h):
                at = QZ[rows, hp, 0, 4 * h:4 * h + 4]
                return bass.AP(tensor=at.tensor, offset=at.offset, ap=[[SIDEW, HD], [P + 16, B], [1, 4]])

            def residual(l, name):
                for t, (n0, r) in enumerate(TILES):
                    for hf in range(2):
                        part = x[0:r, t, 512 * hf:512 * hf + 512]
                        bk.wait_full(dve, l, name, 2 * t + hf)
                        tt(part, part, bk.ap(name, 2 * t + hf)[0:r, :], ALU.add)\
                            .then_inc(bk.out_sem(name, 2 * t + hf), 1)
                for i in range(6):
                    bk.wait_out(dve, l, name, i)

            def top16(l, r, groups, values, spare, out, index):
                for g in range(groups):
                    dve_step.by(v.max(out[0:r, g, 0:8], values[0:r, g, :]))
                settle()
                for g in range(groups):
                    v.max_index(index[0:r, g, 0:8], out[0:r, g, 0:8], values[0:r, g, :])
                    dve_step.by(v.match_replace(spare[0:r, g, :], out[0:r, g, 0:8], values[0:r, g, :], -3.0e38))
                settle()
                for g in range(groups):
                    dve_step.by(v.max(out[0:r, g, 8:16], spare[0:r, g, :]))
                settle()
                for g in range(groups):
                    dve_step.by(v.max_index(index[0:r, g, 8:16], out[0:r, g, 8:16], spare[0:r, g, :]))
                settle()

            def retrieval(l):
                residual(l, "y")
                norm_rows(l, 1, "xT_ffn", 56)
                for t, (n0, r) in enumerate(TILES):
                    for g in range(4):
                        bk.wait_out(dve, l, "sc", (t, g))
                    top16(l, r, 16, scb[t % 2], sc2, topv, topu)
                    top_done.by(v.tensor_copy(topf[0:r], topu[0:r]))
                    top_done.wait(dve, l, t + 1)
                    tv = topv[0:r].rearrange("p (h c) k -> p c h k", c=2)
                    tf = topf[0:r].rearrange("p (h c) k -> p c h k", c=2)
                    cv = cand[0:r, :].rearrange("p (h a b) -> p h a b", h=NH, a=16)
                    step(tt(cv, tv[:, 0][:, :, :, None].to_broadcast([r, NH, 16, 16]),
                               tv[:, 1][:, :, None, :].to_broadcast([r, NH, 16, 16]), ALU.add))
                    top16(l, r, NH, cand.rearrange("p (h k) -> p h k", h=NH),
                          cand2.rearrange("p (h k) -> p h k", h=NH), fv, posu)
                    ts(posw[0:r, 0], posu[0:r], 4, ALU.logical_shift_right)
                    step(ts(posw[0:r, 1], posu[0:r], 15, ALU.bitwise_and))
                    v.tensor_copy(fa[0:r], posw[0:r, 0])
                    step(v.tensor_copy(fb[0:r], posw[0:r, 1]))
                    if t:
                        bk.wait_full(dve, l, "ijwT", t - 1)
                    for c, which in ((0, fa), (1, fb)):
                        oh = oneh[0:r].rearrange("p g k -> p (g k)").rearrange("p (k a) -> p k a", a=16)
                        step(tt(oh, iota16[0:r, None, :].to_broadcast([r, P, 16]),
                                   which[0:r].rearrange("p h k -> p (h k)")[:, :, None].to_broadcast([r, P, 16]),
                                   ALU.is_equal))
                        oh4 = oh.rearrange("p (h k) a -> p h k a", h=NH)
                        step(tt(oh4, oh4, tf[:, c][:, :, None, :].to_broadcast([r, NH, 16, 16]), ALU.mult))
                        step(v.tensor_reduce(ijw[0:r, c, :], oh, AX.X, ALU.add))
                    w = ijw[0:r, 2, :].rearrange("p (h k) -> p h k", h=NH)
                    fv_ready.by(tt(w, fv[0:r], fv[0:r, :, 0:1].to_broadcast([r, NH, 16]), ALU.subtract))
                    fv_exp.wait(dve, l, t + 1)
                    step(v.tensor_reduce(hsum[0:r, 0:8], w, AX.X, ALU.add))
                    step(v.reciprocal(hsum[0:r, 0:8], hsum[0:r, 0:8]))
                    ijw_ready.by(tt(w, w, hsum[0:r, 0:8][:, :, None].to_broadcast([r, NH, 16]), ALU.mult))

            def gates(l):
                def group(i, s, tokens, reuse):
                    if reuse:
                        dve.wait_ge(gate_filled, i + -1)
                    for m, n in enumerate(tokens):
                        v.tensor_scalar(hot[s][:, 0, m, :], iota, ijwT[:, 0, n], None, ALU.is_equal)
                        last = v.tensor_scalar(hot[s][:, 1, m, :], iota, ijwT[:, 1, n], ijwT[:, 2, n],
                                               ALU.is_equal, ALU.mult)
                    last.then_inc(hot_ready, 1)

                for s in range(2):
                    group(l * (N // 4) + s, s, [slice(4 * s + m, 4 * s + m + 1) for m in range(4)], False)
                with dve.Fori(1, N // 8) as g:
                    for s in range(2):
                        group(l * (N // 4) + g * 2 + s, s, [bass.ds(g * 8 + (4 * s + m), 1) for m in range(4)], True)

            def stream(l):
                first = l * NCH
                dve.wait_ge(gate_out, l * (N // 4) + N // 4)

                def turned(j, s, again):
                    dve.wait_ge(ut_filled[1], j + 1)
                    if again:
                        dve.wait_ge(h_filled, j + -1)
                    v.tensor_copy(UT[s][:, 4:8, :], psum[:, 6, :].rearrange("p (c e) -> p c e", c=4))\
                        .then_inc(ut_ready[1], 1)

                def gated(j, s, col, again):
                    dve.wait_ge(gelu_done, j + 1)
                    if again:
                        dve.wait_ge(y_done, j + -1)
                    tt(aT[s][:, :], ge[s][:, :], G[:, col, :], ALU.mult).then_inc(at_ready, 1)

                turned(first, 0, False)
                turned(first + 1, 1, False)
                gated(first, 0, 0, False)
                turned(first + 2, 0, True)
                gated(first + 1, 1, 1, False)
                with dve.Fori(1, NCH // 2 - 1) as m:
                    for s in range(2):
                        turned(first + m * 2 + (s + 1), (s + 1) % 2, True)
                        gated(first + m * 2 + s, s, m * 2 + s, True)
                turned(first + NCH - 1, 1, True)
                gated(first + NCH - 2, 0, NCH - 2, True)
                gated(first + NCH - 1, 1, NCH - 1, True)

            dve_zero = v.memset(small[:, :], 0.0)
            dve_zero.then_inc(init_done, 1)
            dve.wait_ge(init_done, 1)
            dve.wait_ge(x_loaded, 48)
            dve.wait_ge(keep_loaded, 16)
            for l in range(DEPTH):
                mixc_loaded.wait(dve, l, 1)
                project(l)
                phase(dve, l, 0)
                delta(l)
                phase(dve, l, 1)
                attention(l)
                phase(dve, l, 2)
                retrieval(l)
                phase(dve, l, 3)
                gates(l)
                stream(l)
                residual(l, "yb")
                phase(dve, l, 4)
            dve.wait_ge(gfin_loaded, 16)
            for t, (n0, r) in enumerate(TILES):
                row = arena[0:r, D * (t + 1):D * (t + 2)]
                v.tensor_tensor_reduce(row, x[0:r, t, :], x[0:r, t, :], 1.0, 0.0, ALU.mult, ALU.add,
                                       ms[0:r, t:t + 1]).then_inc(final_step, 1)
                dve.wait_ge(final_step, 3 * t + 1)
                ts(ms[0:r, t:t + 1], ms[0:r, t:t + 1], 1.0 / D, ALU.mult, EPS, ALU.add).then_inc(final_ms, 1)
                dve.wait_ge(final_root, t + 1)
                v.reciprocal(ms[0:r, t:t + 1], ms[0:r, t:t + 1]).then_inc(final_step, 1)
                dve.wait_ge(final_step, 3 * t + 2)
                ts(row, x[0:r, t, :], ms[0:r, t:t + 1], ALU.mult).then_inc(final_step, 1)
                dve.wait_ge(final_step, 3 * t + 3)
                tt(row, row, arena[0:r, 0:D], ALU.mult).then_inc(final_ready, 1)

        for name, s in sigs.items():
            assert s.given == s.n * DEPTH, (name, s.given, s.n)


_INS = ["x_prompt", "x_sample", "cache_fox_kv", "cache_fox_logf", "cache_dil_kv", "state_delta", "state_conv",
        "page_table", "norm_mix", "w_in", "b_fox_f", "conv_w", "a_log", "dt_bias", "delta_norm", "w_out", "norm_ffn",
        "peer_wq", "peer_keys", "peer_u", "peer_v", "norm_final"]
_OUTS = [("y_prompt", (1, SEQ, D)), ("y_sample", (B, T, D)),
         ("fox_kv_prompt", (DEPTH, 1, SEQ, 2, 4, HD)), ("fox_logf_prompt", (DEPTH, 1, SEQ, 4)),
         ("dil_kv_prompt", (DEPTH, 1, SEQ, 2, 4, HD)), ("delta_state_prompt", (DEPTH, 1, NH, HD, HD)),
         ("conv_state_prompt", (DEPTH, 1, 3, CONV)),
         ("fox_kv_sample", (DEPTH, B, T, 2, 4, HD)), ("fox_logf_sample", (DEPTH, B, T, 4)),
         ("dil_kv_sample", (DEPTH, B, T, 2, 4, HD)), ("delta_state_sample", (DEPTH, B, NH, HD, HD)),
         ("conv_state_sample", (DEPTH, B, 3, CONV))]


def kernel(**inputs):
    import concourse.bacc as _bacc
    from concourse.bass_utils import run_bass_kernel_spmd as _run

    nc = _bacc.Bacc("TRN2", target_bir_lowering=False, num_devices=1)
    c_keep, c_mix, where = shape_constants()
    arrays, aps = {}, {}
    for name in _INS:
        arrays["in_" + name] = np.ascontiguousarray(inputs[name])
    arrays["in_c_keep"], arrays["in_c_mix"] = c_keep, c_mix
    for name, arr in arrays.items():
        aps[name[3:]] = nc.dram_tensor(name, arr.shape, mybir.dt.from_np(arr.dtype), kind="ExternalInput").ap()
    aps["outs"] = {name: nc.dram_tensor("out_" + name, shape, F32, kind="ExternalOutput").ap() for name, shape in _OUTS}
    build(nc, aps, where)
    r = _run(nc, [arrays], core_ids=[0])
    return tuple(r.results[0]["out_" + name] for name, _ in _OUTS)
```

```python
from contextlib import ExitStack

import numpy as np

import concourse.bass as bass
from concourse import mybir
from concourse.alu_op_type import AluOpType as ALU

F32 = mybir.dt.float32
F32R = mybir.dt.float32r
U32 = mybir.dt.uint32
I32 = mybir.dt.int32
ACT = mybir.ActivationFunctionType
AX = mybir.AxisListType

P = 128
D = 1024
DC = D // P
SEQ = 256
B = 8
T = 4
NS = B * T
N = SEQ + NS
DEPTH = 2
PAST = 1024
PAGES = PAST // P
HD = 64
NPOOL = 80
CONV = 1536
INW = 3604
NH = 8
EPS = 1e-6
NEG = -1e30
TILES = [(0, 128), (128, 128), (256, 32)]
SLOPES = [2.0 ** (-8.0 * (h + 1) / 4) for h in range(4)]
DILK = 5
TOPK = 16
NCH = 128


def shape_constants():
    def dist_table(q, k):
        d = q[:, None] - k[None, :]
        ok = d >= 0
        cnt = ((d <= 128).astype(float) + ((d % 4 == 0) & (d <= 512)) + ((d % 16 == 0) & (d <= 2048))) * ok
        return d, cnt

    r = np.arange(P)
    keep, mix = {}, {}
    keep["ident"] = np.eye(P)
    keep["ones"] = np.ones((P, P))
    keep["iota"] = np.tile(r, (P, 1))
    keep["iota16"] = np.tile(np.arange(16), (P, 1))
    keep["zero"] = np.zeros((P, 512))
    gt = (r[:, None] > r[None, :]).astype(float)
    mix["ones_gt"] = np.concatenate([np.ones((P, 896)), gt], 1)
    mix["neg_le"] = -(r[:, None] <= r[None, :]).astype(float)
    mix["neg_one"] = -np.ones((P, P))
    for name, blk in (("64", 64), ("4", 4)):
        w = P if blk == 64 else NS
        same = (r[:, None] // blk == r[None, :w] // blk)
        mix["le" + name] = ((r[:, None] <= r[None, :w]) & same).astype(float)
        mix["gt" + name] = ((r[:, None] > r[None, :w]) & same).astype(float)
    for s in (1, 2, 4, 8, 16, 32):
        mix[f"lev{s}"] = ((r[:, None] // (2 * s) == r[None, :] // (2 * s)) & (r[:, None] % (2 * s) < s)
                          & (r[None, :] % (2 * s) >= s)).astype(float)
    mix["rowb"] = (r[:, None] // T == np.arange(B)[None, :]).astype(float)
    mix["colb"] = np.tile((np.arange(NS)[None, :] // T == np.arange(B)[:, None]).reshape(1, -1).astype(float), (P, 1))
    mix["half"] = np.concatenate([np.tile((r < 64)[:, None], (1, 64)), np.tile((r >= 64)[:, None], (1, 64))], 1)
    dd, cc = [], []
    for qt in range(2):
        d, cnt = dist_table(128 * qt + r, np.arange(SEQ))
        dd.append(np.where(cnt > 0, d, 1e32))
        cc.append(cnt)
    mix["pdist"] = np.concatenate(dd, 1)
    mix["pcnt"] = np.concatenate(cc, 1)
    mix["causal"] = np.where(r[None, :] <= r[:, None], 0.0, NEG)
    rb, rh, rt = r // 16, (r % 16) // 4, r % 4
    kb, kt = np.arange(NS) // T, np.arange(NS) % T
    mine = (rb[:, None] == kb[None, :]) & (kt[None, :] <= rt[:, None])
    mix["smask"] = np.where(mine, 0.0, NEG)
    mix["neg_le4"] = np.zeros((P, NS))
    mix["neg_le4"][:NS] = -((kb[:, None] == kb[None, :]) & (kt[:, None] <= kt[None, :])).astype(float)
    pos = np.concatenate([(16 * np.arange(32)[:, None] + np.arange(4)[None, :]).ravel(), np.arange(512, PAST)])
    d = PAST + rt[:, None] - pos[None, :]
    cnt = (d <= 128).astype(float) + ((d % 4 == 0) & (d <= 512)) + ((d % 16 == 0) & (d <= 2048))
    dn = rt[:, None] - kt[None, :]
    cn = np.where(mine, 1.0 + (dn % 4 == 0) + (dn % 16 == 0), 0.0)
    d, cnt = np.concatenate([d, dn], 1), np.concatenate([cnt, cn], 1)
    sl = np.array(SLOPES)[rh][:, None]
    mix["sbias"] = np.where(cnt > 0, -sl * d, NEG)
    mix["scnt"] = cnt
    blocks, where = [], {}
    for part in (keep, mix):
        at = 0
        for k, v in part.items():
            where[k] = (at, v.shape[1])
            at += v.shape[1]
        blocks.append(np.ascontiguousarray(np.concatenate(list(part.values()), 1).astype(np.float32)))
    return blocks[0], blocks[1], where


class Banks:

    def __init__(self, filled, drained, psum):
        self.filled, self.drained, self.psum = filled, drained, psum
        self.at, self.uses, self.where = 0, [0] * 8, {}

    def plan(self, name, i, n=1, banks=None):
        got = []
        for b in banks or [(self.at + m) % 8 for m in range(n)]:
            self.at = b + 1
            got.append((b, self.uses[b]))
            self.uses[b] += 1
        self.where[(name, i)] = got

    def ap(self, name, i=0, k=0):
        return self.psum[:, self.where[(name, i)][k][0], :]

    def full_sem(self, name, i=0, k=0):
        return self.filled[self.where[(name, i)][k][0]]

    def out_sem(self, name, i=0, k=0):
        return self.drained[self.where[(name, i)][k][0]]

    def wait_free(self, eng, l, name, i=0, k=0):
        b, o = self.where[(name, i)][k]
        if l * self.uses[b] + o > 0:
            eng.wait_ge(self.drained[b], l * self.uses[b] + o)

    def wait_full(self, eng, l, name, i=0, k=0):
        b, o = self.where[(name, i)][k]
        eng.wait_ge(self.filled[b], l * self.uses[b] + o + 1)

    def wait_out(self, eng, l, name, i=0, k=0):
        b, o = self.where[(name, i)][k]
        eng.wait_ge(self.drained[b], l * self.uses[b] + o + 1)


class Signal:

    def __init__(self, sem, n, step=1):
        self.sem, self.n, self.step, self.given = sem, n, step, 0

    def by(self, ins):
        self.given += 1
        ins.then_inc(self.sem, self.step)
        return ins

    def wait(self, eng, l, k):
        eng.wait_ge(self.sem, l * (self.n * self.step) + k * self.step)


class Steps:

    def __init__(self, sem):
        self.sem, self.given = sem, 0

    def by(self, ins):
        self.given += 1
        ins.then_inc(self.sem, 1)

    def settle(self, eng):
        eng.wait_ge(self.sem, self.given)


STORES = 27


def build(nc, a, where):
    ctx = ExitStack()
    with ctx:
        def sb(name, shape, dt=F32):
            return ctx.enter_context(nc.sbuf_tensor(name, shape, dt))

        def sem(name):
            return ctx.enter_context(nc.semaphore(name))


        KEEPW, MIXW = a["c_keep"].shape[1], a["c_mix"].shape[1]
        SIDEW = 9088
        with nc.sbuf_tensor("x_parts", [P, 3, D], F32R) as x_parts, \
                nc.sbuf_tensor("hT_parts", [P, DC, N], F32R) as hT_parts, \
                nc.sbuf_tensor("side_parts", [P, SIDEW], F32R) as side_parts:
            pass
        x = sb("x", [P, 3, D])
        hT = sb("hT", [P, DC, N])
        side = sb("side", [P, SIDEW])
        parts_of = {"x": x_parts, "hT": hT_parts, "side": side_parts}
        keep = sb("keep", [P, KEEPW])
        small = sb("small", [P, 640])
        ptab = sb("ptab", [1, B * PAGES], I32)
        pidx = sb("pidx", [B * PAGES, 2], I32)
        arena = sb("arena", [P, NCH * N])
        psum = ctx.enter_context(nc.psum_tensor("psum", [P, 8, 512], F32))

        class Area:
            def __init__(self, tensor, at, end):
                self.t, self.at, self.end = tensor, at, end

            def take(self, n):
                got = self.t[:, self.at:self.at + n]
                self.at += n
                assert self.at <= self.end, (self.at, self.end)
                return got

            def rest(self):
                return Area(self.t, self.at, self.end)

        def K(name):
            o, w = where[name]
            return keep[:, o:o + w]

        ident, ones, iota, iota16, zero = (K(n) for n in ("ident", "ones", "iota", "iota16", "zero"))
        sm = Area(small, 0, 640)
        ms, gain, fbias, alog, naexp = sm.take(8), sm.take(64), sm.take(12), sm.take(8), sm.take(8)
        fraw, baraw = sm.take(12), sm.take(48)
        y12, e12, s12, q12, p12, lg = (sm.take(36) for _ in range(6))
        beta, eg, qkss = sm.take(24), sm.take(48), sm.take(16)
        mneg, den, dnorm, gm = sm.take(4), sm.take(4), sm.take(HD), sm.take(64)
        lgv = lg.rearrange("p (t c) -> p t c", t=3)
        egv = eg.rearrange("p (t c) -> p t c", t=3)
        betav = beta.rearrange("p (t c) -> p t c", t=3)

        whole = Area(arena, 0, NCH * N)
        mixc = whole.take(MIXW)
        mixT = whole.take(DC * N).rearrange("p (c n) -> p c n", n=N)
        qkT = whole.take(8 * N).rearrange("p (c n) -> p c n", n=N)
        kvrow = whole.take(3 * 1024).rearrange("p (t g c) -> p t g c", t=3, g=2)
        zrow = whole.take(3 * 512).rearrange("p (t c) -> p t c", t=3)
        tok = whole.take(3 * 1536).rearrange("p (t s c) -> p t s c", t=3, s=3)

        def C(name):
            o, w = where[name]
            return mixc[:, o:o + w]

        pj, bj = whole.rest(), Area(side, 0, SIDEW)
        wring = [pj.take(DC * 528) for _ in range(3)]
        LPAD, LOUT = 3 + SEQ + 7 * B, SEQ + 7 * B
        cT = pj.take(12 * LPAD).rearrange("p (c n) -> p c n", n=LPAD)
        cO = bj.take(12 * LPAD).rearrange("p (c n) -> p c n", n=LPAD)
        cOseq = cO[:, :, 3 + SEQ:LPAD].rearrange("p c (b s) -> p c b s", b=B)
        cS = bj.take(12 * N).rearrange("p (c n) -> p c n", n=N)
        crow = bj.take(CONV)
        xn = side[:, 0:2 * D].rearrange("p (s c) -> p s c", s=2)
        vrows = side[:, 2 * D:2 * D + P]

        dl, db = whole.rest(), Area(side, 0, SIDEW)
        per = [dict(zip(("attnT", "TT", "qeT", "nwT", "vb", "kd"), [dl.take(n) for n in (1024,) * 4 + (512,) * 2]))
               for _ in range(2)]
        sb2 = whole.rest()
        nwm, qem, vnm, s0 = sb2.take(2048), sb2.take(2048), sb2.take(2048), sb2.take(4096)
        GG, EX, EXI, LT = (dl.take(1024) for _ in range(4))
        T0, P1, kT, kq = db.take(1024), db.take(1024), db.take(1024), db.take(2048)
        kb, kbe, qe = (db.take(512) for _ in range(3))
        LM = GG
        per.append(dict(zip(("attnT", "TT", "qeT", "nwT", "vb", "kd"),
                        [db.take(256)] + [dl.take(n) for n in (256,) * 3 + (512,) * 2])))
        vnw = dl.take(512), db.take(512), db.take(512)
        st = dl.take(512)
        otok = db.take(512), db.take(512), dl.take(512)
        eglT = db.take(96)

        at, ab = whole.rest(), Area(side, 0, SIDEW)
        ring = [at.take(2048).rearrange("p (k c) -> p k c", c=256) for _ in range(4)]
        KT = [at.take(2048).rearrange("p (g k) -> p g k", g=2) for _ in range(2)]
        lfr = at.take(1024).rearrange("p (g r) -> p g r", g=PAGES)
        lfb = at.take(1024).rearrange("p (t h q) -> p t h q", t=2, h=4)
        PTs = at.take(1024).rearrange("p (g r) -> p g r", g=PAGES)
        OB = at.take(512)
        QZ = ab.take(2048).rearrange("p (g b r) -> p g b r", g=2, b=B)
        QA = ab.take(256).rearrange("p (g r) -> p g r", g=2)
        SMp = [ab.take(512).rearrange("p (a k) -> p a k", a=2) for _ in range(2)]
        PRp = [ab.take(512).rearrange("p (a k) -> p a k", a=2) for _ in range(2)]
        PTp = [ab.take(512).rearrange("p (g a q) -> p g a q", g=2, a=2) for _ in range(2)]
        PRs = ab.take(1056)
        SNs, PTn, lfrn = ab.take(32), ab.take(128), ab.take(128)
        lfg = ab.take(512)

        ff = Area(arena, MIXW + DC * N, NCH * N)
        wo = ff.take(DC * D).rearrange("p (c n) -> p c n", n=D)
        wq = ff.take(DC * 2 * D).rearrange("p (c n) -> p c n", n=2 * D)
        topv = [ff.take(256).rearrange("p (g k) -> p g k", k=TOPK) for _ in range(3)]
        topf = [ff.take(256).rearrange("p (g k) -> p g k", k=TOPK) for _ in range(3)]
        fv, fa, fb = (ff.take(128).rearrange("p (h k) -> p h k", h=NH) for _ in range(3))
        ijw = [ff.take(384).rearrange("p (s k) -> p s k", s=3) for _ in range(3)]
        hsum = ff.take(16)
        fu = Area(arena, 0, MIXW)
        qTf = fu.take(16 * N).rearrange("p (c n) -> p c n", n=N)
        over_wo = wo.rearrange("p c n -> p (c n)")
        keysr = side[:, 2048:4096].rearrange("p (g d) -> p g d", g=16)
        keysT = side[:, 4096:6144].rearrange("p (g k) -> p g k", g=16)
        scb = [part.rearrange("p (g k) -> p g k", g=16)
               for part in (over_wo[:, 0:2048], over_wo[:, 2048:4096], side[:, 0:2048])]
        sc2 = over_wo[:, 4096:6144].rearrange("p (g k) -> p g k", g=16)
        cand = over_wo[:, 6144:8192]
        cand2 = side[:, 0:2048]
        oneh = ((over_wo[:, 4096:6144], over_wo[:, 0:2048]), (over_wo[:, 2048:4096], side[:, 2048:4096]))
        topu = [ff.take(256).bitcast(U32).rearrange("p (g k) -> p g k", k=TOPK) for _ in range(3)]
        posu = ff.take(128).bitcast(U32).rearrange("p (h k) -> p h k", h=NH)
        posw = ff.take(256).bitcast(U32).rearrange("p (s h k) -> p s h k", s=2, h=NH)

        G = arena[:, :].rearrange("p (j n) -> p j n", n=N)
        pr = Area(side, 0, SIDEW)
        ubuf = [pr.take(D) for _ in range(2)]
        vbuf = [pr.take(D) for _ in range(2)]
        UTh, UTl = (pr.take(D).rearrange("p (c e) -> p c e", c=DC) for _ in range(2))
        aT = [pr.take(N) for _ in range(2)]
        vh = [pr.take(D) for _ in range(2)]
        over_x = x.rearrange("p t c -> p (t c)")
        hTh = over_x[:, 0:DC * N].rearrange("p (c n) -> p c n", n=N)
        ge = [over_x[:, DC * N + N * i:DC * N + N * (i + 1)] for i in range(2)]
        YT = side[:, 0:DC * N].rearrange("p (c n) -> p c n", n=N)
        NHOT = 4
        hot = [side[:, 4096 + 1024 * i:5120 + 1024 * i].rearrange("p (s m k) -> p s m k", s=2, m=4)
               for i in range(NHOT)]
        ijwT = side[:, SIDEW - 3 * N:SIDEW].rearrange("p (s n) -> p s n", s=3)

        def exact(ap):
            whole_tensor = parts_of[ap.tensor.name][:]
            return bass.AP(tensor=whole_tensor.tensor, offset=ap.offset, ap=ap.ap)

        filled = [sem(f"bank_filled{b}") for b in range(8)]
        drained = [sem(f"bank_drained{b}") for b in range(8)]
        bk = Banks(filled, drained, psum)
        sigs = {}

        def sig(name, n, step=1):
            sigs[name] = Signal(sem(name), n, step)
            return sigs[name]

        keep_loaded = sem("keep_loaded")
        ptab_loaded = sem("ptab_loaded")
        pidx_loaded = sem("pidx_loaded")
        x_loaded = sem("x_loaded")
        y_stored = sem("y_stored")
        init_done = sem("init_done")
        final_step = sem("final_step")
        pidx_moved = sem("pidx_moved")
        final_ready = sem("final_ready")
        final_ms = sem("final_ms")
        final_root = sem("final_root")
        gfin_loaded = sem("gfin_loaded")
        phase_done = sem("phase_done")
        NPH, ARRIVE = 5, 4
        dve_step = Steps(sem("dve_step"))
        mixc_loaded = sig("mixc_loaded", 1, 16)
        rows_loaded = sig("rows_loaded", 3, 16)
        params_loaded = sig("params_loaded", 4, 16)
        crow_loaded = sig("crow_loaded", 1, 16)
        w_loaded = [sem(f"w_loaded{i}") for i in range(3)]
        ms_ready = sig("ms_ready", 12)
        root_ready = sig("root_ready", 12)
        xn_ready = sig("xn_ready", 6)
        gate_arg = sig("gate_arg", 1)
        gate_exp = sig("gate_exp", 1)
        gates_ready = sig("gates_ready", 1)
        pad_zeroed = sig("pad_zeroed", 1)
        conv_done = sig("conv_done", 3)
        silu_done = sig("silu_done", 3)
        tile_rows = sig("tile_rows", 3)
        gg_ready = sig("gg_ready", 3)
        lm_ready = sig("lm_ready", 14)
        gm_ready = sig("gm_ready", 1)
        state_zeroed = sig("state_zeroed", 1)
        spread_ready = sig("spread_ready", 1)
        vnm_ready = sig("vnm_ready", 2)
        s0_loaded = sig("s0_loaded", 8, 16)
        states_ready = sig("states_ready", 2)
        onorm_ready = sig("onorm_ready", 3)
        lfb_ready = sig("lfb_ready", 1)
        negmax_ready = sig("negmax_ready", 8)
        exp_ready = sig("exp_ready", 8)
        probs_ready = sig("probs_ready", 8)
        lfg_loaded = sig("lfg_loaded", 1, 16)
        q_zeroed = sig("q_zeroed", 1)
        q_spread = sig("q_spread", 2)
        s_negmax = sig("s_negmax", 2)
        s_exp = sig("s_exp", 2)
        s_probs = sig("s_probs", 2)
        ring_loaded = [sem(f"ring_loaded{i}") for i in range(4)]
        v_used = sig("v_used", 16)
        wo_loaded = [sig(f"wo_loaded{i}", 1, 16) for i in range(2)]
        wq_loaded = [sig(f"wq_loaded{i}", 1, 16) for i in range(4)]
        keys_loaded = sig("keys_loaded", 2, 16)
        fv_ready = sig("fv_ready", 3)
        fv_exp = sig("fv_exp", 3)
        ijw_ready = sig("ijw_ready", 3)
        rows_hot = sig("rows_hot", 3)
        looked = sig("looked", 12)
        looked_up = sig("looked_up", 3)
        stored = sig("stored", STORES, 16)
        hot_ready = sem("hot_ready")
        hot_weighted = sem("hot_weighted")
        gate_filled = sem("gate_filled")
        gate_out = sem("gate_out")
        x_spilled = sig("x_spilled", 3, 16)
        x_summed = sig("x_summed", 1)
        x_reloaded = sig("x_reloaded", 3, 16)
        hT_high = sig("hT_high", 1)
        hT_split = sig("hT_split", 1)
        u_loaded = [sem(f"u_loaded{i}") for i in range(2)]
        v_loaded = [sem(f"v_loaded{i}") for i in range(2)]
        ut_filled = [sem(f"ut_filled{i}") for i in range(2)]
        ut_high = [sem(f"ut_high{i}") for i in range(2)]
        ut_split = [sem(f"ut_split{i}") for i in range(2)]
        v_high = sem("v_high")
        v_split = sem("v_split")
        gated_ready = sem("gated_ready")
        at_high = sem("at_high")
        h_filled = sem("h_filled")
        gelu_done = sem("gelu_done")
        at_split = sem("at_split")
        y_done = sem("y_done")
        yt_ready = sig("yt_ready", 1)

        bk.plan("vecT", 0)
        for i in range(6):
            bk.plan("xT_mix", i)
        bk.plan("csT", 0)
        for t in range(3):
            bk.plan("fv", t)
        for t in range(3):
            bk.plan("ba", t)
            bk.plan("z", t)
        for i in range(8):
            bk.plan("pT", i)
        for t in range(3):
            bk.plan("ktok", t)
        for t in range(3):
            bk.plan("dv", t)
        for i in range(8, 16):
            bk.plan("pT", i)
        for t in range(3):
            bk.plan("tk", (0, t))
        for i in range(16, 20):
            bk.plan("pT", i)
        for t in range(3):
            bk.plan("tk", (1, t))
        for i in range(3):
            bk.plan("craw", i)
        for t in range(3):
            bk.plan("tk", (2, t))
        LEV = ((1, 2, 4, 8, 16, 32), (1, 2, 4, 8, 16, 32), (1, 2))
        bk.plan("gl", 0)
        bk.plan("gls", 0)
        for t in range(3):
            nb = 2 if t < 2 else 1
            bk.plan("gcs", t)
            bk.plan("dec", t, nb)
            for kind in range(4):
                bk.plan("tr", (t, kind), nb)
            bk.plan("kk", t, 4 if t < 2 else 1)
            for s in LEV[t]:
                bk.plan("p1", (t, s), nb)
                if s > 1:
                    if s != LEV[t][-1]:
                        bk.plan("dd", (t, s), nb)
                    bk.plan("dt", (t, s), nb)
            bk.plan("wT", t, nb)
            if t == 1:
                for c in range(4):
                    bk.plan("vn", c)
                    bk.plan("oo", c)
                    bk.plan("st", c)
        bk.plan("vn", 4)
        bk.plan("oo", 4)
        for h in range(NH):
            bk.plan("st", 4 + h)
        for t in range(3):
            bk.plan("oT", t)
        bk.plan("S", (0, 0))
        bk.plan("S", (0, 1))
        for u in range(8):
            if u < 7:
                bk.plan("S", (u + 1, 0))
                bk.plan("S", (u + 1, 1))
            bk.plan("PT", u)
            bk.plan("O", u)
        bk.plan("lfT", 0)
        for g in range(2):
            bk.plan("SS", g, banks=(0, 1))
            bk.plan("SN", g, banks=(2,))
            for b in range(B):
                bk.plan("kTs", (g, b), banks=(3, 4, 5, 6))
            bk.plan("PTs", g, banks=(3, 4, 5))
            bk.plan("OS", g, banks=(7,))
            bk.plan("OT", g, banks=(6,))
        for i in range(4):
            bk.plan("kyT", i)
        for hf in range(2):
            for t in range(3):
                bk.plan("y", 2 * t + hf)
        for i in range(6):
            bk.plan("xT_ffn", i)
        for g in range(4):
            for i in range(4 * g, 4 * g + 4):
                bk.plan("qf", i)
            for t in range(3):
                bk.plan("sc", (t, g))
        for t in range(3):
            bk.plan("ijwT", t)
        for i in range(6):
            bk.plan("yb", i)

        YBANKS, SPARE = 6, 512 - N
        PIECES = [[(c, 0, 0, N)] for c in range(YBANKS)]
        for i in range(DC - YBANKS):
            PIECES.append([(i, N, 0, SPARE), (i + 2, N, SPARE, N)])

        CHUNKS = [(512, 260), (3076, 528), (0, 512), (772, 512), (1284, 256), (1540, 512), (2052, 512), (2564, 512)]
        LASTUSE = [("fv", 2), ("z", 2), ("pT", 3), ("pT", 7), ("dv", 2), ("pT", 11), ("pT", 15), ("pT", 19)]
        WUSES = [3, 3, 2]
        CACHE = [(g, kv, b) for g in range(2) for kv in range(2) for b in range(B)]
        RINC = [8 * 16, 2 * 16]
        rcount, RUSE = [0] * 4, {}
        for i, (g, kv, b) in enumerate(CACHE):
            rcount[i % 4] += RINC[g]
            RUSE[(g, kv, b)] = (i % 4, rcount[i % 4])

        def wchunk(i):
            return wring[i % 3][:, 0:DC * CHUNKS[i][1]].rearrange("p (c n) -> p c n", c=DC)

        def w_wait(eng, l, i):
            eng.wait_ge(w_loaded[i % 3], (l * WUSES[i % 3] + i // 3 + 1) * 16)

        def ring_wait(eng, l, key):
            s, c = RUSE[key]
            eng.wait_ge(ring_loaded[s], l * rcount[s] + c)

        def phase(eng, l, k, arrive=True):
            if arrive:
                eng.drain().then_inc(phase_done, 1)
            eng.wait_ge(phase_done, l * (NPH * ARRIVE) + ARRIVE * (k + 1))

        def row0(l, ap):
            return ap[l:l + 1]

        def cache_loads(eng, l, odd):
            for i, (g, kv, b) in enumerate(CACHE):
                if i % 2 != odd:
                    continue
                if i >= 4:
                    g0, kv0, b0 = CACHE[i - 4]
                    if kv0:
                        v_used.wait(eng, l, B * g0 + b0 + 1)
                    else:
                        bk.wait_full(eng, l, "kTs", (g0, b0), 3)
                dst = ring[i % 4]
                if g == 0:
                    for pg in range(PAGES):
                        page = eng.value_load(ptab[0:1, b * PAGES + pg:b * PAGES + pg + 1], min_val=0,
                                              max_val=NPOOL - 1)
                        src = a["cache_fox_kv"].rearrange("l n s k h d -> (l n) s k (h d)")[
                            bass.ds(page + l * NPOOL, 1), :, kv, :].rearrange("o s c -> (o s) c")
                        eng.dma_start(dst[:, pg, :], src).then_inc(ring_loaded[i % 4], 16)
                else:
                    src = row0(l, a["cache_dil_kv"])[:, b, :, kv].rearrange("o s h d -> (o s) (h d)")
                    eng.dma_start(dst[:, 0, :], src[0:512, :].rearrange("(m s) c -> m s c", s=16)[:, 0:4, :])\
                        .then_inc(ring_loaded[i % 4], 16)
                    eng.dma_start(dst[:, 1:DILK, :], src[512:PAST, :].rearrange("(k s) c -> s k c", s=P))\
                        .then_inc(ring_loaded[i % 4], 16)

        x_kept = nc.dram_tensor("x_kept", (N, D), F32, kind="Internal").ap()
        block = ctx.enter_context(nc.Block())

        @block.sync
        def _(sp):
            def load_w(l, i):
                c0, w = CHUNKS[i]
                src = row0(l, a["w_in"]).rearrange("o (c p) n -> (o p) c n", p=P)[:, :, c0:c0 + w]
                sp.dma_start(wchunk(i), src).then_inc(w_loaded[i % 3], 16)

            sp.dma_start(keep[:, :], a["c_keep"]).then_inc(keep_loaded, 16)
            for t, (n0, r) in enumerate(TILES):
                src = a["x_prompt"][0, n0:n0 + r, :] if t < 2 else a["x_sample"].rearrange("b t d -> (b t) d")
                sp.dma_start(x[0:r, t, :], src).then_inc(x_loaded, 16)
            sp.dma_start(ptab[:, :], a["page_table"].rearrange("(o b) g -> o (b g)", o=1)).then_inc(ptab_loaded, 16)
            sp.wait_ge(ptab_loaded, 16)
            sp.wait_ge(init_done, 1)
            for l in range(DEPTH):
                if l:
                    sp.wait_ge(phase_done, l * (NPH * ARRIVE))
                rows_loaded.by(sp.dma_start(vrows[0:48, :], row0(l, a["conv_w"]).rearrange(
                    "o i (c p) -> (o i c) p", p=P)))
                rows_loaded.by(sp.dma_start(vrows[48:56, :], row0(l, a["norm_mix"]).rearrange(
                    "o (c p) -> (o c) p", p=P)))
                rows_loaded.by(sp.dma_start(vrows[56:64, :], row0(l, a["norm_ffn"]).rearrange(
                    "o (c p) -> (o c) p", p=P)))
                for dst, name, w in ((fbias[:, 0:4], "b_fox_f", 4), (fbias[:, 4:12], "dt_bias", 8), (alog, "a_log", 8),
                                     (dnorm, "delta_norm", HD)):
                    params_loaded.by(sp.dma_start(dst, row0(l, a[name]).to_broadcast([P, w])))
                crow_loaded.by(sp.dma_start(crow[0:24, :], row0(l, a["state_conv"]).rearrange("o b i c -> (o b i) c")))
                for i in range(0 if l == 0 else 3, len(CHUNKS)):
                    if i < 3:
                        load_w(l, i)
                        continue
                    if i == 4:
                        mixc_loaded.by(sp.dma_start(mixc, a["c_mix"]))
                    bk.wait_full(sp, l, *LASTUSE[i - 3])
                    load_w(l, i)
                phase(sp, l, 0, arrive=False)
                bk.wait_full(sp, l, "st", 3)
                for b in range(B):
                    s0_loaded.by(sp.dma_start(
                        s0[0:HD, 512 * b:512 * (b + 1)].rearrange("p (h v) -> p h v", h=NH),
                        row0(l, a["state_delta"])[:, b].rearrange("o h d v -> (o d) h v")))
                phase(sp, l, 1, arrive=False)
                cache_loads(sp, l, 0)
                phase(sp, l, 2, arrive=False)
                for i in range(2):
                    keys_loaded.by(sp.dma_start(keysr[:, 8 * i:8 * i + 8, :], row0(l, a["peer_keys"]).rearrange(
                        "o h c k d -> (o k) (h c) d")[:, 8 * i:8 * i + 8, :]))
                for i in range(2):
                    wo_loaded[i].by(sp.dma_start(wo[:, :, 512 * i:512 * (i + 1)], row0(l, a["w_out"]).rearrange(
                        "o (c p) n -> (o p) c n", p=P)[:, :, 512 * i:512 * (i + 1)]))
                for i in range(4):
                    wq_loaded[i].by(sp.dma_start(wq[:, :, 512 * i:512 * (i + 1)], row0(l, a["peer_wq"]).rearrange(
                        "o (c p) n -> (o p) c n", p=P)[:, :, 512 * i:512 * (i + 1)]))
                phase(sp, l, 3, arrive=False)

                def load_u(j, s, turned):
                    rows = row0(l, a["peer_u"]).rearrange("o (i j) d -> (o i) j d", j=NCH)[:, j, :]
                    if turned is not None:
                        sp.wait_ge(ut_filled[1], turned)
                    sp.dma_start(ubuf[s], rows).then_inc(u_loaded[s], 16)

                def load_v(j, s, used):
                    rows = row0(l, a["peer_v"]).rearrange("o (i j) d -> (o i) j d", j=NCH)[:, j, :]
                    if used is not None:
                        sp.wait_ge(y_done, used)
                    sp.dma_start(vbuf[s], rows).then_inc(v_loaded[s], 16)

                first = l * NCH
                for j in range(2):
                    load_u(j, j, None)
                    load_v(j, j, None)
                load_u(2, 0, first + 1)
                with sp.Fori(1, NCH // 2 - 1) as m:
                    for s in range(2):
                        load_u(bass.ds(m * 2 + (s + 1), 1), 1 - s, m * 2 + (first + s))
                        load_v(bass.ds(m * 2 + s, 1), s, m * 2 + (first + s - 1))
                load_u(NCH - 1, 1, first + NCH - 2)
                load_v(NCH - 2, 0, first + NCH - 3)
                load_v(NCH - 1, 1, first + NCH - 2)
                if l + 1 < DEPTH:
                    sp.wait_ge(gated_ready, first + 112)
                    for i in range(3):
                        load_w(l + 1, i)
                sp.wait_ge(y_done, first + NCH)
                for t, (n0, r) in enumerate(TILES):
                    x_reloaded.by(sp.dma_start(x[0:r, t, :], x_kept[n0:n0 + r, :]))
            sp.wait_ge(phase_done, DEPTH * NPH * ARRIVE)
            sp.dma_start(arena[:, 0:D], a["norm_final"].rearrange("(o n) -> o n", o=1).to_broadcast([P, D]))\
                .then_inc(gfin_loaded, 16)

        @block.gpsimd
        def _(pool):
            outs = a["outs"]
            pool.wait_ge(ptab_loaded, 16)
            pool.dma_start(pidx[:, 0:1], a["page_table"].rearrange("b g -> (b g)").rearrange("(n o) -> n o", o=1))\
                .then_inc(pidx_loaded, 16)
            pool.wait_ge(pidx_loaded, 16)

            def gate_weights(l):
                def group(i, s, tokens):
                    pool.wait_ge(hot_ready, i + 1)
                    pool.tensor_tensor(hot[s][:, 1], hot[s][:, 1],
                                       ijwT[:, 2, tokens][:, :, None].to_broadcast([P, 4, P]), ALU.mult)\
                        .then_inc(hot_weighted, 1)

                for s in range(NHOT):
                    group(l * (N // 4) + s, s, slice(4 * s, 4 * s + 4))
                with pool.Fori(1, N // (4 * NHOT)) as g:
                    for s in range(NHOT):
                        group(l * (N // 4) + g * NHOT + s, s, bass.ds(g * (4 * NHOT) + 4 * s, 4))

            for l in range(DEPTH):
                gates_ready.wait(pool, l, 1)
                lo = row0(l, outs["fox_logf_prompt"]).rearrange("o b s h -> (o b s) h")
                stored.by(pool.dma_start(lo[0:128, :], lgv[:, 0, 0:4]))
                stored.by(pool.dma_start(lo[128:256, :], lgv[:, 1, 0:4]))
                stored.by(pool.dma_start(row0(l, outs["fox_logf_sample"]).rearrange("o b s h -> (o b s) h"),
                                         lgv[0:NS, 2, 0:4]))
                for t in range(3):
                    bk.wait_out(pool, l, "ktok", t)
                    bk.wait_out(pool, l, "fv", t)
                    bk.wait_out(pool, l, "dv", t)
                    for g, name in ((0, "fox_kv"), (1, "dil_kv")):
                        dst = row0(l, outs[name + ("_prompt" if t < 2 else "_sample")])\
                            .rearrange("o b s k h d -> (o b s) (k h d)")
                        n0, r = TILES[t] if t < 2 else (0, NS)
                        stored.by(pool.dma_start(dst[n0:n0 + r, :], kvrow[0:r, t, g, :]))
                for i in range(3):
                    bk.wait_out(pool, l, "craw", i)
                stored.by(pool.dma_start(row0(l, outs["conv_state_prompt"]).rearrange("o b i c -> (o b i) c"),
                                         crow[0:3, :]))
                for b in range(B):
                    stored.by(pool.dma_start(row0(l, outs["conv_state_sample"])[:, b].rearrange("o i c -> (o i) c"),
                                             crow[7 + 7 * b:10 + 7 * b, :]))
                NP0 = 3 + 6 + 9
                stored.wait(pool, l, NP0)
                phase(pool, l, 0)
                states_ready.wait(pool, l, 1)
                stored.by(pool.dma_start(row0(l, outs["delta_state_prompt"]).rearrange("o b h d v -> (o b d) h v"),
                                         st[0:HD, :].rearrange("p (h v) -> p h v", h=NH)))
                states_ready.wait(pool, l, 2)
                for b in range(B):
                    stored.by(pool.dma_start(
                        row0(l, outs["delta_state_sample"])[:, b].rearrange("o h d v -> (o d) h v"),
                        s0[0:HD, 512 * b:512 * (b + 1)].rearrange("p (h v) -> p h v", h=NH)))
                stored.wait(pool, l, NP0 + 9)
                phase(pool, l, 1)
                if l:
                    pool.wait_ge(pidx_moved, l)
                pool.memset(OB, 0.0)
                q_zeroed.by(pool.memset(side[:, 0:2304], 0.0))
                lfg_loaded.by(pool.indirect_dma_start(
                    lfg[0:B * PAGES, :], None, a["cache_fox_logf"].rearrange("l n s h -> (l n) (s h)"),
                    bass.IndirectOffsetOnAxis(ap=pidx[:, 0:1].bitcast(U32), axis=0)))
                lfg_loaded.wait(pool, l, 1)
                pool.tensor_scalar(pidx[:, 0:1], pidx[:, 0:1], float(NPOOL), None, ALU.add).then_inc(pidx_moved, 1)
                cache_loads(pool, l, 1)
                phase(pool, l, 2)
                x_summed.wait(pool, l, 1)
                for t, (n0, r) in enumerate(TILES):
                    x_spilled.by(pool.dma_start(x_kept[n0:n0 + r, :], x[0:r, t, :]))
                for t, (n0, r) in enumerate(TILES):
                    rows_hot.wait(pool, l, t + 1)
                    tf = topf[t][0:r].rearrange("p (h c) k -> p c h k", c=2)
                    for c in range(2):
                        oh = oneh[t % 2][c][0:r].rearrange("p (h k a) -> p h k a", h=NH, a=16)
                        last = pool.tensor_tensor(oh, oh, tf[:, c][:, :, None, :].to_broadcast([r, NH, 16, 16]),
                                                  ALU.mult)
                    looked.by(last)
                    for n, w in enumerate((8, 4, 2, 1)):
                        looked.wait(pool, l, 4 * t + n + 1)
                        for c in range(2):
                            oh = oneh[t % 2][c][0:r].rearrange("p (k a) -> p k a", a=16)
                            out = oh[:, :, 0:w] if w > 1 else ijw[t][0:r, c, :][:, :, None]
                            last = pool.tensor_tensor(out, oh[:, :, 0:w], oh[:, :, w:2 * w], ALU.add)
                        (looked if w > 1 else looked_up).by(last)
                x_spilled.wait(pool, l, 3)
                phase(pool, l, 3)
                gate_weights(l)
                phase(pool, l, 4)
            for t, (n0, r) in enumerate(TILES):
                dst = outs["y_prompt"][0, n0:n0 + r, :] if t < 2 else outs["y_sample"].rearrange("b t d -> (b t) d")
                pool.wait_ge(final_ready, t + 1)
                pool.dma_start(dst, arena[0:r, D * (t + 1):D * (t + 2)]).then_inc(y_stored, 16)
            pool.wait_ge(y_stored, 48)

        @block.tensor
        def _(pe):
            pe.wait_ge(keep_loaded, 16)

            def mm(out, lhsT, rhs, start=True, stop=True):
                return pe.matmul(out, lhsT, rhs, start=start, stop=stop)

            def transposes(l, name, i, k, pieces):
                bk.wait_free(pe, l, name, i, k)
                o = 0
                for piece in pieces:
                    r, w = piece.shape[0], piece.shape[1]
                    last = pe.transpose(bk.ap(name, i, k)[0:w, o:o + r], piece, ident[0:r, 0:r])
                    o += r
                last.then_inc(bk.full_sem(name, i, k), 1)

            def norm_transposes(l, name, base):
                for t, (n0, r) in enumerate(TILES):
                    xn_ready.wait(pe, l, base + t + 1)
                    for hf in range(2):
                        transposes(l, name, 2 * t + hf, 0,
                                   [xn[0:r, t % 2, (4 * hf + k) * P:(4 * hf + k + 1) * P] for k in range(4)])

            def token_rows(l, name, t, chunk, c0, w):
                n0, r = TILES[t]
                bk.wait_free(pe, l, name, t)
                for c in range(DC):
                    last = mm(bk.ap(name, t)[0:r, 0:w], hT[:, c, n0:n0 + r], wchunk(chunk)[:, c, c0:c0 + w],
                              c == 0, c == DC - 1)
                last.then_inc(bk.full_sem(name, t), 1)

            def feature_rows(l, chunk, i0):
                w_wait(pe, l, chunk)
                for i in range(i0, i0 + 4):
                    bk.wait_free(pe, l, "pT", i)
                    o = (i - i0) * P
                    for c in range(DC):
                        last = mm(bk.ap("pT", i)[:, 0:N], wchunk(chunk)[:, c, o:o + P], hT[:, c, :],
                                  c == 0, c == DC - 1)
                    last.then_inc(bk.full_sem("pT", i), 1)

            def project(l):
                rows_loaded.wait(pe, l, 3)
                transposes(l, "vecT", 0, 0, [vrows[0:64, :]])
                norm_transposes(l, "xT_mix", 0)
                crow_loaded.wait(pe, l, 1)
                transposes(l, "csT", 0, 0, [crow[0:24, c * P:(c + 1) * P] for c in range(12)])
                bk.wait_out(pe, l, "xT_mix", 5)
                w_wait(pe, l, 0)
                for t in range(3):
                    token_rows(l, "fv", t, 0, 0, 260)
                w_wait(pe, l, 1)
                for t in range(3):
                    token_rows(l, "ba", t, 1, 0, 16)
                    token_rows(l, "z", t, 1, 16, 512)
                feature_rows(l, 2, 0)
                feature_rows(l, 3, 4)
                for t, (n0, r) in enumerate(TILES):
                    if t == 0:
                        for i in (2, 3, 6, 7):
                            bk.wait_out(pe, l, "pT", i)
                    transposes(l, "ktok", t, 0, [qkT[:, i, n0:n0 + r] for i in (2, 3, 6, 7)])
                w_wait(pe, l, 4)
                for t in range(3):
                    token_rows(l, "dv", t, 4, 0, 256)
                feature_rows(l, 5, 8)
                feature_rows(l, 6, 12)
                conv_rows(l, 0)
                feature_rows(l, 7, 16)
                conv_rows(l, 1)
                for i in range(3):
                    for c in range(4 * i, 4 * i + 4):
                        bk.wait_out(pe, l, "pT", 8 + c)
                    transposes(l, "craw", i, 0, [cT[:, c, SEQ:SEQ + 59] for c in range(4 * i, 4 * i + 4)])
                conv_rows(l, 2)

            def conv_rows(l, s):
                silu_done.wait(pe, l, s + 1)
                for t, (n0, r) in enumerate(TILES):
                    transposes(l, "tk", (s, t), 0, [cS[:, 4 * s + k, n0:n0 + r] for k in range(4)])

            def each_head(l, name, i, W, r, parts, ready=None):
                hpb = 512 // W if W > 32 else NH
                for k in range(NH // hpb):
                    bk.wait_free(pe, l, name, i, k)
                    if ready:
                        ready(k)
                    for hh in range(hpb):
                        h = k * hpb + hh
                        lhsT, rhs = parts(h)
                        last = mm(bk.ap(name, i, k)[0:r, hh * W:(hh + 1) * W], lhsT, rhs)
                    last.then_inc(bk.full_sem(name, i, k), 1)

            def delta_tile(l, t):
                r = W = TILES[t][1]
                q = per[t]
                le, gt = (C("le64"), C("gt64")) if t < 2 else (C("le4"), C("gt4"))
                bk.wait_free(pe, l, "gcs", t)
                mm(bk.ap("gcs", t)[0:r, 0:8], le[0:r, :], lgv[0:r, t, 4:12])
                mm(bk.ap("gcs", t)[0:r, 8:16], gt[0:r, :], lgv[0:r, t, 4:12]).then_inc(bk.full_sem("gcs", t), 1)
                gg_ready.wait(pe, l, t + 1)
                each_head(l, "dec", t, W, r, lambda h: (GG[0:r, h * W:(h + 1) * W], le[0:r, :]))
                tile_rows.wait(pe, l, t + 1)
                rows = (tok[:, t, 1, :], kb, tok[:, t, 0, :], qe)
                for kind in range(4):
                    for k in range(2 if t < 2 else 1):
                        hs = range(4 * k, 4 * k + 4) if t < 2 else range(NH)
                        transposes(l, "tr", (t, kind), k, [rows[kind][0:r, h * HD:(h + 1) * HD] for h in hs])
                for kind in range(3):
                    for k in range(2 if t < 2 else 1):
                        bk.wait_out(pe, l, "tr", (t, kind), k)
                kqv = kq[0:HD, 0:16 * W].rearrange("p (s h w) -> p s h w", s=2, h=NH)
                hpb = 256 // W
                for k in range(NH // hpb):
                    bk.wait_free(pe, l, "kk", t, k)
                    for hh in range(hpb):
                        h = k * hpb + hh
                        last = mm(bk.ap("kk", t, k)[0:r, hh * 2 * W:(hh + 1) * 2 * W], kT[0:HD, h * W:(h + 1) * W],
                                  kqv[:, :, h, :])
                    last.then_inc(bk.full_sem("kk", t, k), 1)
                nb = 2 if t < 2 else 1
                for n, s in enumerate(LEV[t]):
                    before = LEV[t][n - 1] if n else None

                    def t_ready(k):
                        if n:
                            bk.wait_out(pe, l, *(("dd", (t, before), k) if n > 1 else ("p1", (t, 1), k)))

                    def p1_ready(k):
                        bk.wait_out(pe, l, "p1", (t, s), k)
                        if n > 1:
                            bk.wait_out(pe, l, "dt", (t, before), k)

                    lm_ready.wait(pe, l, 6 * t + n + 1)
                    each_head(l, "p1", (t, s), W, r,
                              lambda h: (LM[0:r, h * W:(h + 1) * W], T0[0:r, h * W:(h + 1) * W] if n else
                                         ident[0:r, 0:W]), t_ready)
                    if n:
                        if s != LEV[t][-1]:
                            each_head(l, "dd", (t, s), W, r, lambda h: (q["TT"][0:r, h * W:(h + 1) * W],
                                                                        P1[0:r, h * W:(h + 1) * W]), p1_ready)
                        each_head(l, "dt", (t, s), W, r, lambda h: (P1[0:r, h * W:(h + 1) * W],
                                                                    q["TT"][0:r, h * W:(h + 1) * W]), p1_ready)
                for k in range(nb):
                    bk.wait_out(pe, l, "dt", (t, LEV[t][-1]), k)
                each_head(l, "wT", t, W, HD, lambda h: (kbe[0:r, h * HD:(h + 1) * HD], q["TT"][0:r, h * W:(h + 1) * W]))

            def delta_chunk(l, c):
                t, hf = c // 2, c % 2
                q = per[t]
                rows = slice(64 * hf, 64 * hf + 64)
                if c == 0:
                    state_zeroed.wait(pe, l, 1)
                else:
                    bk.wait_out(pe, l, "st", c - 1)
                for k in range(2):
                    bk.wait_out(pe, l, "wT", t, k)
                    bk.wait_out(pe, l, "tr", (t, 3), k)
                bk.wait_free(pe, l, "vn", c)
                for h in range(NH):
                    o = bk.ap("vn", c)[:, h * HD:(h + 1) * HD]
                    mm(o, q["TT"][:, h * P:(h + 1) * P], q["vb"][:, h * HD:(h + 1) * HD], True, False)
                    last = mm(o, q["nwT"][0:HD, h * P:(h + 1) * P], st[0:HD, h * HD:(h + 1) * HD], False, True)
                last.then_inc(bk.full_sem("vn", c), 1)
                bk.wait_free(pe, l, "oo", c)
                bk.wait_out(pe, l, "vn", c)
                for h in range(NH):
                    o = bk.ap("oo", c)[:, h * HD:(h + 1) * HD]
                    mm(o, q["qeT"][0:HD, h * P:(h + 1) * P], st[0:HD, h * HD:(h + 1) * HD], True, False)
                    last = mm(o, q["attnT"][:, h * P:(h + 1) * P], vnw[t][:, h * HD:(h + 1) * HD], False, True)
                last.then_inc(bk.full_sem("oo", c), 1)
                bk.wait_free(pe, l, "st", c)
                for h in range(NH):
                    last = mm(bk.ap("st", c)[0:HD, h * HD:(h + 1) * HD], q["kd"][rows, h * HD:(h + 1) * HD],
                              vnw[t][rows, h * HD:(h + 1) * HD])
                last.then_inc(bk.full_sem("st", c), 1)

            def delta_sample(l):
                q = per[2]
                s0_loaded.wait(pe, l, 8)
                spread_ready.wait(pe, l, 1)
                bk.wait_free(pe, l, "vn", 4)
                for h in range(NH):
                    o = bk.ap("vn", 4)[0:NS, h * HD:(h + 1) * HD]
                    mm(o, q["TT"][0:NS, h * NS:(h + 1) * NS], q["vb"][0:NS, h * HD:(h + 1) * HD], True, False)
                    for b in range(B):
                        last = mm(o, nwm[0:HD, (h * B + b) * NS:(h * B + b + 1) * NS],
                                  s0[0:HD, b * 512 + h * HD:b * 512 + (h + 1) * HD], False, b == B - 1)
                last.then_inc(bk.full_sem("vn", 4), 1)
                bk.wait_free(pe, l, "oo", 4)
                bk.wait_out(pe, l, "vn", 4)
                for h in range(NH):
                    o = bk.ap("oo", 4)[0:NS, h * HD:(h + 1) * HD]
                    for b in range(B):
                        mm(o, qem[0:HD, (h * B + b) * NS:(h * B + b + 1) * NS],
                           s0[0:HD, b * 512 + h * HD:b * 512 + (h + 1) * HD], b == 0, False)
                    last = mm(o, q["attnT"][0:NS, h * NS:(h + 1) * NS], vnw[2][0:NS, h * HD:(h + 1) * HD], False, True)
                last.then_inc(bk.full_sem("oo", 4), 1)
                for h in range(NH):
                    vnm_ready.wait(pe, l, h // 4 + 1)
                    bk.wait_free(pe, l, "st", 4 + h)
                    mm(bk.ap("st", 4 + h)[0:HD, :], q["kd"][0:NS, h * HD:(h + 1) * HD],
                       vnm[0:NS, (h % 4) * 512:(h % 4 + 1) * 512]).then_inc(bk.full_sem("st", 4 + h), 1)

            def delta(l):
                gates_ready.wait(pe, l, 1)
                bk.wait_free(pe, l, "gl", 0)
                for c in range(4):
                    last = mm(bk.ap("gl")[0:HD, 8 * c:8 * c + 8], C("half")[:, 64 * (c % 2):64 * (c % 2) + 64],
                              lgv[:, c // 2, 4:12])
                last.then_inc(bk.full_sem("gl"), 1)
                gm_ready.wait(pe, l, 1)
                bk.wait_free(pe, l, "gls", 0)
                mm(bk.ap("gls")[0:HD, 0:64], ones[0:NS, 0:HD], gm[0:NS, :]).then_inc(bk.full_sem("gls"), 1)
                delta_tile(l, 0)
                delta_tile(l, 1)
                for c in range(4):
                    delta_chunk(l, c)
                delta_tile(l, 2)
                delta_sample(l)
                for t, (n0, r) in enumerate(TILES):
                    onorm_ready.wait(pe, l, t + 1)
                    transposes(l, "oT", t, 0, [otok[t][0:r, k * P:(k + 1) * P] for k in range(4)])

            def prompt_scores(l, u):
                g, hp, qt = u // 4, (u // 2) % 2, u % 2
                KW = P * (qt + 1)
                for ah in range(2):
                    po = 64 * ah
                    bk.wait_free(pe, l, "S", (u, ah))
                    o = bk.ap("S", (u, ah))
                    last = mm(o[:, 0:KW], qkT[po:po + 64, 4 * g + hp, qt * P:(qt + 1) * P],
                              qkT[po:po + 64, 4 * g + 2 + hp, 0:KW], True, g == 1)
                    if g == 0:
                        for kt in range(qt + 1):
                            for tt in range(kt + 1):
                                last = mm(o[:, kt * P:(kt + 1) * P], lfb[:, tt, 2 * hp + ah, :],
                                          C("neg_le") if tt == kt else C("neg_one"), False, (kt, tt) == (qt, qt))
                    last.then_inc(bk.full_sem("S", (u, ah)), 1)

            def prompt_values(l, u):
                g, hp, qt = u // 4, (u // 2) % 2, u % 2
                probs_ready.wait(pe, l, u + 1)
                transposes(l, "PT", u, 0, [PRp[u % 2][:, ah, kt * P:(kt + 1) * P]
                                           for kt in range(qt + 1) for ah in range(2)])
                bk.wait_out(pe, l, "PT", u)
                bk.wait_free(pe, l, "O", u)
                for kt in range(qt + 1):
                    last = mm(bk.ap("O", u)[:, 0:256], kvrow[:, kt, g, 256 + hp * P:256 + (hp + 1) * P],
                              PTp[u % 2][:, kt, :, :], kt == 0, kt == qt)
                last.then_inc(bk.full_sem("O", u), 1)

            def sample_attention(l, g):
                q_spread.wait(pe, l, g + 1)
                nk = PAGES if g == 0 else DILK
                widths = (512, 512) if g == 0 else (512, 128)
                for k in range(2):
                    if k == 0:
                        bk.wait_free(pe, l, "SS", g, 0)
                    else:
                        bk.wait_free(pe, l, "SN", g)
                banks = psum[:, 0:2, :]
                if g == 0:
                    bk.wait_out(pe, l, "lfT", 0)
                    for pg in range(PAGES - 1, -1, -1):
                        if pg >= 4:
                            w = P * (pg - 3)
                            mm(banks[:, 1, 0:w], lfr[:, pg, :], C("ones_gt")[:, 1024 - w:1024], pg == 7, False)
                            mm(banks[:, 0, :], lfr[:, pg, :], C("ones_gt")[:, 0:512], pg == 7, False)
                        else:
                            w = P * (pg + 1)
                            mm(banks[:, 0, 0:w], lfr[:, pg, :], C("ones_gt")[:, 1024 - w:1024], False, False)

                def scores(b):
                    for hp in range(2):
                        for k in range(2):
                            bk.wait_out(pe, l, "kTs", (g, b), 2 * hp + k)
                            w = widths[k]
                            fin = b == B - 1 and hp == 1
                            last = mm(banks[:, k, 0:w], QZ[:, hp, b, :], KT[b % 2][:, hp, 512 * k:512 * k + w],
                                      g == 1 and b == 0 and hp == 0, fin)
                            if fin:
                                last.then_inc(bk.full_sem("SS", g, k), 1)

                for b in range(B):
                    ring_wait(pe, l, (g, 0, b))
                    tile = ring[RUSE[(g, 0, b)][0]]
                    for hp in range(2):
                        for k in range(2):
                            tiles = range(4 * k, min(nk, 4 * k + 4))
                            transposes(l, "kTs", (g, b), 2 * hp + k, [tile[:, kt, hp * P:(hp + 1) * P] for kt in tiles])
                    if b:
                        scores(b - 1)
                scores(B - 1)
                bk.wait_free(pe, l, "SN", g)
                o = bk.ap("SN", g)[:, 0:NS]
                mm(o, QA[:, 0, :], qkT[:, 4 * g + 2, SEQ:N], True, False)
                last = mm(o, QA[:, 1, :], qkT[:, 4 * g + 3, SEQ:N], False, g == 1)
                if g == 0:
                    last = mm(o, lfrn[0:NS, :], C("neg_le4")[0:NS, :], False, True)
                last.then_inc(bk.full_sem("SN", g), 1)
                s_probs.wait(pe, l, g + 1)
                for k in range(2):
                    transposes(l, "PTs", g, k, [PRs[:, kt * P:(kt + 1) * P] for kt in range(4 * k, min(nk, 4 * k + 4))])
                transposes(l, "PTs", g, 2, [PRs[:, nk * P:nk * P + NS]])
                for k in range(3):
                    bk.wait_out(pe, l, "PTs", g, k)
                bk.wait_free(pe, l, "OS", g)
                for b in range(B):
                    ring_wait(pe, l, (g, 1, b))
                    tile = ring[RUSE[(g, 1, b)][0]]
                    o = bk.ap("OS", g)[32 * (b % 4):32 * (b % 4) + 16, 256 * (b // 4):256 * (b // 4) + 256]
                    for kt in range(nk):
                        last = mm(o, PTs[:, kt, 16 * b:16 * b + 16], tile[:, kt, :], kt == 0, False)
                    v_used.by(last)
                    last = mm(o, PTn[0:NS, 16 * b:16 * b + 16], kvrow[0:NS, 2, g, 256:512], False, True)
                last.then_inc(bk.full_sem("OS", g), 1)
                bk.wait_out(pe, l, "OS", g)
                transposes(l, "OT", g, 0, [OB[:, k * P:(k + 1) * P] for k in range(4)])

            def attention(l):
                lfb_ready.wait(pe, l, 1)
                prompt_scores(l, 0)
                for u in range(8):
                    if u < 7:
                        prompt_scores(l, u + 1)
                    prompt_values(l, u)
                lfg_loaded.wait(pe, l, 1)
                transposes(l, "lfT", 0, 0, [lfg[0:B * PAGES, :].rearrange("p (s h) -> p h s", h=4)[:, h, :]
                                            for h in range(4)])
                for g in range(2):
                    sample_attention(l, g)

            def out_projection(l):
                keys_loaded.wait(pe, l, 2)
                for i in range(4):
                    transposes(l, "kyT", i, 0, [keysr[:, 4 * i + k, :] for k in range(4)])
                for hf in range(2):
                    wo_loaded[hf].wait(pe, l, 1)
                    for t, (n0, r) in enumerate(TILES):
                        bk.wait_free(pe, l, "y", 2 * t + hf)
                        for c in range(DC):
                            last = mm(bk.ap("y", 2 * t + hf)[0:r, :], mixT[:, c, n0:n0 + r],
                                      wo[:, c, 512 * hf:512 * hf + 512], c == 0, c == DC - 1)
                        last.then_inc(bk.full_sem("y", 2 * t + hf), 1)

            def retrieval(l):
                norm_transposes(l, "xT_ffn", 3)
                for i in range(6):
                    bk.wait_out(pe, l, "xT_ffn", i)
                for g in range(4):
                    wq_loaded[g].wait(pe, l, 1)
                    for i in range(4 * g, 4 * g + 4):
                        bk.wait_free(pe, l, "qf", i)
                        for c in range(DC):
                            last = mm(bk.ap("qf", i)[:, 0:N], wq[:, c, i * P:(i + 1) * P], hT[:, c, :],
                                      c == 0, c == DC - 1)
                        last.then_inc(bk.full_sem("qf", i), 1)
                    bk.wait_out(pe, l, "kyT", g)
                    for i in range(4 * g, 4 * g + 4):
                        bk.wait_out(pe, l, "qf", i)
                    for t, (n0, r) in enumerate(TILES):
                        bk.wait_free(pe, l, "sc", (t, g))
                        for k in range(4):
                            i = 4 * g + k
                            last = mm(bk.ap("sc", (t, g))[0:r, k * P:(k + 1) * P], qTf[:, i, n0:n0 + r],
                                      keysT[:, i, :])
                        last.then_inc(bk.full_sem("sc", (t, g)), 1)
                for t, (n0, r) in enumerate(TILES):
                    ijw_ready.wait(pe, l, t + 1)
                    looked_up.wait(pe, l, t + 1)
                    transposes(l, "ijwT", t, 0, [ijw[t][0:r, s, :] for s in range(3)])

            def gates(l):
                def group(i, s, reuse):
                    pe.wait_ge(hot_weighted, i + 1)
                    if reuse:
                        pe.wait_ge(gate_out, i + (1 - NHOT))
                    for m in range(4):
                        last = mm(psum[:, 8 - NHOT + s, m * P:(m + 1) * P], hot[s][:, 0, m, :], hot[s][:, 1, m, :])
                    last.then_inc(gate_filled, 1)

                for s in range(NHOT):
                    group(l * (N // 4) + s, s, False)
                with pe.Fori(1, N // (4 * NHOT)) as m:
                    for s in range(NHOT):
                        group(l * (N // 4) + m * NHOT + s, s, True)

            def stream(l):
                first = l * NCH
                pe.wait_ge(gate_out, l * (N // 4) + N // 4)
                for b in range(YBANKS):
                    last = mm(psum[:, b, :], zero[0:32, 0:P], zero[0:32, :], True, False)

                def turn(j, s, k):
                    if k == 0:
                        pe.wait_ge(u_loaded[s], j[1])
                    if k:
                        pe.wait_ge(ut_split[0], j[0] + 1)
                    elif j[2]:
                        pe.wait_ge(ut_split[1], j[0])
                    for c in range(4):
                        last = pe.transpose(psum[:, 6, c * P:(c + 1) * P],
                                            ubuf[s][:, (4 * k + c) * P:(4 * k + c + 1) * P], ident)
                    last.then_inc(ut_filled[k], 1)

                def hidden(j):
                    for k in range(2):
                        pe.wait_ge(ut_split[k], j[0] + 1)
                    if j[2]:
                        pe.wait_ge(gelu_done, j[0])
                    for c in range(DC):
                        for n, (u, h) in enumerate(((UTh, hTh), (UTh, hT), (UTl, hTh))):
                            last = mm(psum[:, 7, 0:N], exact(u[:, c, :]), exact(h[:, c, :]),
                                      c == 0 and n == 0, c == DC - 1 and n == 2)
                    last.then_inc(h_filled, 1)

                FIRST = 5

                def down(j, s, half, last_chunk=False):
                    if half == 0:
                        pe.wait_ge(v_split, j[0] + 1)
                        pe.wait_ge(at_split, j[0] + 1)
                    for c in (range(FIRST), range(FIRST, DC))[half]:
                        for v, at_ in ((vh, ge), (vh, aT), (vbuf, ge)):
                            for bank, o, n0, n1 in PIECES[c]:
                                last = pe.matmul(psum[:, bank, o:o + n1 - n0], exact(v[s][:, c * P:(c + 1) * P]),
                                                 exact(at_[s][:, n0:n1]), start=False, stop=False,
                                                 skip_group_check=True)
                    if last_chunk:
                        for b in range(YBANKS):
                            last = mm(psum[:, b, :], zero[0:32, 0:P], zero[0:32, :], False, True)
                    if half:
                        last.then_inc(y_done, 1)

                def chunk(j):
                    return (first + j, l * (16 * NCH // 2) + 16 * (j // 2 + 1), j > 0)

                hT_split.wait(pe, l, 1)
                turn(chunk(0), 0, 0)
                turn(chunk(0), 0, 1)
                turn(chunk(1), 1, 0)
                hidden(chunk(0))
                turn(chunk(1), 1, 1)
                with pe.Fori(1, NCH // 2) as m:
                    for s in range(2):
                        this = (first + m * 2 + s, l * (16 * NCH // 2) + m * 16 + 16, True)
                        two_back = (first + m * 2 + (s - 2), 0)
                        turn(this, s, 0)
                        hidden((first + m * 2 + (s - 1), 0, True))
                        down(two_back, s, 0)
                        turn(this, s, 1)
                        down(two_back, s, 1)
                hidden(chunk(NCH - 1))
                for j in (NCH - 2, NCH - 1):
                    for half in range(2):
                        down(chunk(j), j % 2, half, half == 1 and j == NCH - 1)
                yt_ready.wait(pe, l, 1)
                for t, (n0, r) in enumerate(TILES):
                    for hf in range(2):
                        bk.wait_free(pe, l, "yb", 2 * t + hf)
                        for k in range(4):
                            last = pe.transpose(bk.ap("yb", 2 * t + hf)[0:r, k * P:(k + 1) * P],
                                                YT[:, 4 * hf + k, n0:n0 + r], ident)
                        last.then_inc(bk.full_sem("yb", 2 * t + hf), 1)

            for l in range(DEPTH):
                project(l)
                phase(pe, l, 0)
                mixc_loaded.wait(pe, l, 1)
                delta(l)
                phase(pe, l, 1)
                attention(l)
                phase(pe, l, 2)
                out_projection(l)
                retrieval(l)
                phase(pe, l, 3)
                gates(l)
                stream(l)
                phase(pe, l, 4)

        @block.scalar
        def _(act):
            def out_of(l, name, i, k, dst, src, func=ACT.Copy, scale=1.0):
                bk.wait_full(act, l, name, i, k)
                act.activation(dst, src, func, scale=scale).then_inc(bk.out_sem(name, i, k), 1)

            def roots(l, i, t, r, w=1):
                ms_ready.wait(act, l, i + 1)
                root_ready.by(act.activation(ms[0:r, t:t + w], ms[0:r, t:t + w], ACT.Sqrt))

            def project(l):
                for t, (n0, r) in enumerate(TILES):
                    roots(l, t, t, r)
                bk.wait_full(act, l, "csT")
                seq = cT[:, :, 3 + SEQ:LPAD].rearrange("p c (b s) -> p c b s", b=B)
                for c in range(12):
                    last = act.activation(seq[:, c, :, 0:3], bk.ap("csT")[:, 24 * c:24 * c + 24].rearrange(
                        "p (b s) -> p b s", b=B), ACT.Copy)
                last.then_inc(bk.out_sem("csT"), 1)
                for t, (n0, r) in enumerate(TILES):
                    bk.wait_full(act, l, "fv", t)
                    act.activation(kvrow[0:r, t, 0, 256:512], bk.ap("fv", t)[0:r, 0:256], ACT.Copy)
                    act.activation(fraw[0:r, 4 * t:4 * t + 4], bk.ap("fv", t)[0:r, 256:260], ACT.Copy)\
                        .then_inc(bk.out_sem("fv", t), 1)
                for t, (n0, r) in enumerate(TILES):
                    out_of(l, "ba", t, 0, baraw[0:r, 16 * t:16 * t + 16], bk.ap("ba", t)[0:r, 0:16])
                    out_of(l, "z", t, 0, zrow[0:r, t, :], bk.ap("z", t)[0:r, :], ACT.Silu)
                gate_arg.wait(act, l, 1)
                act.activation(e12, e12, ACT.Exp)
                act.activation(beta.rearrange("p (t c) -> p t c", t=3),
                               baraw.rearrange("p (t c) -> p t c", t=3)[:, :, 0:8], ACT.Exp, scale=-1.0)
                params_loaded.wait(act, l, 4)
                gate_exp.by(act.activation(naexp, alog, ACT.Exp))
                for i in range(8):
                    out_of(l, "pT", i, 0, qkT[:, i, :], bk.ap("pT", i)[:, 0:N], scale=0.125 if i % 4 < 2 else 1.0)
                for t, (n0, r) in enumerate(TILES):
                    out_of(l, "ktok", t, 0, kvrow[0:r, t, :, 0:256],
                           bk.ap("ktok", t)[0:r, :].rearrange("p (g c) -> p g c", g=2))
                for t, (n0, r) in enumerate(TILES):
                    out_of(l, "dv", t, 0, kvrow[0:r, t, 1, 256:512], bk.ap("dv", t)[0:r, 0:256])

                def conv_in(i0):
                    for i in range(i0, i0 + 4):
                        bk.wait_full(act, l, "pT", i)
                        act.activation(cT[:, i - 8, 3:3 + SEQ], bk.ap("pT", i)[:, 0:SEQ], ACT.Copy)
                        act.activation(seq[:, i - 8, :, 3:7], bk.ap("pT", i)[:, SEQ:N].rearrange(
                            "p (b s) -> p b s", b=B), ACT.Copy).then_inc(bk.out_sem("pT", i), 1)

                def conv_silu(s):
                    conv_done.wait(act, l, s + 1)
                    act.activation(cS[:, 4 * s:4 * s + 4, 0:SEQ], cO[:, 4 * s:4 * s + 4, 0:SEQ], ACT.Silu)
                    for c in range(4 * s, 4 * s + 4):
                        last = act.activation(cS[:, c, SEQ:N].rearrange("p (b s) -> p b s", b=B),
                                              cOseq[:, c, :, 0:4], ACT.Silu)
                    silu_done.by(last)

                conv_in(8)
                conv_in(12)
                conv_silu(0)
                for t, (n0, r) in enumerate(TILES):
                    out_of(l, "tk", (0, t), 0, tok[0:r, t, 0, :], bk.ap("tk", (0, t))[0:r, :])
                conv_in(16)
                conv_silu(1)
                for t, (n0, r) in enumerate(TILES):
                    out_of(l, "tk", (1, t), 0, tok[0:r, t, 1, :], bk.ap("tk", (1, t))[0:r, :])
                for i in range(3):
                    out_of(l, "craw", i, 0, crow[0:59, 512 * i:512 * i + 512], bk.ap("craw", i)[0:59, :])
                conv_silu(2)
                for t, (n0, r) in enumerate(TILES):
                    out_of(l, "tk", (2, t), 0, tok[0:r, t, 2, :], bk.ap("tk", (2, t))[0:r, :])

            def delta_tile(l, t):
                r = W = TILES[t][1]
                q = per[t]
                nb = 2 if t < 2 else 1
                bw = 512 if t < 2 else 256
                out_of(l, "gcs", t, 0, egv[0:r, t, :], bk.ap("gcs", t)[0:r, 0:16], ACT.Exp)
                ms_ready.wait(act, l, 3 + t + 1)
                root_ready.by(act.activation(qkss[0:r, :], qkss[0:r, :], ACT.Sqrt))
                for k in range(nb):
                    out_of(l, "dec", t, k, EX[0:r, 512 * k:512 * k + bw], bk.ap("dec", t, k)[0:r, 0:bw], ACT.Exp)
                dsts = (kT, kq, kq[:, NH * W:], q["qeT"])
                for kind in range(4):
                    for k in range(nb):
                        out_of(l, "tr", (t, kind), k, dsts[kind][0:HD, 512 * k:512 * k + bw],
                               bk.ap("tr", (t, kind), k)[0:HD, 0:bw])
                for s in LEV[t][1:]:
                    for k in range(nb):
                        out_of(l, "p1", (t, s), k, P1[0:r, 512 * k:512 * k + bw], bk.ap("p1", (t, s), k)[0:r, 0:bw])
                for k in range(nb):
                    out_of(l, "wT", t, k, q["nwT"][0:HD, 512 * k:512 * k + bw], bk.ap("wT", t, k)[0:HD, 0:bw],
                           scale=-1.0)

            def delta(l):
                out_of(l, "gl", 0, 0, eglT[0:HD, 0:32], bk.ap("gl")[0:HD, 0:32], ACT.Exp)
                out_of(l, "gls", 0, 0, eglT[0:HD, 32:96], bk.ap("gls")[0:HD, 0:64], ACT.Exp)
                delta_tile(l, 0)
                delta_tile(l, 1)
                state_zeroed.wait(act, l, 1)
                for c in range(4):
                    t, rows = c // 2, slice(64 * (c % 2), 64 * (c % 2) + 64)
                    out_of(l, "vn", c, 0, vnw[t][rows, :], bk.ap("vn", c)[rows, :])
                    out_of(l, "oo", c, 0, otok[t][rows, :], bk.ap("oo", c)[rows, :])
                delta_tile(l, 2)
                out_of(l, "vn", 4, 0, vnw[2][0:NS, :], bk.ap("vn", 4)[0:NS, :])
                out_of(l, "oo", 4, 0, otok[2][0:NS, :], bk.ap("oo", 4)[0:NS, :])
                for t, (n0, r) in enumerate(TILES):
                    ms_ready.wait(act, l, 6 + t + 1)
                    root_ready.by(act.activation(ms[0:r, 0:8], ms[0:r, 0:8], ACT.Sqrt))
                for t, (n0, r) in enumerate(TILES):
                    out_of(l, "oT", t, 0, mixT[:, 4:8, n0:n0 + r],
                           bk.ap("oT", t)[:, 0:4 * r].rearrange("p (c n) -> p c n", c=4))

            def attention(l):
                for u in range(8):
                    g, hp, qt = u // 4, (u // 2) % 2, u % 2
                    KW = P * (qt + 1)
                    negmax_ready.wait(act, l, u + 1)
                    for ah in range(2):
                        m = 2 * (u % 2) + ah
                        last = act.activation(PRp[u % 2][:, ah, 0:KW], SMp[u % 2][:, ah, 0:KW], ACT.Exp,
                                              bias=mneg[:, m:m + 1], accum_out=den[:, m:m + 1])
                    exp_ready.by(last)
                    nt = 2 * (qt + 1)
                    out_of(l, "PT", u, 0, PTp[u % 2][:, 0:qt + 1, :, :], bk.ap("PT", u)[:, 0:nt * P].rearrange(
                        "p (g a q) -> p g a q", a=2, q=P))
                    bk.wait_full(act, l, "O", u)
                    for ah in range(2):
                        last = act.activation(mixT[64 * ah:64 * ah + 64, 2 * g + hp, qt * P:(qt + 1) * P],
                                              bk.ap("O", u)[64 * ah:64 * ah + 64, ah * P:(ah + 1) * P], ACT.Copy)
                    last.then_inc(bk.out_sem("O", u), 1)
                bk.wait_full(act, l, "lfT")
                rep = lfr.rearrange("p g (b h q) -> p g b h q", b=B, h=4)
                lf = bk.ap("lfT")[:, 0:256].rearrange("p (h b g) -> p g b h", h=4, b=B)
                for pg in range(PAGES):
                    last = act.activation(rep[:, pg], lf[:, pg][:, :, :, None].to_broadcast([P, B, 4, 4]), ACT.Copy)
                last.then_inc(bk.out_sem("lfT"), 1)
                for g in range(2):
                    w4 = (512, 512) if g == 0 else (512, 128)
                    for b in range(B):
                        for hp in range(2):
                            out_of(l, "kTs", (g, b), 2 * hp, KT[b % 2][:, hp, 0:512], bk.ap("kTs", (g, b), 2 * hp)[:, :])
                    s_negmax.wait(act, l, g + 1)
                    if g == 0:
                        for k in range(2):
                            bk.wait_full(act, l, "SS", 0, k)
                            act.activation(PRs[:, 512 * k:512 * k + 512], psum[:, k, :], ACT.Exp, bias=mneg[:, 0:1],
                                           accum_out=den[:, k:k + 1]).then_inc(bk.out_sem("SS", 0, k), 1)
                        s_exp.by(act.activation(PRs[:, 1024:1056], SNs, ACT.Exp, bias=mneg[:, 0:1],
                                                accum_out=den[:, 2:3]))
                    else:
                        s_exp.by(act.activation(PRs[:, 0:DILK * P + NS], PRs[:, 0:DILK * P + NS], ACT.Exp,
                                                bias=mneg[:, 0:1]))
                    for k in range(2):
                        w = w4[k]
                        out_of(l, "PTs", g, k, PTs[:, 4 * k:4 * k + w // P, :],
                               bk.ap("PTs", g, k)[:, 0:w].rearrange("p (g r) -> p g r", r=P))
                    out_of(l, "PTs", g, 2, PTn[0:NS, :], bk.ap("PTs", g, 2)[0:NS, 0:P])
                    bk.wait_full(act, l, "OS", g)
                    for q in range(4):
                        last = act.activation(OB[32 * q:32 * q + 16, :], bk.ap("OS", g)[32 * q:32 * q + 16, :], ACT.Copy)
                    last.then_inc(bk.out_sem("OS", g), 1)

            def retrieval(l):
                for i in range(4):
                    out_of(l, "kyT", i, 0, keysT[:, 4 * i:4 * i + 4, :],
                           bk.ap("kyT", i)[:, :].rearrange("p (g k) -> p g k", g=4))
                for t, (n0, r) in enumerate(TILES):
                    roots(l, 9 + t, t, r)
                for g in range(4):
                    for i in range(4 * g, 4 * g + 4):
                        out_of(l, "qf", i, 0, qTf[:, i, :], bk.ap("qf", i)[:, 0:N])
                    for t, (n0, r) in enumerate(TILES):
                        out_of(l, "sc", (t, g), 0, scb[t][0:r, 4 * g:4 * g + 4, :],
                               bk.ap("sc", (t, g))[0:r, :].rearrange("p (g k) -> p g k", g=4))
                for t, (n0, r) in enumerate(TILES):
                    fv_ready.wait(act, l, t + 1)
                    fv_exp.by(act.activation(ijw[t][0:r, 2, :], ijw[t][0:r, 2, :], ACT.Exp))
                    out_of(l, "ijwT", t, 0, ijwT[:, :, n0:n0 + r],
                           bk.ap("ijwT", t)[:, 0:3 * r].rearrange("p (s n) -> p s n", s=3))

            def gates(l):
                def group(i, s, n0):
                    act.wait_ge(gate_filled, i + 1)
                    act.activation(G[:, :, n0], psum[:, 8 - NHOT + s, :].rearrange("p (m j) -> p j m", m=4),
                                   ACT.Copy).then_inc(gate_out, 1)

                hT_high.by(act.activation(exact(hTh), hT[:, :, :], ACT.Copy))
                with act.Fori(0, N // (4 * NHOT)) as m:
                    for s in range(NHOT):
                        group(l * (N // 4) + m * NHOT + s, s, bass.ds(m * (4 * NHOT) + 4 * s, 4))

            def stream(l):
                first = l * NCH

                def high_u(j, k, again):
                    if again and k == 0:
                        act.wait_ge(h_filled, j)
                    act.wait_ge(ut_filled[k], j + 1)
                    act.activation(exact(UTh[:, 4 * k:4 * k + 4, :]),
                                   psum[:, 6, :].rearrange("p (c e) -> p c e", c=4), ACT.Copy)\
                        .then_inc(ut_high[k], 1)

                def gelu(j, s, again):
                    act.wait_ge(h_filled, j + 1)
                    if again:
                        act.wait_ge(y_done, j + -1)
                    act.activation(ge[s], psum[:, 7, 0:N], ACT.Gelu).then_inc(gelu_done, 1)

                def high_v(j, s, loaded, again):
                    act.wait_ge(v_loaded[s], loaded)
                    if again:
                        act.wait_ge(y_done, j + -1)
                    act.activation(exact(vh[s]), vbuf[s], ACT.Copy).then_inc(v_high, 1)

                def high_a(j, s):
                    act.wait_ge(gated_ready, j + 1)
                    act.activation(exact(ge[s]), aT[s], ACT.Copy).then_inc(at_high, 1)

                def chunk(j, s, loaded, again, following=True):
                    if following:
                        high_u(j + 1, 0, True)
                    gelu(j, s, again)
                    if following:
                        high_u(j + 1, 1, True)
                    high_a(j, s)
                    high_v(j, s, loaded, again)

                v0 = l * (16 * NCH // 2) + 16
                for k in range(2):
                    high_u(first, k, False)
                chunk(first, 0, v0, False)
                chunk(first + 1, 1, v0, False)
                with act.Fori(1, NCH // 2 - 1) as m:
                    for s in range(2):
                        chunk(first + m * 2 + s, s, m * 16 + v0, True)
                chunk(first + NCH - 2, 0, v0 + 16 * (NCH // 2 - 1), True)
                chunk(first + NCH - 1, 1, v0 + 16 * (NCH // 2 - 1), True, False)
                act.wait_ge(y_done, first + NCH)
                for c in range(DC):
                    for bank, o, n0, n1 in PIECES[c]:
                        last = act.activation(YT[:, c, n0:n1], psum[:, bank, o:o + n1 - n0], ACT.Copy)
                yt_ready.by(last)

            for l in range(DEPTH):
                project(l)
                phase(act, l, 0)
                delta(l)
                phase(act, l, 1)
                attention(l)
                phase(act, l, 2)
                retrieval(l)
                phase(act, l, 3)
                gates(l)
                stream(l)
                phase(act, l, 4)
            for t, (n0, r) in enumerate(TILES):
                act.wait_ge(final_ms, t + 1)
                act.activation(ms[0:r, t:t + 1], ms[0:r, t:t + 1], ACT.Sqrt).then_inc(final_root, 1)

        @block.vector
        def _(dve):
            v = nc.vector

            def settle():
                dve_step.settle(dve)

            def step(ins):
                dve_step.by(ins)
                settle()

            def tt(out, in0, in1, op):
                return v.tensor_tensor(out, in0, in1, op)

            def ts(out, in0, s1, op0, s2=None, op1=None):
                if op1 is None:
                    return v.tensor_scalar(out, in0, s1, None, op0)
                return v.tensor_scalar(out, in0, s1, s2, op0, op1)

            def stt(out, in0, scalar, in1, op0, op1):
                return v.scalar_tensor_tensor(out=out, in0=in0, scalar=scalar, in1=in1, op0=op0, op1=op1)

            def norm_rows(l, base, name, g0, between=None):
                for t, (n0, r) in enumerate(TILES):
                    if t == 2:
                        bk.wait_full(dve, l, name, 1)
                    junk = xn[0:r, t % 2, :]
                    step(v.tensor_tensor_reduce(junk, x[0:r, t, :], x[0:r, t, :], 1.0, 0.0, ALU.mult, ALU.add,
                                                   ms[0:r, t:t + 1]))
                    ms_ready.by(ts(ms[0:r, t:t + 1], ms[0:r, t:t + 1], 1.0 / D, ALU.mult, EPS, ALU.add))
                    root_ready.wait(dve, l, (0 if base == 0 else 9) + t + 1)
                    step(v.reciprocal(ms[0:r, t:t + 1], ms[0:r, t:t + 1]))
                    xn_ready.by(ts(junk, x[0:r, t, :], ms[0:r, t:t + 1], ALU.mult))
                    if between and t == 1:
                        between()
                for t, (n0, r) in enumerate(TILES):
                    for hf in range(2):
                        bk.wait_full(dve, l, name, 2 * t + hf)
                        tt(hT[:, 4 * hf:4 * hf + 4, n0:n0 + r],
                           bk.ap(name, 2 * t + hf)[:, 0:4 * r].rearrange("p (c n) -> p c n", c=4),
                           gain[:, g0 + 4 * hf:g0 + 4 * hf + 4][:, :, None].to_broadcast([P, 4, r]), ALU.mult)\
                            .then_inc(bk.out_sem(name, 2 * t + hf), 1)

            def log1p_exp(l, y, out):
                step(stt(e12, y, -1.0, y, ALU.mult, ALU.min))
                gate_arg.by(ts(q12, y, 1.0, ALU.mult))
                gate_exp.wait(dve, l, 1)
                step(ts(s12, e12, 2.0, ALU.add))
                step(v.reciprocal(s12, s12))
                step(tt(s12, e12, s12, ALU.mult))
                step(tt(q12, s12, s12, ALU.mult))
                step(ts(p12, q12, 1.0 / 17, ALU.mult))
                for n in (15, 13, 11, 9, 7, 5, 3):
                    step(stt(p12, p12, 1.0 / n, q12, ALU.add, ALU.mult))
                step(stt(p12, p12, 1.0, s12, ALU.add, ALU.mult))
                step(ts(p12, p12, 2.0, ALU.mult))
                step(stt(out, y, 0.0, p12, ALU.max, ALU.add))

            def project(l):
                pad_zeroed.by(v.memset(cT[:, :, 0:3], 0.0))

                def gains():
                    bk.wait_full(dve, l, "vecT")
                    v.tensor_copy(gain, bk.ap("vecT")[:, 0:64]).then_inc(bk.out_sem("vecT"), 1)
                    bk.wait_out(dve, l, "vecT")

                norm_rows(l, 0, "xT_mix", 48, gains)
                params_loaded.wait(dve, l, 4)
                for t in range(3):
                    bk.wait_out(dve, l, "fv", t)
                    bk.wait_out(dve, l, "ba", t)
                yv = y12.rearrange("p (t c) -> p t c", t=3)
                fb3 = fbias[:, None, :].to_broadcast([P, 3, 12])
                stt(yv[:, :, 0:4], fraw.rearrange("p (t c) -> p t c", t=3), -1.0, fb3[:, :, 0:4], ALU.mult,
                    ALU.subtract)
                step(tt(yv[:, :, 4:12], baraw.rearrange("p (t c) -> p t c", t=3)[:, :, 8:16], fb3[:, :, 4:12],
                           ALU.add))
                log1p_exp(l, y12, lg)
                step(ts(beta, beta, 1.0, ALU.add))
                step(v.reciprocal(beta, beta))
                step(ts(lgv[:, :, 0:4], lgv[:, :, 0:4], -1.0, ALU.mult))
                gates_ready.by(stt(lgv[:, :, 4:12], lgv[:, :, 4:12], -1.0,
                                   naexp[:, None, :].to_broadcast([P, 3, 8]), ALU.mult, ALU.mult))

                def conv(s):
                    for c in range(4 * s, 4 * s + 4):
                        bk.wait_out(dve, l, "pT", 8 + c)
                    for c in range(4 * s, 4 * s + 4):
                        dve_step.by(ts(cO[:, c, 0:LOUT], cT[:, c, 0:LOUT], gain[:, c:c + 1], ALU.mult))
                    for i in range(1, 4):
                        settle()
                        for c in range(4 * s, 4 * s + 4):
                            last = stt(cO[:, c, 0:LOUT], cT[:, c, i:i + LOUT], gain[:, 12 * i + c:12 * i + c + 1],
                                       cO[:, c, 0:LOUT], ALU.mult, ALU.add)
                            (conv_done if (i, c) == (3, 4 * s + 3) else dve_step).by(last)

                bk.wait_out(dve, l, "csT")
                pad_zeroed.wait(dve, l, 1)
                for s in range(3):
                    conv(s)

            def heads(ap, w=HD):
                return ap.rearrange("p (h d) -> p h d", d=w)

            def delta_tile(l, t):
                r = W = TILES[t][1]
                q = per[t]
                nb = 2 if t < 2 else 1
                hpb = NH // nb
                le, gt = (C("le64"), C("gt64")) if t < 2 else (C("le4"), C("gt4"))
                qk = tok[0:r, t, 0:2, :].rearrange("p s (h d) -> p (s h) d", d=HD)
                if t:
                    for k in range(2):
                        bk.wait_full(dve, l, "wT", t - 1, k)
                gg_ready.by(tt(heads(GG[0:r, 0:NH * W], W), gt[0:r, None, :].to_broadcast([r, NH, W]),
                               lgv[0:r, t, 4:12][:, :, None].to_broadcast([r, NH, W]), ALU.mult))
                sq = LT[0:r, :]
                step(tt(heads(sq), qk, qk, ALU.mult))
                step(v.tensor_reduce(qkss[0:r, :], heads(sq), AX.X, ALU.add))
                ms_ready.by(ts(qkss[0:r, :], qkss[0:r, :], EPS, ALU.add))
                root_ready.wait(dve, l, 3 + t + 1)
                step(v.reciprocal(qkss[0:r, :], qkss[0:r, :]))
                step(ts(qkss[0:r, 0:8], qkss[0:r, 0:8], 0.125, ALU.mult))
                step(tt(qk, qk, qkss[0:r, :][:, :, None].to_broadcast([r, 16, HD]), ALU.mult))
                bk.wait_out(dve, l, "gcs", t)

                def scaled(out, rows, by):
                    return tt(heads(out[0:r, :]), heads(rows), by[:, :, None].to_broadcast([r, NH, HD]), ALU.mult)

                step(scaled(kb, tok[0:r, t, 1, :], betav[0:r, t, :]))
                scaled(q["vb"], tok[0:r, t, 2, :], betav[0:r, t, :])
                scaled(kbe, kb[0:r, :], egv[0:r, t, 0:8])
                scaled(qe, tok[0:r, t, 0, :], egv[0:r, t, 0:8])
                tile_rows.by(scaled(q["kd"], tok[0:r, t, 1, :], egv[0:r, t, 8:16]))
                for k in range(nb):
                    bk.wait_out(dve, l, "dec", t, k)
                step(tt(heads(EXI[0:r, 0:NH * W], W), heads(EX[0:r, 0:NH * W], W),
                           le[0:r, None, :].to_broadcast([r, NH, W]), ALU.mult))
                nk, hk = (4, 2) if t < 2 else (1, 8)
                for k in range(nk):
                    bk.wait_full(dve, l, "kk", t, k)
                    pair = bk.ap("kk", t, k)[0:r, 0:2 * hk * W].rearrange("p (h s w) -> p s h w", h=hk, s=2)
                    cols = slice(k * hk * W, (k + 1) * hk * W)
                    tt(heads(LT[0:r, cols], W), pair[:, 0], heads(EX[0:r, cols], W), ALU.mult)
                    tt(heads(q["attnT"][0:r, cols], W), pair[:, 1], heads(EXI[0:r, cols], W), ALU.mult)\
                        .then_inc(bk.out_sem("kk", t, k), 1)
                for k in range(nk):
                    bk.wait_out(dve, l, "kk", t, k)
                T, TT = T0[0:r, 0:NH * W], q["TT"][0:r, 0:NH * W]
                idb = ident[0:r, None, 0:W].to_broadcast([r, hpb, W])

                def level_blocks(n):
                    lm_ready.by(tt(heads(LM[0:r, 0:NH * W], W), heads(LT[0:r, 0:NH * W], W),
                                   C(f"lev{LEV[t][n]}")[0:r, None, 0:W].to_broadcast([r, NH, W]), ALU.mult))

                level_blocks(0)
                lm_ready.wait(dve, l, 6 * t + 1)
                for n, s in enumerate(LEV[t]):
                    if n == 0:
                        for k in range(nb):
                            cols = slice(k * hpb * W, (k + 1) * hpb * W)
                            tt(heads(TT[:, cols], W), idb, heads(LM[0:r, cols], W), ALU.subtract)
                            bk.wait_full(dve, l, "p1", (t, s), k)
                            tt(heads(T[:, cols], W), idb, heads(bk.ap("p1", (t, s), k)[0:r, 0:hpb * W], W),
                               ALU.subtract).then_inc(bk.out_sem("p1", (t, s), k), 1)
                        for k in range(nb):
                            bk.wait_out(dve, l, "p1", (t, s), k)
                        level_blocks(1)
                        continue
                    if s != LEV[t][-1]:
                        for k in range(nb):
                            bk.wait_full(dve, l, "p1", (t, s), k)
                        level_blocks(n + 1)
                        for k in range(nb):
                            cols = slice(k * hpb * W, (k + 1) * hpb * W)
                            if n > 1:
                                bk.wait_out(dve, l, "dd", (t, LEV[t][n - 1]), k)
                            bk.wait_full(dve, l, "dd", (t, s), k)
                            tt(T[:, cols], T[:, cols], bk.ap("dd", (t, s), k)[0:r, 0:hpb * W], ALU.subtract)\
                                .then_inc(bk.out_sem("dd", (t, s), k), 1)
                    for k in range(nb):
                        cols = slice(k * hpb * W, (k + 1) * hpb * W)
                        if n > 1:
                            bk.wait_out(dve, l, "dt", (t, LEV[t][n - 1]), k)
                        bk.wait_full(dve, l, "dt", (t, s), k)
                        tt(TT[:, cols], TT[:, cols], bk.ap("dt", (t, s), k)[0:r, 0:hpb * W], ALU.subtract)\
                            .then_inc(bk.out_sem("dt", (t, s), k), 1)

            def delta(l):
                v.memset(st[0:HD, :], 0.0)
                v.memset(vnw[0], 0.0)
                state_zeroed.by(v.memset(vnw[1], 0.0))
                gates_ready.wait(dve, l, 1)
                gm_ready.by(tt(gm[0:NS, :].rearrange("p (b h) -> p b h", b=B),
                               C("rowb")[0:NS, :][:, :, None].to_broadcast([NS, B, NH]),
                               lgv[0:NS, 2, 4:12][:, None, :].to_broadcast([NS, B, NH]), ALU.mult))
                delta_tile(l, 0)
                delta_tile(l, 1)
                bk.wait_out(dve, l, "gl")
                state_zeroed.wait(dve, l, 1)
                for c in range(4):
                    bk.wait_full(dve, l, "oo", c)
                    if c:
                        bk.wait_out(dve, l, "st", c - 1)
                    step(tt(heads(st[0:HD, :]), heads(st[0:HD, :]),
                               eglT[0:HD, 8 * c:8 * c + 8][:, :, None].to_broadcast([HD, NH, HD]), ALU.mult))
                    bk.wait_full(dve, l, "st", c)
                    tt(st[0:HD, :], st[0:HD, :], bk.ap("st", c)[0:HD, :], ALU.add).then_inc(bk.out_sem("st", c), 1)
                bk.wait_out(dve, l, "st", 3)
                states_ready.by(v.memset(vnm[0:NS, 0:8], 0.0))
                delta_tile(l, 2)
                bk.wait_out(dve, l, "wT", 2)
                bk.wait_out(dve, l, "tr", (2, 3))
                colb = C("colb").rearrange("p (b n) -> p b n", b=B)

                def per_sequence(out, src):
                    for h in range(NH):
                        last = tt(out[0:HD, h * B * NS:(h + 1) * B * NS].rearrange("p (b n) -> p b n", b=B),
                                  src[0:HD, h * NS:(h + 1) * NS][:, None, :].to_broadcast([HD, B, NS]),
                                  colb[0:HD], ALU.mult)
                    return last

                per_sequence(nwm, per[2]["nwT"])
                spread_ready.by(per_sequence(qem, per[2]["qeT"]))
                bk.wait_full(dve, l, "oo", 4)
                bk.wait_out(dve, l, "gls")
                bk.wait_out(dve, l, "vn", 4)
                s0_loaded.wait(dve, l, 8)
                step(tt(s0[0:HD, :].rearrange("p (g v) -> p g v", v=HD), s0[0:HD, :].rearrange(
                    "p (g v) -> p g v", v=HD), eglT[0:HD, 32:96][:, :, None].to_broadcast([HD, B * NH, HD]), ALU.mult))
                for hf in range(2):
                    if hf:
                        bk.wait_full(dve, l, "st", 7)
                    for h in range(4):
                        last = tt(vnm[0:NS, 512 * h:512 * h + 512].rearrange("p (b v) -> p b v", b=B),
                                  vnw[2][0:NS, (4 * hf + h) * HD:(4 * hf + h + 1) * HD][:, None, :]
                                  .to_broadcast([NS, B, HD]),
                                  C("rowb")[0:NS, :][:, :, None].to_broadcast([NS, B, HD]), ALU.mult)
                    vnm_ready.by(last)
                    for h in range(4 * hf, 4 * hf + 4):
                        bk.wait_full(dve, l, "st", 4 + h)
                        own = s0[0:HD, :].rearrange("p (b h v) -> p b h v", b=B, h=NH)[:, :, h, :]
                        tt(own, own, bk.ap("st", 4 + h)[0:HD, :].rearrange("p (b v) -> p b v", b=B), ALU.add)\
                            .then_inc(bk.out_sem("st", 4 + h), 1)
                bk.wait_out(dve, l, "st", 11)
                states_ready.by(v.memset(ms[:, 0:8], 1.0))
                states_ready.wait(dve, l, 2)
                for t, (n0, r) in enumerate(TILES):
                    for c in ((2 * t, 2 * t + 1) if t < 2 else (4,)):
                        bk.wait_out(dve, l, "oo", c)
                    sq = LT[0:r, 0:512]
                    o = otok[t][0:r, :]
                    step(tt(sq, o, o, ALU.mult))
                    step(v.tensor_reduce(ms[0:r, 0:8], heads(sq), AX.X, ALU.add))
                    ms_ready.by(ts(ms[0:r, 0:8], ms[0:r, 0:8], 1.0 / HD, ALU.mult, EPS, ALU.add))
                    root_ready.wait(dve, l, 6 + t + 1)
                    step(v.reciprocal(ms[0:r, 0:8], ms[0:r, 0:8]))
                    step(tt(heads(o), heads(o), ms[0:r, 0:8][:, :, None].to_broadcast([r, NH, HD]), ALU.mult))
                    step(tt(heads(o), heads(o), dnorm[0:r, None, :].to_broadcast([r, NH, HD]), ALU.mult))
                    onorm_ready.by(tt(o, o, zrow[0:r, t, :], ALU.mult))

            def prompt_unit(l, u):
                g, hp, qt = u // 4, (u // 2) % 2, u % 2
                KW = P * (qt + 1)
                s = u % 2
                for ah in range(2):
                    S = bk.ap("S", (u, ah))
                    bk.wait_full(dve, l, "S", (u, ah))
                    if g == 0:
                        if qt:
                            v.tensor_copy(SMp[s][:, ah, 0:P], S[:, 0:P])
                        last = tt(SMp[s][:, ah, KW - P:KW], S[:, KW - P:KW], C("causal"), ALU.add)
                    else:
                        last = stt(SMp[s][:, ah, 0:KW], C("pdist")[:, qt * SEQ:qt * SEQ + KW], -SLOPES[2 * hp + ah],
                                   S[:, 0:KW], ALU.mult, ALU.add)
                    last.then_inc(bk.out_sem("S", (u, ah)), 1)
                for ah in range(2):
                    bk.wait_out(dve, l, "S", (u, ah))
                negmax_ready.by(v.tensor_reduce(mneg[:, 2 * s:2 * s + 2], SMp[s][:, :, 0:KW], AX.X, ALU.max,
                                                negate=True))

            def prompt_probs(l, u):
                g, hp, qt = u // 4, (u // 2) % 2, u % 2
                KW = P * (qt + 1)
                s = u % 2
                exp_ready.wait(dve, l, u + 1)
                pr, dn = PRp[s][:, :, 0:KW], den[:, 2 * s:2 * s + 2]
                if g:
                    step(tt(pr, pr, C("pcnt")[:, None, qt * SEQ:qt * SEQ + KW].to_broadcast([P, 2, KW]), ALU.mult))
                    step(v.tensor_reduce(dn, pr, AX.X, ALU.add))
                step(v.reciprocal(dn, dn))
                probs_ready.by(tt(pr, pr, dn[:, :, None].to_broadcast([P, 2, KW]), ALU.mult))

            def attention(l):
                lfb_ready.by(v.tensor_copy(lfb, lgv[:, 0:2, 0:4][:, :, :, None].to_broadcast([P, 2, 4, P])))
                prompt_unit(l, 0)
                for u in range(8):
                    if u < 7:
                        prompt_unit(l, u + 1)
                    prompt_probs(l, u)
                for g in range(2):
                    if g == 0:
                        q_zeroed.wait(dve, l, 1)
                        v.tensor_copy(lfrn[0:NS, :].rearrange("p (b h q) -> p b h q", b=B, h=4),
                                      lgv[0:NS, 2, 0:4][:, None, :, None].to_broadcast([NS, B, 4, 4]))
                    else:
                        bk.wait_full(dve, l, "SN", 0)
                    for h in range(4):
                        rows, hp = slice(64 * (h % 2), 64 * (h % 2) + 64), h // 2
                        qs = qkT[rows, 4 * g + hp, SEQ:N].rearrange("p (b q) -> p b q", b=B)
                        v.tensor_copy(QA[rows, hp, :].rearrange("p (b h q) -> p b h q", b=B, h=4)[:, :, h, :], qs)
                        last = v.tensor_copy(diag_of(rows, hp, h), qs)
                    q_spread.by(last)
                    nk = PAGES if g == 0 else DILK
                    w2 = 512 if g == 0 else 128
                    for b in range(B):
                        for hp in range(2):
                            k = 2 * hp + 1
                            bk.wait_full(dve, l, "kTs", (g, b), k)
                            v.tensor_copy(KT[b % 2][:, hp, 512:512 + w2], bk.ap("kTs", (g, b), k)[:, 0:w2])\
                                .then_inc(bk.out_sem("kTs", (g, b), k), 1)
                    for k in range(2):
                        bk.wait_full(dve, l, "SS", g, k)
                    bk.wait_full(dve, l, "SN", g)
                    if g == 0:
                        tt(SNs, bk.ap("SN", 0)[:, 0:NS], C("smask"), ALU.add).then_inc(bk.out_sem("SN", 0), 1)
                        bk.wait_out(dve, l, "SN", 0)
                        v.tensor_reduce(mneg[:, 1:2], psum[:, 0:2, :], AX.XY, ALU.max, negate=True)
                        step(v.tensor_reduce(mneg[:, 2:3], SNs, AX.X, ALU.max, negate=True))
                        s_negmax.by(tt(mneg[:, 0:1], mneg[:, 1:2], mneg[:, 2:3], ALU.min))
                        s_exp.wait(dve, l, 1)
                        step(v.tensor_reduce(den[:, 3:4], den[:, 0:3], AX.X, ALU.add))
                        wd = 1056
                    else:
                        wd = DILK * P + NS
                        tt(PRs[:, 0:512], psum[:, 0, :], C("sbias")[:, 0:512], ALU.add)\
                            .then_inc(bk.out_sem("SS", 1, 0), 1)
                        tt(PRs[:, 512:640], psum[:, 1, 0:128], C("sbias")[:, 512:640], ALU.add)\
                            .then_inc(bk.out_sem("SS", 1, 1), 1)
                        tt(PRs[:, 640:672], bk.ap("SN", 1)[:, 0:NS], C("sbias")[:, 640:672], ALU.add)\
                            .then_inc(bk.out_sem("SN", 1), 1)
                        bk.wait_out(dve, l, "SN", 1)
                        s_negmax.by(v.tensor_reduce(mneg[:, 0:1], PRs[:, 0:wd], AX.X, ALU.max, negate=True))
                        s_exp.wait(dve, l, 2)
                        step(tt(PRs[:, 0:wd], PRs[:, 0:wd], C("scnt"), ALU.mult))
                        step(v.tensor_reduce(den[:, 3:4], PRs[:, 0:wd], AX.X, ALU.add))
                    step(v.reciprocal(den[:, 3:4], den[:, 3:4]))
                    s_probs.by(ts(PRs[:, 0:wd], PRs[:, 0:wd], den[:, 3:4], ALU.mult))
                    bk.wait_full(dve, l, "OT", g)
                    own = bk.ap("OT", g).rearrange("p (c f q s) -> p c f q s", c=2, f=2, q=4)
                    for h in range(4):
                        rows, hp = slice(64 * (h % 2), 64 * (h % 2) + 64), h // 2
                        last = v.tensor_copy(
                            mixT[rows, 2 * g + hp, SEQ:N].rearrange("p (c q t) -> p c q t", c=2, q=4),
                            own[rows, :, hp, :, 4 * h:4 * h + 4])
                    last.then_inc(bk.out_sem("OT", g), 1)

            def diag_of(rows, hp, h):
                at = QZ[rows, hp, 0, 4 * h:4 * h + 4]
                return bass.AP(tensor=at.tensor, offset=at.offset, ap=[[SIDEW, HD], [P + 16, B], [1, 4]])

            def residual(l, name, order=range(6)):
                for i in order:
                    t, hf = i // 2, i % 2
                    r = TILES[t][1]
                    part = x[0:r, t, 512 * hf:512 * hf + 512]
                    bk.wait_full(dve, l, name, i)
                    tt(part, part, bk.ap(name, i)[0:r, :], ALU.add).then_inc(bk.out_sem(name, i), 1)
                for i in range(6):
                    bk.wait_out(dve, l, name, i)

            def top16(jobs):
                rows = [[ap[:, g, :] for ap in job] for job in jobs for g in range(job[0].shape[1])]
                for values, spare, out, index in rows:
                    dve_step.by(v.max(out[:, 0:8], values))
                settle()
                for values, spare, out, index in rows:
                    v.max_index(index[:, 0:8], out[:, 0:8], values)
                    dve_step.by(v.match_replace(spare, out[:, 0:8], values, -3.0e38))
                settle()
                for values, spare, out, index in rows:
                    dve_step.by(v.max(out[:, 8:16], spare))
                settle()
                for values, spare, out, index in rows:
                    dve_step.by(v.max_index(index[:, 8:16], out[:, 8:16], spare))
                settle()

            def retrieval(l):
                residual(l, "y", (0, 2, 4, 1, 3, 5))
                x_summed.by(v.memset(hsum[:, 8:16], 0.0))
                norm_rows(l, 1, "xT_ffn", 56)
                for g in range(4):
                    for t in range(3):
                        bk.wait_out(dve, l, "sc", (t, g))
                    part = slice(4 * g, 4 * g + 4)
                    top16([(scb[t][0:r, part], sc2[0:r, 4 * t:4 * t + 4], topv[t][0:r, part], topu[t][0:r, part])
                           for t, (n0, r) in enumerate(TILES)])
                for t, (n0, r) in enumerate(TILES):
                    v.tensor_copy(topf[t][0:r], topu[t][0:r])
                    tv = topv[t][0:r].rearrange("p (h c) k -> p c h k", c=2)
                    cv = cand[0:r, :].rearrange("p (h a b) -> p h a b", h=NH, a=16)
                    step(tt(cv, tv[:, 0][:, :, :, None].to_broadcast([r, NH, 16, 16]),
                               tv[:, 1][:, :, None, :].to_broadcast([r, NH, 16, 16]), ALU.add))
                    top16([(cand[0:r].rearrange("p (h k) -> p h k", h=NH),
                            cand2[0:r].rearrange("p (h k) -> p h k", h=NH), fv[0:r], posu[0:r])])
                    ts(posw[0:r, 0], posu[0:r], 4, ALU.logical_shift_right)
                    step(ts(posw[0:r, 1], posu[0:r], 15, ALU.bitwise_and))
                    v.tensor_copy(fa[0:r], posw[0:r, 0])
                    step(v.tensor_copy(fb[0:r], posw[0:r, 1]))
                    if t == 2:
                        looked_up.wait(dve, l, 1)
                    for c, which in ((0, fa), (1, fb)):
                        last = tt(oneh[t % 2][c][0:r].rearrange("p (k a) -> p k a", a=16),
                                  iota16[0:r, None, :].to_broadcast([r, P, 16]),
                                  which[0:r].rearrange("p h k -> p (h k)")[:, :, None].to_broadcast([r, P, 16]),
                                  ALU.is_equal)
                    rows_hot.by(last)
                    w = ijw[t][0:r, 2, :].rearrange("p (h k) -> p h k", h=NH)
                    fv_ready.by(tt(w, fv[0:r], fv[0:r, :, 0:1].to_broadcast([r, NH, 16]), ALU.subtract))
                    fv_exp.wait(dve, l, t + 1)
                    step(v.tensor_reduce(hsum[0:r, 0:8], w, AX.X, ALU.add))
                    step(v.reciprocal(hsum[0:r, 0:8], hsum[0:r, 0:8]))
                    ijw_ready.by(tt(w, w, hsum[0:r, 0:8][:, :, None].to_broadcast([r, NH, 16]), ALU.mult))

            def gates(l):
                def group(i, s, tokens, reuse):
                    if reuse:
                        dve.wait_ge(gate_filled, i + (1 - NHOT))
                    tt(hot[s], iota[:, None, None, :].to_broadcast([P, 2, 4, P]),
                       ijwT[:, 0:2, tokens][:, :, :, None].to_broadcast([P, 2, 4, P]), ALU.is_equal)\
                        .then_inc(hot_ready, 1)

                for s in range(NHOT):
                    group(l * (N // 4) + s, s, slice(4 * s, 4 * s + 4), False)
                with dve.Fori(1, N // (4 * NHOT)) as g:
                    for s in range(NHOT):
                        group(l * (N // 4) + g * NHOT + s, s, bass.ds(g * (4 * NHOT) + 4 * s, 4), True)

            def stream(l):
                first = l * NCH

                hT_high.wait(dve, l, 1)
                hT_split.by(tt(exact(hT[:, :, :]), hT[:, :, :], exact(hTh), ALU.subtract))

                def low_u(j, k):
                    dve.wait_ge(ut_high[k], j + 1)
                    bank = psum[:, 6, :].rearrange("p (c e) -> p c e", c=4)
                    part = slice(4 * k, 4 * k + 4)
                    tt(exact(UTl[:, part, :]), bank, exact(UTh[:, part, :]), ALU.subtract).then_inc(ut_split[k], 1)

                def gated(j, s, col):
                    dve.wait_ge(gelu_done, j + 1)
                    tt(aT[s], ge[s], G[:, col, :], ALU.mult).then_inc(gated_ready, 1)

                def low_a(j, s):
                    dve.wait_ge(at_high, j + 1)
                    tt(exact(aT[s]), aT[s], exact(ge[s]), ALU.subtract).then_inc(at_split, 1)

                def low_v(j, s):
                    dve.wait_ge(v_high, j + 1)
                    tt(exact(vbuf[s]), vbuf[s], exact(vh[s]), ALU.subtract).then_inc(v_split, 1)

                def chunk(j, s, col, following=True):
                    if following:
                        low_u(j + 1, 0)
                    gated(j, s, col)
                    if following:
                        low_u(j + 1, 1)
                    low_a(j, s)
                    low_v(j, s)

                for k in range(2):
                    low_u(first, k)
                chunk(first, 0, 0)
                chunk(first + 1, 1, 1)
                with dve.Fori(1, NCH // 2 - 1) as m:
                    for s in range(2):
                        chunk(first + m * 2 + s, s, m * 2 + s)
                chunk(first + NCH - 2, 0, NCH - 2)
                chunk(first + NCH - 1, 1, NCH - 1, False)

            dve_zero = v.memset(small[:, :], 0.0)
            dve_zero.then_inc(init_done, 1)
            dve.wait_ge(init_done, 1)
            dve.wait_ge(x_loaded, 48)
            dve.wait_ge(keep_loaded, 16)
            for l in range(DEPTH):
                project(l)
                phase(dve, l, 0)
                mixc_loaded.wait(dve, l, 1)
                delta(l)
                phase(dve, l, 1)
                attention(l)
                phase(dve, l, 2)
                retrieval(l)
                phase(dve, l, 3)
                gates(l)
                stream(l)
                x_reloaded.wait(dve, l, 3)
                residual(l, "yb")
                phase(dve, l, 4)
            dve.wait_ge(gfin_loaded, 16)
            for t, (n0, r) in enumerate(TILES):
                row = arena[0:r, D * (t + 1):D * (t + 2)]
                v.tensor_tensor_reduce(row, x[0:r, t, :], x[0:r, t, :], 1.0, 0.0, ALU.mult, ALU.add,
                                       ms[0:r, t:t + 1]).then_inc(final_step, 1)
                dve.wait_ge(final_step, 3 * t + 1)
                ts(ms[0:r, t:t + 1], ms[0:r, t:t + 1], 1.0 / D, ALU.mult, EPS, ALU.add).then_inc(final_ms, 1)
                dve.wait_ge(final_root, t + 1)
                v.reciprocal(ms[0:r, t:t + 1], ms[0:r, t:t + 1]).then_inc(final_step, 1)
                dve.wait_ge(final_step, 3 * t + 2)
                ts(row, x[0:r, t, :], ms[0:r, t:t + 1], ALU.mult).then_inc(final_step, 1)
                dve.wait_ge(final_step, 3 * t + 3)
                tt(row, row, arena[0:r, 0:D], ALU.mult).then_inc(final_ready, 1)

        for name, s in sigs.items():
            assert s.given == s.n * DEPTH, (name, s.given, s.n)


_INS = ["x_prompt", "x_sample", "cache_fox_kv", "cache_fox_logf", "cache_dil_kv", "state_delta", "state_conv",
        "page_table", "norm_mix", "w_in", "b_fox_f", "conv_w", "a_log", "dt_bias", "delta_norm", "w_out", "norm_ffn",
        "peer_wq", "peer_keys", "peer_u", "peer_v", "norm_final"]
_OUTS = [("y_prompt", (1, SEQ, D)), ("y_sample", (B, T, D)),
         ("fox_kv_prompt", (DEPTH, 1, SEQ, 2, 4, HD)), ("fox_logf_prompt", (DEPTH, 1, SEQ, 4)),
         ("dil_kv_prompt", (DEPTH, 1, SEQ, 2, 4, HD)), ("delta_state_prompt", (DEPTH, 1, NH, HD, HD)),
         ("conv_state_prompt", (DEPTH, 1, 3, CONV)),
         ("fox_kv_sample", (DEPTH, B, T, 2, 4, HD)), ("fox_logf_sample", (DEPTH, B, T, 4)),
         ("dil_kv_sample", (DEPTH, B, T, 2, 4, HD)), ("delta_state_sample", (DEPTH, B, NH, HD, HD)),
         ("conv_state_sample", (DEPTH, B, 3, CONV))]


def kernel(**inputs):
    import concourse.bacc as _bacc
    from concourse.bass_utils import run_bass_kernel_spmd as _run

    nc = _bacc.Bacc("TRN2", target_bir_lowering=False, num_devices=1)
    c_keep, c_mix, where = shape_constants()
    arrays, aps = {}, {}
    for name in _INS:
        arrays["in_" + name] = np.ascontiguousarray(inputs[name])
    arrays["in_c_keep"], arrays["in_c_mix"] = c_keep, c_mix
    for name, arr in arrays.items():
        aps[name[3:]] = nc.dram_tensor(name, arr.shape, mybir.dt.from_np(arr.dtype), kind="ExternalInput").ap()
    aps["outs"] = {name: nc.dram_tensor("out_" + name, shape, F32, kind="ExternalOutput").ap() for name, shape in _OUTS}
    build(nc, aps, where)
    r = _run(nc, [arrays], core_ids=[0])
    return tuple(r.results[0]["out_" + name] for name, _ in _OUTS)
```
